# Optimizing a Trainium2 kernel written in Bass

```python
import jax, jax.numpy as jnp
from jax import lax
import numpy as np

D_MODEL = 1024
BATCH = 1
SEQ = 2048
DEPTH = 1

CHUNK = 64
EPS = 1e-6

HG_WIDTH = D_MODEL // 2
HG_DK = 128
HG_DV = 128
HG_HEADS = HG_WIDTH // HG_DK

RW_WIDTH = D_MODEL - HG_WIDTH
RW_HEAD = 64
RW_HEADS = RW_WIDTH // RW_HEAD
RW_DECAY_LORA = 64
RW_A_LORA = 64
RW_GATE_LORA = 128
RW_GN_EPS = 64e-5

HG_COLS = 4 * HG_WIDTH
RW_COLS = 3 * RW_WIDTH + RW_DECAY_LORA + RW_A_LORA + RW_GATE_LORA
IN_COLS = HG_COLS + RW_COLS

D_FF = ((8 * D_MODEL // 3 + 255) // 256) * 256

kernel_name = 'hymba_hgrn2_rwkv7_hybrid_block'

def rmsnorm(x, w):
    xf = x.astype(jnp.float32)
    y = xf * lax.rsqrt(jnp.mean(xf * xf, axis=-1, keepdims=True) + EPS)
    return (y * w.astype(jnp.float32)).astype(x.dtype)

def token_shift(p):
    return jnp.pad(p[:, :-1], ((0, 0), (1, 0), (0, 0)))

def hgrn2_mixer(q, f_logit, i, g, lb, norm_w):
    B, T, _ = q.shape
    N = T // CHUNK
    f32 = jnp.float32
    qf = jax.nn.silu(q.astype(f32))
    fs = lb + (1.0 - lb) * jax.nn.sigmoid(f_logit.astype(f32))
    logf = jnp.log(fs)
    kf = 1.0 - fs
    vf = i.astype(f32)

    def blocks(z, d):
        return z.reshape(B, N, CHUNK, HG_HEADS, d).transpose(0, 3, 1, 2, 4)

    qb, kb, lb_ = blocks(qf, HG_DK), blocks(kf, HG_DK), blocks(logf, HG_DK)
    vb = blocks(vf, HG_DV)
    b = jnp.cumsum(lb_, axis=3)
    b_ref = b[:, :, :, CHUNK // 2:CHUNK // 2 + 1]
    b_last = b[:, :, :, -1:]
    scores = jnp.einsum('bhnik,bhnjk->bhnij', qb * jnp.exp(b - b_ref), kb * jnp.exp(b_ref - b))
    mask = jnp.tril(jnp.ones((CHUNK, CHUNK), dtype=bool))
    scores = jnp.where(mask, scores, 0.0)
    o = jnp.einsum('bhnij,bhnjv->bhniv', scores, vb)
    U = jnp.einsum('bhnck,bhncv->bhnkv', kb * jnp.exp(b_last - b), vb)
    chunk_decay = jnp.exp(b_last[:, :, :, 0])

    def step(S, inp):
        dec, u = inp
        return dec[..., None] * S + u, S

    S0 = jnp.zeros((B, HG_HEADS, HG_DK, HG_DV), f32)
    _, S_prev = lax.scan(step, S0, (jnp.moveaxis(chunk_decay, 2, 0), jnp.moveaxis(U, 2, 0)))
    S_prev = jnp.moveaxis(S_prev, 0, 2)
    o = o + jnp.einsum('bhnck,bhnkv->bhncv', qb * jnp.exp(b), S_prev)
    o = o * lax.rsqrt(jnp.mean(o * o, axis=-1, keepdims=True) + EPS)
    o = o.transpose(0, 2, 3, 1, 4).reshape(B, T, HG_WIDTH)
    o = o * norm_w.astype(f32) * jax.nn.silu(g.astype(f32))
    return o.astype(q.dtype)

def rwkv7_mixer(p, mix, w0, w2, a0, a2, g2, k_k, k_a, r_k, ln_w, ln_b):
    B, T, _ = p.shape
    f32 = jnp.float32
    dtype = p.dtype
    pf = p.astype(f32)
    pf = pf + (token_shift(pf) - pf) * mix.astype(f32)
    r, k, v, dw, da, dg = jnp.split(pf, [RW_WIDTH, 2 * RW_WIDTH, 3 * RW_WIDTH,
                                         3 * RW_WIDTH + RW_DECAY_LORA,
                                         3 * RW_WIDTH + RW_DECAY_LORA + RW_A_LORA], axis=-1)
    w = -jax.nn.softplus(-(w0.astype(f32) + jnp.tanh(dw) @ w2.astype(f32))) - 0.5
    decay = jnp.exp(-jnp.exp(w))
    a = jax.nn.sigmoid(a0.astype(f32) + da @ a2.astype(f32))
    g = jax.nn.sigmoid(dg) @ g2.astype(f32)

    def heads(z):
        return z.reshape(B, T, RW_HEADS, RW_HEAD)

    kk = heads(k * k_k.astype(f32))
    kk = kk / jnp.maximum(jnp.sqrt(jnp.sum(kk * kk, axis=-1, keepdims=True)), 1e-12)
    k = k * (1.0 + (a - 1.0) * k_a.astype(f32))
    rh, wh, kh, vh, ah = heads(r), heads(decay), heads(k), heads(v), heads(a)

    def step(S, inp):
        r_t, w_t, k_t, v_t, kk_t, a_t = inp
        sa = jnp.einsum('bhvk,bhk->bhv', S, -kk_t)
        S = S * w_t[:, :, None, :] + sa[..., None] * (kk_t * a_t)[:, :, None, :] \
            + v_t[..., None] * k_t[:, :, None, :]
        return S, jnp.einsum('bhvk,bhk->bhv', S, r_t)

    S0 = jnp.zeros((B, RW_HEADS, RW_HEAD, RW_HEAD), f32)
    xs = tuple(jnp.moveaxis(z, 1, 0) for z in (rh, wh, kh, vh, kk, ah))
    _, y = lax.scan(step, S0, xs)
    y = jnp.moveaxis(y, 0, 1)
    mu = jnp.mean(y, axis=-1, keepdims=True)
    var = jnp.mean(jnp.square(y - mu), axis=-1, keepdims=True)
    y = ((y - mu) * lax.rsqrt(var + RW_GN_EPS)).reshape(B, T, RW_WIDTH)
    y = y * ln_w.astype(f32) + ln_b.astype(f32)
    bonus = jnp.sum(rh * kh * r_k.astype(f32), axis=-1, keepdims=True) * vh
    y = (y + bonus.reshape(B, T, RW_WIDTH)) * g
    return y.astype(dtype)

def setup_inputs(seed: int = 0) -> dict:
    key = jax.random.key(seed)
    ks = jax.random.split(key, 24)
    f32 = jnp.float32
    nrm = lambda k, shape, s: jax.random.normal(k, shape, f32) * s
    return {
        'x': jax.random.normal(ks[0], (BATCH, SEQ, D_MODEL), f32),
        'norm1_w': 1.0 + nrm(ks[1], (DEPTH, D_MODEL), 0.05),
        'w_in': nrm(ks[2], (DEPTH, D_MODEL, IN_COLS), D_MODEL ** -0.5),
        'hg_lower_bounds': nrm(ks[3], (DEPTH + 1, HG_WIDTH), 0.1),
        'hg_norm_w': 1.0 + nrm(ks[4], (DEPTH, HG_WIDTH), 0.05),
        'rw_mix': jax.random.uniform(ks[5], (DEPTH, RW_COLS), f32),
        'rw_w0': jax.random.uniform(ks[6], (DEPTH, RW_WIDTH), f32, -5.0, -0.5),
        'rw_w2': nrm(ks[7], (DEPTH, RW_DECAY_LORA, RW_WIDTH), 0.1 * RW_DECAY_LORA ** -0.5),
        'rw_a0': nrm(ks[8], (DEPTH, RW_WIDTH), 0.5),
        'rw_a2': nrm(ks[9], (DEPTH, RW_A_LORA, RW_WIDTH), 0.5 * RW_A_LORA ** -0.5),
        'rw_g2': nrm(ks[10], (DEPTH, RW_GATE_LORA, RW_WIDTH), RW_GATE_LORA ** -0.5),
        'rw_k_k': 0.85 + nrm(ks[11], (DEPTH, RW_WIDTH), 0.05),
        'rw_k_a': 1.0 + nrm(ks[12], (DEPTH, RW_WIDTH), 0.05),
        'rw_r_k': nrm(ks[13], (DEPTH, RW_HEADS, RW_HEAD), 0.1),
        'rw_ln_w': 1.0 + nrm(ks[14], (DEPTH, RW_WIDTH), 0.05),
        'rw_ln_b': nrm(ks[15], (DEPTH, RW_WIDTH), 0.02),
        'w_out': nrm(ks[16], (DEPTH, D_MODEL, D_MODEL), D_MODEL ** -0.5),
        'norm2_w': 1.0 + nrm(ks[17], (DEPTH, D_MODEL), 0.05),
        'ffn_w1': nrm(ks[18], (DEPTH, D_MODEL, D_FF), D_MODEL ** -0.5),
        'ffn_w3': nrm(ks[19], (DEPTH, D_MODEL, D_FF), D_MODEL ** -0.5),
        'ffn_w2': nrm(ks[20], (DEPTH, D_FF, D_MODEL), D_FF ** -0.5),
        'final_norm_w': 1.0 + nrm(ks[21], (D_MODEL,), 0.05),
    }

def reference(x, norm1_w, w_in, hg_lower_bounds, hg_norm_w, rw_mix, rw_w0, rw_w2, rw_a0,
              rw_a2, rw_g2, rw_k_k, rw_k_a, rw_r_k, rw_ln_w, rw_ln_b, w_out, norm2_w,
              ffn_w1, ffn_w3, ffn_w2, final_norm_w):
    lbs = jnp.cumsum(jax.nn.softmax(hg_lower_bounds.astype(jnp.float32), axis=0), axis=0)
    for l in range(DEPTH):
        h = rmsnorm(x, norm1_w[l])
        proj = h @ w_in[l]
        q, f_logit, i, g = jnp.split(proj[..., :HG_COLS], 4, axis=-1)
        o_hg = hgrn2_mixer(q, f_logit, i, g, lbs[l], hg_norm_w[l])
        o_rw = rwkv7_mixer(proj[..., HG_COLS:], rw_mix[l], rw_w0[l], rw_w2[l], rw_a0[l], rw_a2[l],
                           rw_g2[l], rw_k_k[l], rw_k_a[l], rw_r_k[l], rw_ln_w[l], rw_ln_b[l])
        x = x + jnp.concatenate([o_hg, o_rw], axis=-1) @ w_out[l]
        h = rmsnorm(x, norm2_w[l])
        x = x + (jax.nn.silu(h @ ffn_w1[l]) * (h @ ffn_w3[l])) @ ffn_w2[l]
    return rmsnorm(x, final_norm_w)


_drawn_inputs = setup_inputs


def setup_inputs(seed=0):
    import zlib

    import numpy as np

    out = dict(_drawn_inputs(seed))
    spreads = {}
    factors = {'hg_lower_bounds': 8.0,
     'hg_norm_w': 2.844,
     'rw_w2': 8.0,
     'rw_k_k': 3.921,
     'rw_k_a': 2.761,
     'rw_ln_w': 3.086,
     'rw_ln_b': 7.759,
     'norm2_w': 2.686}
    for name, (base, spread) in spreads.items():
        noise = np.random.default_rng([zlib.crc32(name.encode()), seed]).standard_normal(out[name].shape)
        drawn = base * np.exp(spread * noise) if base else spread * noise
        out[name] = __import__('jax').numpy.asarray(drawn.astype(out[name].dtype))
    for name, factor in factors.items():
        out[name] = (out[name] * factor).astype(out[name].dtype)
    return out
```

```python
from contextlib import ExitStack

import concourse.bass as bass
from concourse import mybir

F32 = mybir.dt.float32
F32R = mybir.dt.float32r
I32 = mybir.dt.int32
ALU = mybir.AluOpType
ACT = mybir.ActivationFunctionType
AX = mybir.AxisListType

P = 128
CHUNK = 64
BLOCK = 512
EPS = 1e-6
GN_EPS = 64e-5
KK_GUARD = 1e-24
LN_SCALE = 65536.0
HALF_LN_LN_SCALE = 0.5 * 16 * 0.6931471805599453
DECAY = 0.6065306597126334
ONE_SET = "natural_log_exp_and_others"
SILU_SET = "silu_and_others"
SQRT_SET = "sqrt_and_others"


class Stages:

    def __init__(self, sem, names, ahead=0):
        self.sem, self.names, self.ahead, self.next = sem, names.split(), ahead, 0

    def at(self, step, name):
        return (step + self.ahead) * len(self.names) + self.names.index(name) + 1

    def one(self, name):
        assert self.names[self.next] == name, (self.names[self.next], name)
        self.next = (self.next + 1) % len(self.names)
        return 1


def apart(eng, between):
    eng.sem_inc(between, 1)


def split_hi(eng, hi, raw):
    return eng.activation(hi, raw, ACT.Copy)


def split_lo(eng, lo, raw, hi):
    return eng.tensor_tensor(lo, raw, hi.bitcast(F32), ALU.subtract)


def three_passes(eng, out, lhs, rhs, first, last):
    eng.matmul(out, lhs[0], rhs[0], start=first, stop=False)
    eng.matmul(out, lhs[0], rhs[1], start=False, stop=False)
    return eng.matmul(out, lhs[1], rhs[0], start=False, stop=last)


def column(table, c):
    return table[:, bass.ds(c, 1)]


def project(nc, dims, consts, keep, A, S):
    D, T, W = dims["D"], dims["T"], dims["W"]
    KT = D // P
    HALVES = 2
    TH = T // HALVES
    NB = TH // BLOCK
    TILES = TH // P
    BT = BLOCK // P
    BC = BLOCK // CHUNK
    UNITS = W // P
    RW0 = 4 * W
    LORA0 = RW0 + 3 * W
    COL = dims["COL"]
    prm, ident, headsum = consts["prm"], consts["ident"], consts["headsum"]
    w_in = A["w_in"]

    with ExitStack() as ctx:
        def sb(name, shape, dt=F32):
            return ctx.enter_context(nc.sbuf_tensor("p_" + name, shape, dt))

        def sem(name):
            return ctx.enter_context(nc.semaphore("p_" + name))

        hT = [sb("hT_hi", [P, KT, TH], F32R), sb("hT_lo", [P, KT, TH], F32R)]
        raw = sb("raw", [P, 4, KT, P])
        wt = [sb("w_hi", [P, 4, KT, P], F32R), sb("w_lo", [P, 4, KT, P], F32R)]
        norm_row = sb("norm_row", [P, D])
        xt = sb("xt", [P, 2, D])
        xs = sb("xs", [P, D])
        stat = sb("stat", [P, 4])
        lora2 = sb("lora2", [P, W])
        lora_unit = sb("lora_unit", [P, P])
        k_a_unit = sb("k_a_unit", [P, 2])
        tda = sb("tda", [P, max(TH, D)])
        resets = sb("resets", [P, BLOCK])
        carry = sb("carry", [P, 16])
        m = {k: sb("m_" + k, [P, BLOCK + 1]) for k in "krv"}
        t = {k: sb("t_" + k, [P, BLOCK]) for k in
             "k r e1 e2 s1 s2 cs dm dx pp qq px sq ln kk tt kp ak".split()}
        out = {k: sb("out_" + k, [P, BLOCK]) for k in ("al", "rh", "v", "rk")}
        out_bk = sb("out_bk", [P, BC, 2, CHUNK])
        bank = [ctx.enter_context(nc.psum_tensor(f"p_bank{i}", [P, BLOCK], F32)) for i in range(8)]
        K_, WD, AA, R_, SS, V_ = bank[0:6]
        F_, Q_, G_, I_ = bank[6], bank[7], bank[0], bank[1]
        DWDA, DG = bank[2], bank[3]
        TURN = [bank[4][:, :].rearrange("p (a b) -> p a b", a=BT),
                bank[5][:, :].rearrange("p (a b) -> p a b", a=BT)]

        loaded_c, resets_made = sem("loaded_consts"), sem("resets_made")
        between = {k: sem("between_" + k) for k in ("sp", "pe", "act", "dve", "pool")}
        loaded_x = [sem("loaded_x0"), sem("loaded_x1")]
        loaded_l, loaded_r, loaded_h = sem("loaded_w_lora"), sem("loaded_w_rw"), sem("loaded_w_hg")
        NPE = Stages(sem("norm_pe"), "turn0 turn1", ahead=2)
        NACT = Stages(sem("norm_act"), "square ln rstd hi0 hi1", ahead=2)
        NDVE = Stages(sem("norm_dve"), "scaled lo0 lo1", ahead=2)
        WLA, WLD = Stages(sem("split_lora_hi"), "dwda dg"), Stages(sem("split_lora_lo"), "dwda dg")
        WRA, WRD = Stages(sem("split_rw_hi"), "k r v"), Stages(sem("split_rw_lo"), "k r v")
        WHA, WHD = Stages(sem("split_hg_hi"), "f q g i"), Stages(sem("split_hg_lo"), "f q g i")
        ULD = Stages(sem("rw_unit_dve"), "k_a omka lora", ahead=1)
        LPE = Stages(sem("lora_pe"), "dwda dg", ahead=1)
        LACT = Stages(sem("lora_act"), "mixa expa copya mixg expg", ahead=1)
        LDVE = Stages(sem("lora_dve"), "pa a1 rec tanh pg g1 sdg", ahead=1)
        LPOOL = Stages(sem("lora_pool"), "ca sa cg sg", ahead=1)
        RPE = Stages(sem("rw_pe"), "k w a r ss v", ahead=1)
        RACT = Stages(sem("rw_act"), "mk ew ea sq mr pp qq px ee dd mv ln inv", ahead=1)
        RDVE = Stages(sem("rw_dve"), "k w1 sg cs dm dx a1 a r rho mx v kappa rk kk alpha beta", ahead=1)
        RPOOL = Stages(sem("rw_pool"), "ck sk cr sr t kp cv sv ak", ahead=1)
        HPE = Stages(sem("hg_pe"), "f q g i", ahead=1)
        HACT = Stages(sem("hg_act"), "ef lf eq pp qq ee dd eg i", ahead=1)
        HDVE = Stages(sem("hg_dve"), "f1 sf kf cs dm q1 sq qs qt kt g1 sg gs", ahead=1)
        LSP, RSP, HSP = (Stages(sem(k + "_stored"), "s", ahead=1) for k in ("lora", "rw", "hg"))
        st_lo, st_rw, st_hg = sem("st_lora"), sem("st_rw"), sem("st_hg")
        credit = {"pe": [NPE, LPE, RPE, HPE], "act": [NACT, LACT, RACT, HACT],
                  "dve": [NDVE, LDVE, RDVE, HDVE], "pool": [LPOOL, RPOOL], "sp": [LSP, RSP, HSP]}

        def begin(eng, who):
            for s in credit[who]:
                eng.sem_inc(s.sem, s.ahead * len(s.names))

        def wait(eng, s, step, name):
            eng.wait_ge(s.sem, s.at(step, name))

        def lora_over(eng, hf):
            n = hf * NB + NB - 1
            for s, name in ((LPE, "dg"), (LACT, "expg"), (LDVE, "sdg"), (LPOOL, "sg"), (LSP, "s")):
                wait(eng, s, n, name)

        def rw_over(eng, hf):
            n = (hf * UNITS + UNITS) * NB - 1
            for s, name in ((RPE, "v"), (RACT, "inv"), (RDVE, "beta"), (RPOOL, "ak"), (RSP, "s")):
                wait(eng, s, n, name)

        def hg_over(eng, hf):
            n = (hf * UNITS + UNITS) * NB - 1
            for s, name in ((HPE, "i"), (HACT, "i"), (HDVE, "gs"), (HSP, "s")):
                wait(eng, s, n, name)

        def lora_tiles():
            return [(2, "dwda", LORA0), (3, "dg", LORA0 + P)]

        def rw_tiles(p):
            return [(0, "k", RW0 + W + p * P), (1, "r", RW0 + p * P), (2, "v", RW0 + 2 * W + p * P)]

        def hg_tiles(h):
            return [(0, "f", W + h * P), (1, "q", h * P), (2, "g", 3 * W + h * P), (3, "i", 2 * W + h * P)]

        block = ctx.enter_context(nc.Block())

        @block.sync
        def _(sp):
            begin(sp, "sp")

            def wait_sp(s, step, name):
                wait(sp, s, step, name)
                apart(sp, between["sp"])

            sp.dma_start(norm_row[:, :], A["norm1_w"].partition_broadcast(P)).then_inc(loaded_c, 16)
            sp.dma_start(lora2[0:64, :], A["rw_w2"]).then_inc(loaded_c, 16)
            sp.dma_start(lora2[64:128, :], A["rw_a2"]).then_inc(loaded_c, 16)

            def load(tiles, landed):
                for slot, _, first in tiles:
                    sp.dma_start(raw[:, slot], w_in[:, bass.ds(first, P)].rearrange("(k p) c -> p k c", p=P))\
                      .then_inc(landed, 16)

            def store(dst, kind, src, tile0):
                return sp.dma_start(dst[bass.ds(tile0, BT), :, kind, :].rearrange("t p k -> p t k"),
                                    src[:, :].rearrange("p (t k) -> p t k", t=BT))

            def rw_unit(hf, p, ahead):
                u = hf * UNITS + p
                for k in ("k", "r", "v"):
                    wait_sp(WRD, u, k)
                load(*ahead)
                for b in range(NB):
                    n = u * NB + b
                    tile0 = hf * TILES + b * BT
                    for kind, name, stage in ((1, "rh", "rho"), (4, "v", "v"), (5, "rk", "rk"), (0, "al", "alpha")):
                        wait_sp(RDVE, n, stage)
                        store(S["rw"], p * 6 + kind, out[name], tile0).then_inc(st_rw, 16)
                    wait_sp(RDVE, n, "beta")
                    sp.dma_start(S["rw"][bass.ds(tile0, BT), :, bass.ds(p * 6 + 2, 2), :].rearrange("t p k c -> p t (k c)"),
                                 out_bk[:, :, :, :].rearrange("p (t c) k i -> p t (c k i)", t=BT)).then_inc(st_rw, 16)
                    sp.wait_ge(st_rw, (n + 1) * 80)
                    apart(sp, between["sp"])
                    sp.sem_inc(RSP.sem, RSP.one("s"))

            def hg_unit(hf, h, ahead):
                u = hf * UNITS + h
                for k in ("f", "q", "g", "i"):
                    wait_sp(WHD, u, k)
                if ahead:
                    load(*ahead)
                for b in range(NB):
                    n = u * NB + b
                    tile0 = hf * TILES + b * BT
                    for i, (src, s, stage) in enumerate(((out["al"], HDVE, "qt"), (out["rh"], HDVE, "kt"),
                                                         (out["v"], HACT, "i"), (out["rk"], HDVE, "gs"))):
                        wait_sp(s, n, stage)
                        store(S["hg"], h * 4 + i, src, tile0).then_inc(st_hg, 16)
                    sp.wait_ge(st_hg, (n + 1) * 64)
                    apart(sp, between["sp"])
                    sp.sem_inc(HSP.sem, HSP.one("s"))

            with sp.Fori(0, HALVES) as hf:
                load(lora_tiles(), loaded_l)
                load(rw_tiles(0)[:2], loaded_r)
                with sp.Fori(0, TILES // 2) as j:
                    for s in range(2):
                        n = hf * TILES + j * 2 + s
                        wait_sp(NDVE, n - 2, "scaled")
                        wait_sp(NACT, n - 2, "square")
                        sp.dma_start(xt[:, s], A["x"][bass.ds(n * P, P), :]).then_inc(loaded_x[s], 16)
                wait_sp(WLD, hf, "dwda")
                load(rw_tiles(0)[2:], loaded_r)
                for b in range(NB):
                    n = hf * NB + b
                    wait_sp(LDVE, n, "sdg")
                    sp.dma_start(S["sdg"][bass.ds(hf * TILES + b * BT, BT)].rearrange("t p k -> p t k"),
                                 t["s2"][:, :].rearrange("p (t k) -> p t k", t=BT)).then_inc(st_lo, 16)
                    sp.wait_ge(st_lo, (n + 1) * 16)
                    apart(sp, between["sp"])
                    sp.sem_inc(LSP.sem, LSP.one("s"))
                with sp.Fori(0, UNITS - 1) as p:
                    rw_unit(hf, p, (rw_tiles(p + 1), loaded_r))
                rw_unit(hf, UNITS - 1, (hg_tiles(0), loaded_h))
                with sp.Fori(0, UNITS - 1) as h:
                    hg_unit(hf, h, (hg_tiles(h + 1), loaded_h))
                hg_unit(hf, UNITS - 1, None)

        def weights_hi(act, s, name, slot, landed, landings):
            act.wait_ge(landed, landings)
            split_hi(act, wt[0][:, slot], raw[:, slot]).then_inc(s.sem, s.one(name))

        def weights_lo(dve, s, his, step, name, slot):
            wait(dve, his, step, name)
            split_lo(dve, wt[1][:, slot], raw[:, slot], wt[0][:, slot]).then_inc(s.sem, s.one(name))

        @block.tensor
        def _(pe):
            begin(pe, "pe")

            def product(dst, slot, b):
                for k in range(KT):
                    last = three_passes(pe, dst[:, :], (wt[0][:, slot, k], wt[1][:, slot, k]),
                                        (hT[0][:, k, b * BLOCK:(b + 1) * BLOCK], hT[1][:, k, b * BLOCK:(b + 1) * BLOCK]),
                                        k == 0, k == KT - 1)
                return last

            def rw_unit(hf, p):
                u = hf * UNITS + p
                for b in range(NB):
                    n = u * NB + b

                    wait(pe, WRA, u, "k"), wait(pe, WRD, u, "k")
                    wait(pe, RACT, n - 1, "mk"), wait(pe, RDVE, n - 1, "k")
                    product(K_, 0, b).then_inc(RPE.sem, RPE.one("k"))
                    wait(pe, ULD, u, "lora")
                    wait(pe, RACT, n - 1, "ew")
                    pe.matmul(WD[:, :], lora_unit[0:64, :], tda[0:64, b * BLOCK:(b + 1) * BLOCK], start=True, stop=True)\
                      .then_inc(RPE.sem, RPE.one("w"))
                    wait(pe, RACT, n - 1, "ea")
                    pe.matmul(AA[:, :], lora_unit[64:128, :], tda[64:128, b * BLOCK:(b + 1) * BLOCK], start=True, stop=True)\
                      .then_inc(RPE.sem, RPE.one("a"))
                    wait(pe, WRA, u, "r"), wait(pe, WRD, u, "r")
                    wait(pe, RACT, n - 1, "mr"), wait(pe, RDVE, n - 1, "r")
                    product(R_, 1, b).then_inc(RPE.sem, RPE.one("r"))
                    wait(pe, RDVE, n - 1, "mx")
                    wait(pe, RACT, n, "sq")
                    pe.matmul(SS[:, :], headsum[:, :], t["sq"][:, :], start=True, stop=True)\
                      .then_inc(RPE.sem, RPE.one("ss"))
                    wait(pe, WRA, u, "v"), wait(pe, WRD, u, "v")
                    wait(pe, RACT, n - 1, "mv"), wait(pe, RDVE, n - 1, "v")
                    product(V_, 2, b).then_inc(RPE.sem, RPE.one("v"))

            def hg_unit(hf, h):
                u = hf * UNITS + h
                for b in range(NB):
                    n = u * NB + b
                    for dst, slot, name, readers in (
                            (F_, 0, "f", [(HACT, "ef")]), (Q_, 1, "q", [(HACT, "eq"), (HDVE, "qs")]),
                            (G_, 2, "g", [(HACT, "eg"), (HDVE, "gs")]), (I_, 3, "i", [(HACT, "i")])):
                        wait(pe, WHA, u, name), wait(pe, WHD, u, name)
                        for s, stage in readers:
                            wait(pe, s, n - 1, stage)
                        product(dst, slot, b).then_inc(HPE.sem, HPE.one(name))

            with pe.Fori(0, HALVES) as hf:
                rw_over(pe, hf - 1)
                hg_over(pe, hf - 1)
                apart(pe, between["pe"])
                with pe.Fori(0, TILES) as j:
                    n = hf * TILES + j
                    wait(pe, NDVE, n, "scaled")
                    for i in range(2):
                        wait(pe, NACT, n - 1, f"hi{i}"), wait(pe, NDVE, n - 1, f"lo{i}")
                        for a in range(BT):
                            k = i * BT + a
                            last = pe.transpose(TURN[i][:, a], xs[:, k * P:(k + 1) * P], ident[:, :])
                        last.then_inc(NPE.sem, NPE.one(f"turn{i}"))
                wait(pe, NACT, hf * TILES + TILES - 1, "hi1"), wait(pe, NDVE, hf * TILES + TILES - 1, "lo1")
                for b in range(NB):
                    n = hf * NB + b
                    wait(pe, WLD, hf, "dwda")
                    wait(pe, LACT, n - 1, "copya"), wait(pe, LDVE, n - 1, "pa")
                    product(DWDA, 2, b).then_inc(LPE.sem, LPE.one("dwda"))
                    wait(pe, WLD, hf, "dg")
                    wait(pe, LACT, n - 1, "mixg"), wait(pe, LDVE, n - 1, "pg")
                    product(DG, 3, b).then_inc(LPE.sem, LPE.one("dg"))
                lora_over(pe, hf)
                apart(pe, between["pe"])
                with pe.Fori(0, UNITS - 1) as p:
                    rw_unit(hf, p)
                rw_unit(hf, UNITS - 1)
                rw_over(pe, hf)
                apart(pe, between["pe"])
                with pe.Fori(0, UNITS - 1) as h:
                    hg_unit(hf, h)
                hg_unit(hf, UNITS - 1)

        @block.scalar
        def _(act):
            begin(act, "act")
            act.preload_act_table_set(ONE_SET)

            def shifted(dst, src, mixcol, s, stage):
                apart(act, between["act"])
                act.activation(dst[:, 1:BLOCK + 1], src[:, :], ACT.Copy, scale=column(prm, mixcol))\
                   .then_inc(s.sem, s.one(stage))

            def rw_unit(hf, p, nxt):
                u = hf * UNITS + p
                for b in range(NB):
                    n = u * NB + b
                    chunk0 = (hf * NB + b) * BC

                    def ahead(i, freed):
                        if nxt is None or b < NB - 1:
                            return
                        s, landed, landings, tiles = nxt
                        wait(act, RPE, n, freed)
                        slot, name, _ = tiles[i]
                        weights_hi(act, s, name, slot, landed, landings)

                    wait(act, RPE, n, "k"), wait(act, RDVE, n - 1, "k"), wait(act, RPOOL, n - 1, "sk")
                    shifted(m["k"], K_, COL["mix"] + UNITS + p, RACT, "mk")
                    wait(act, RPE, n, "w"), wait(act, RDVE, n - 1, "sg")
                    apart(act, between["act"])
                    act.activation(t["e1"][:, :], WD[:, :], ACT.Exp, scale=-1.0, bias=column(prm, COL["nw0"] + p))\
                       .then_inc(RACT.sem, RACT.one("ew"))
                    wait(act, RPE, n, "a"), wait(act, RDVE, n - 1, "a")
                    apart(act, between["act"])
                    act.activation(t["e2"][:, :], AA[:, :], ACT.Exp, scale=-1.0, bias=column(prm, COL["na0"] + p))\
                       .then_inc(RACT.sem, RACT.one("ea"))
                    wait(act, RDVE, n, "k"), wait(act, RPE, n - 1, "ss")
                    apart(act, between["act"])
                    act.activation(t["sq"][:, :], t["k"][:, :], ACT.Square, scale=column(prm, COL["k_k"] + p))\
                       .then_inc(RACT.sem, RACT.one("sq"))
                    ahead(0, "k")
                    wait(act, RPE, n, "r"), wait(act, RDVE, n - 1, "r"), wait(act, RPOOL, n - 1, "sr")
                    shifted(m["r"], R_, COL["mix"] + p, RACT, "mr")
                    wait(act, RDVE, n, "dm"), wait(act, RDVE, n - 1, "rho")
                    act.activation(t["pp"][:, :], t["dm"][:, :], ACT.Exp, scale=-DECAY).then_inc(RACT.sem, RACT.one("pp"))
                    wait(act, RDVE, n - 1, "beta")
                    act.activation(t["qq"][:, :], t["dm"][:, :], ACT.Exp, scale=DECAY).then_inc(RACT.sem, RACT.one("qq"))
                    wait(act, RDVE, n, "dx")
                    act.activation(t["px"][:, :], t["dx"][:, :], ACT.Exp, scale=-DECAY).then_inc(RACT.sem, RACT.one("px"))
                    act.activation(keep["E"][:, bass.ds(p * keep["NC"] + chunk0, BC)],
                                   t["cs"][:, CHUNK // 2::CHUNK], ACT.Exp, scale=-DECAY).then_inc(RACT.sem, RACT.one("ee"))
                    wait(act, RACT, n, "pp")
                    act.activation(keep["L"][:, bass.ds(p * keep["NC"] + chunk0, BC)],
                                   t["pp"][:, CHUNK - 1::CHUNK], ACT.Copy).then_inc(RACT.sem, RACT.one("dd"))
                    wait(act, RPE, n, "v"), wait(act, RDVE, n - 1, "v"), wait(act, RPOOL, n - 1, "sv")
                    shifted(m["v"], V_, COL["mix"] + 2 * UNITS + p, RACT, "mv")
                    ahead(1, "r")
                    wait(act, RDVE, n, "mx")
                    act.activation(t["ln"][:, :], t["ln"][:, :], ACT.Ln, scale=LN_SCALE).then_inc(RACT.sem, RACT.one("ln"))
                    wait(act, RACT, n, "ln")
                    act.activation(t["ln"][:, :], t["ln"][:, :], ACT.Exp, scale=-0.5, bias=column(prm, COL["half"]))\
                       .then_inc(RACT.sem, RACT.one("inv"))
                    ahead(2, "v")
                    if nxt is not None and len(nxt[3]) > 3:
                        ahead(3, "v")

            def hg_unit(hf, h, nxt):
                u = hf * UNITS + h
                for b in range(NB):
                    n = u * NB + b
                    chunk0 = (hf * NB + b) * BC

                    def ahead(i):
                        if nxt is None or b < NB - 1:
                            return
                        slot, name, _ = nxt[i]
                        wait(act, HPE, n, name)
                        weights_hi(act, WHA, name, slot, loaded_h, (u + 2) * 64)

                    wait(act, HPE, n, "f"), wait(act, HDVE, n - 1, "sf")
                    act.activation(t["e1"][:, :], F_[:, :], ACT.Exp, scale=-1.0).then_inc(HACT.sem, HACT.one("ef"))
                    wait(act, HDVE, n, "sf"), wait(act, HDVE, n - 1, "cs")
                    apart(act, between["act"])
                    act.activation(t["dx"][:, :], t["s1"][:, :], ACT.Ln, scale=column(prm, COL["oml"] + h),
                                   bias=column(prm, COL["lb"] + h)).then_inc(HACT.sem, HACT.one("lf"))
                    ahead(0)
                    wait(act, HPE, n, "q"), wait(act, HDVE, n - 1, "sq")
                    act.activation(t["e2"][:, :], Q_[:, :], ACT.Exp, scale=-1.0).then_inc(HACT.sem, HACT.one("eq"))
                    wait(act, HDVE, n, "dm"), wait(act, HDVE, n - 1, "qt")
                    act.activation(t["pp"][:, :], t["dm"][:, :], ACT.Exp).then_inc(HACT.sem, HACT.one("pp"))
                    wait(act, HDVE, n - 1, "kt")
                    act.activation(t["qq"][:, :], t["dm"][:, :], ACT.Exp, scale=-1.0).then_inc(HACT.sem, HACT.one("qq"))
                    act.activation(keep["E"][:, bass.ds((UNITS + h) * keep["NC"] + chunk0, BC)],
                                   t["cs"][:, CHUNK // 2::CHUNK], ACT.Exp).then_inc(HACT.sem, HACT.one("ee"))
                    wait(act, HACT, n, "pp")
                    act.activation(keep["L"][:, bass.ds((UNITS + h) * keep["NC"] + chunk0, BC)],
                                   t["pp"][:, CHUNK - 1::CHUNK], ACT.Copy).then_inc(HACT.sem, HACT.one("dd"))
                    ahead(1)
                    wait(act, HPE, n, "g"), wait(act, HDVE, n - 1, "sg")
                    act.activation(t["kk"][:, :], G_[:, :], ACT.Exp, scale=-1.0).then_inc(HACT.sem, HACT.one("eg"))
                    ahead(2)
                    wait(act, HPE, n, "i"), wait(act, HSP, n - 1, "s")
                    act.activation(out["v"][:, :], I_[:, :], ACT.Copy).then_inc(HACT.sem, HACT.one("i"))
                    ahead(3)

            with act.Fori(0, HALVES) as hf:
                rw_over(act, hf - 1)
                hg_over(act, hf - 1)
                for slot, name, _ in lora_tiles():
                    weights_hi(act, WLA, name, slot, loaded_l, (hf + 1) * 32)
                with act.Fori(0, TILES // 2) as j:
                    for s in range(2):
                        n = hf * TILES + j * 2 + s
                        act.wait_ge(loaded_x[s], (hf * (TILES // 2) + j + 1) * 16)
                        act.activation(tda[:, 0:D], xt[:, s], ACT.Square, accum_out=stat[:, 0:1])\
                           .then_inc(NACT.sem, NACT.one("square"))
                        wait(act, NACT, n, "square")
                        act.activation(stat[:, 1:2], stat[:, 0:1], ACT.Ln, scale=1.0 / D, bias=column(prm, COL["eps"]))\
                           .then_inc(NACT.sem, NACT.one("ln"))
                        wait(act, NACT, n, "ln"), wait(act, NDVE, n - 1, "scaled")
                        act.activation(stat[:, 2:3], stat[:, 1:2], ACT.Exp, scale=-0.5)\
                           .then_inc(NACT.sem, NACT.one("rstd"))
                        for i in range(2):
                            wait(act, NPE, n, f"turn{i}")
                            split_hi(act, hT[0][:, i * BT:(i + 1) * BT, bass.ds((j * 2 + s) * P, P)], TURN[i])\
                                .then_inc(NACT.sem, NACT.one(f"hi{i}"))
                for slot, name, _ in rw_tiles(0)[:2]:
                    weights_hi(act, WRA, name, slot, loaded_r, (hf * UNITS + 1) * 48)
                for b in range(NB):
                    n = hf * NB + b
                    wait(act, LPE, n, "dwda"), wait(act, LDVE, n - 1, "pa"), wait(act, LPOOL, n - 1, "sa")
                    shifted(m["k"], DWDA, COL["mix"] + 3 * UNITS, LACT, "mixa")
                    wait(act, LDVE, n, "pa"), wait(act, LDVE, n - 1, "rec")
                    act.activation(t["e1"][0:64, :], t["k"][0:64, :], ACT.Exp, scale=-2.0).then_inc(LACT.sem, LACT.one("expa"))
                    act.activation(tda[64:128, b * BLOCK:(b + 1) * BLOCK], t["k"][64:128, :], ACT.Copy)\
                       .then_inc(LACT.sem, LACT.one("copya"))
                    wait(act, LPE, n, "dg"), wait(act, LDVE, n - 1, "pg"), wait(act, LPOOL, n - 1, "sg")
                    shifted(m["r"], DG, COL["mix"] + 3 * UNITS + 1, LACT, "mixg")
                    wait(act, LDVE, n, "pg"), wait(act, LDVE, n - 1, "sdg")
                    act.activation(t["e2"][:, :], t["r"][:, :], ACT.Exp, scale=-1.0).then_inc(LACT.sem, LACT.one("expg"))
                wait(act, LPE, hf * NB + NB - 1, "dwda")
                weights_hi(act, WRA, "v", 2, loaded_r, (hf * UNITS + 1) * 48)
                lora_over(act, hf)
                with act.Fori(0, UNITS - 1) as p:
                    rw_unit(hf, p, (WRA, loaded_r, (hf * UNITS + p + 2) * 48, rw_tiles(p + 1)))
                rw_unit(hf, UNITS - 1, (WHA, loaded_h, (hf * UNITS + 1) * 64, hg_tiles(0)))
                rw_over(act, hf)
                with act.Fori(0, UNITS - 1) as h:
                    hg_unit(hf, h, hg_tiles(0))
                hg_unit(hf, UNITS - 1, None)

        @block.vector
        def _(dve):
            begin(dve, "dve")
            dve.wait_ge(loaded_c, 48)

            def unshift(dst, src, c, mm, s, stage):
                dve.scalar_tensor_tensor(out=dst[:, :], in0=src[:, :], scalar=column(prm, COL["omm"] + c),
                                         in1=mm[:, 0:BLOCK], op0=ALU.mult, op1=ALU.add).then_inc(s.sem, s.one(stage))

            def one_plus(e, s, stage):
                dve.tensor_scalar(e, e, 1.0, None, ALU.add).then_inc(s.sem, s.one(stage))

            def mult(dst, a, b, s, stage):
                dve.tensor_tensor(dst[:, :], a[:, :], b[:, :], ALU.mult).then_inc(s.sem, s.one(stage))

            def key(kind, a, stage):
                dve.tensor_tensor(out_bk[:, :, kind, :], a[:, :].rearrange("p (c t) -> p c t", t=CHUNK),
                                  t["qq"][:, :].rearrange("p (c t) -> p c t", t=CHUNK), ALU.mult)\
                   .then_inc(RDVE.sem, RDVE.one(stage))

            def relative(s, n):
                cs = t["cs"][:, :].rearrange("p (c t) -> p c t", t=CHUNK)
                wait(dve, s, n, "cs")
                dve.tensor_tensor(t["dm"][:, :].rearrange("p (c t) -> p c t", t=CHUNK), cs,
                                  cs[:, :, CHUNK // 2:CHUNK // 2 + 1].broadcast_to([P, BC, CHUNK]), ALU.subtract)\
                   .then_inc(s.sem, s.one("dm"))

            def rw_unit(hf, p, nxt):
                u = hf * UNITS + p
                wait(dve, RPE, u * NB - 1, "a")
                dve.tensor_copy(k_a_unit[:, 0:1], column(prm, COL["k_a"] + p)).then_inc(ULD.sem, ULD.one("k_a"))
                dve.tensor_copy(k_a_unit[:, 1:2], column(prm, COL["omka"] + p)).then_inc(ULD.sem, ULD.one("omka"))
                dve.tensor_copy(lora_unit[:, :], lora2[:, bass.ds(p * P, P)]).then_inc(ULD.sem, ULD.one("lora"))
                for b in range(NB):
                    n = u * NB + b

                    def ahead(i):
                        if b == NB - 1:
                            s, his, step, tiles = nxt
                            slot, name, _ = tiles[i]
                            weights_lo(dve, s, his, step, name, slot)

                    wait(dve, RACT, n, "mk"), wait(dve, RPOOL, n, "ck")
                    wait(dve, RACT, n - 1, "sq"), wait(dve, RPOOL, n - 1, "kp")
                    unshift(t["k"], K_, UNITS + p, m["k"], RDVE, "k")
                    wait(dve, RACT, n, "ew")
                    one_plus(t["e1"][:, :], RDVE, "w1")
                    wait(dve, RDVE, n, "w1")
                    dve.reciprocal(t["s1"][:, :], t["e1"][:, :]).then_inc(RDVE.sem, RDVE.one("sg"))
                    wait(dve, RDVE, n, "sg"), wait(dve, RACT, n - 1, "ee")
                    dve.tensor_tensor_scan(t["cs"][:, :], resets[:, :], t["s1"][:, :], 0.0, ALU.mult, ALU.add)\
                       .then_inc(RDVE.sem, RDVE.one("cs"))
                    wait(dve, RACT, n - 1, "qq")
                    relative(RDVE, n)
                    wait(dve, RDVE, n, "dm"), wait(dve, RACT, n - 1, "px")
                    dve.tensor_tensor(t["dx"][:, :], t["dm"][:, :], t["s1"][:, :], ALU.subtract)\
                       .then_inc(RDVE.sem, RDVE.one("dx"))
                    wait(dve, RACT, n, "ea")
                    one_plus(t["e2"][:, :], RDVE, "a1")
                    wait(dve, RDVE, n, "a1"), wait(dve, RPOOL, n - 1, "ak")
                    dve.reciprocal(t["s2"][:, :], t["e2"][:, :]).then_inc(RDVE.sem, RDVE.one("a"))
                    ahead(0)
                    wait(dve, RACT, n, "mr"), wait(dve, RPOOL, n, "cr")
                    unshift(t["r"], R_, p, m["r"], RDVE, "r")
                    wait(dve, RDVE, n, "r"), wait(dve, RACT, n, "pp"), wait(dve, RSP, n - 1, "s")
                    mult(out["rh"], t["r"], t["pp"], RDVE, "rho")
                    wait(dve, RPE, n, "ss")
                    dve.tensor_scalar(t["ln"][:, :], SS[:, :], KK_GUARD, None, ALU.max).then_inc(RDVE.sem, RDVE.one("mx"))
                    wait(dve, RACT, n, "mv"), wait(dve, RPOOL, n, "cv")
                    unshift(out["v"], V_, 2 * UNITS + p, m["v"], RDVE, "v")
                    ahead(1)
                    wait(dve, RPOOL, n, "kp"), wait(dve, RACT, n, "qq")
                    key(1, t["kp"], "kappa")
                    dve.scalar_tensor_tensor(out=out["rk"][:, :], in0=t["r"][:, :], scalar=column(prm, COL["r_k"] + p),
                                             in1=t["kp"][:, :], op0=ALU.mult, op1=ALU.mult).then_inc(RDVE.sem, RDVE.one("rk"))
                    wait(dve, RACT, n, "inv"), wait(dve, RPOOL, n - 1, "ak")
                    dve.scalar_tensor_tensor(out=t["kk"][:, :], in0=t["k"][:, :], scalar=column(prm, COL["k_k"] + p),
                                             in1=t["ln"][:, :], op0=ALU.mult, op1=ALU.mult).then_inc(RDVE.sem, RDVE.one("kk"))
                    wait(dve, RDVE, n, "kk"), wait(dve, RACT, n, "px")
                    mult(out["al"], t["kk"], t["px"], RDVE, "alpha")
                    wait(dve, RPOOL, n, "ak")
                    key(0, t["ak"], "beta")
                    ahead(2)
                    if len(nxt[3]) > 3:
                        ahead(3)

            def hg_unit(hf, h, nxt):
                u = hf * UNITS + h
                for b in range(NB):
                    n = u * NB + b

                    def ahead(i):
                        if nxt is not None and b == NB - 1:
                            slot, name, _ = nxt[i]
                            weights_lo(dve, WHD, WHA, u + 1, name, slot)

                    wait(dve, HACT, n, "ef")
                    one_plus(t["e1"][:, :], HDVE, "f1")
                    wait(dve, HDVE, n, "f1"), wait(dve, HACT, n - 1, "lf")
                    dve.reciprocal(t["s1"][:, :], t["e1"][:, :]).then_inc(HDVE.sem, HDVE.one("sf"))
                    wait(dve, HDVE, n, "sf")
                    dve.tensor_scalar(t["tt"][:, :], t["s1"][:, :], column(prm, COL["noml"] + h),
                                      column(prm, COL["oml"] + h), ALU.mult, ALU.add).then_inc(HDVE.sem, HDVE.one("kf"))
                    wait(dve, HACT, n, "lf"), wait(dve, HACT, n - 1, "ee")
                    dve.tensor_tensor_scan(t["cs"][:, :], resets[:, :], t["dx"][:, :], 0.0, ALU.mult, ALU.add)\
                       .then_inc(HDVE.sem, HDVE.one("cs"))
                    wait(dve, HACT, n - 1, "qq")
                    relative(HDVE, n)
                    ahead(0)
                    wait(dve, HACT, n, "eq")
                    one_plus(t["e2"][:, :], HDVE, "q1")
                    wait(dve, HDVE, n, "q1")
                    dve.reciprocal(t["s2"][:, :], t["e2"][:, :]).then_inc(HDVE.sem, HDVE.one("sq"))
                    wait(dve, HDVE, n, "sq")
                    mult(t["r"], Q_, t["s2"], HDVE, "qs")
                    wait(dve, HDVE, n, "qs"), wait(dve, HACT, n, "pp"), wait(dve, HSP, n - 1, "s")
                    mult(out["al"], t["r"], t["pp"], HDVE, "qt")
                    wait(dve, HACT, n, "qq")
                    mult(out["rh"], t["tt"], t["qq"], HDVE, "kt")
                    ahead(1)
                    wait(dve, HACT, n, "eg")
                    one_plus(t["kk"][:, :], HDVE, "g1")
                    wait(dve, HDVE, n, "g1")
                    dve.reciprocal(t["ak"][:, :], t["kk"][:, :]).then_inc(HDVE.sem, HDVE.one("sg"))
                    wait(dve, HDVE, n, "sg")
                    dve.scalar_tensor_tensor(out=out["rk"][:, :], in0=G_[:, :], scalar=column(prm, COL["hgw"] + h),
                                             in1=t["ak"][:, :], op0=ALU.mult, op1=ALU.mult).then_inc(HDVE.sem, HDVE.one("gs"))
                    ahead(2)
                    ahead(3)

            dve.memset(carry[:, :], 0.0).then_inc(ULD.sem, ULD.ahead * len(ULD.names))
            dve.memset(resets[:, :], 1.0).then_inc(resets_made, 1)
            dve.wait_ge(resets_made, 1)
            dve.memset(resets[:, ::CHUNK], 0.0).then_inc(resets_made, 1)
            dve.wait_ge(resets_made, 2)
            with dve.Fori(0, HALVES) as hf:
                rw_over(dve, hf - 1)
                hg_over(dve, hf - 1)
                for slot, name, _ in lora_tiles():
                    weights_lo(dve, WLD, WLA, hf, name, slot)
                apart(dve, between["dve"])
                with dve.Fori(0, TILES // 2) as j:
                    for s in range(2):
                        n = hf * TILES + j * 2 + s
                        wait(dve, NACT, n, "rstd"), wait(dve, NPE, n - 1, "turn1")
                        dve.scalar_tensor_tensor(out=xs[:, :], in0=xt[:, s], scalar=stat[:, 2:3], in1=norm_row[:, :],
                                                 op0=ALU.mult, op1=ALU.mult).then_inc(NDVE.sem, NDVE.one("scaled"))
                        for i in range(2):
                            cols = (slice(None), slice(i * BT, (i + 1) * BT), bass.ds((j * 2 + s) * P, P))
                            wait(dve, NACT, n, f"hi{i}")
                            split_lo(dve, hT[1][cols], TURN[i], hT[0][cols]).then_inc(NDVE.sem, NDVE.one(f"lo{i}"))
                for slot, name, _ in rw_tiles(0)[:2]:
                    weights_lo(dve, WRD, WRA, hf * UNITS, name, slot)
                for b in range(NB):
                    n = hf * NB + b
                    wait(dve, LACT, n, "mixa"), wait(dve, LPOOL, n, "ca")
                    unshift(t["k"], DWDA, 3 * UNITS, m["k"], LDVE, "pa")
                    wait(dve, LACT, n, "expa")
                    one_plus(t["e1"][0:64, :], LDVE, "a1")
                    wait(dve, LDVE, n, "a1")
                    dve.reciprocal(t["s1"][0:64, :], t["e1"][0:64, :]).then_inc(LDVE.sem, LDVE.one("rec"))
                    wait(dve, LDVE, n, "rec")
                    dve.tensor_scalar(tda[0:64, b * BLOCK:(b + 1) * BLOCK], t["s1"][0:64, :], 2.0, -1.0, ALU.mult, ALU.add)\
                       .then_inc(LDVE.sem, LDVE.one("tanh"))
                    wait(dve, LACT, n, "mixg"), wait(dve, LPOOL, n, "cg")
                    unshift(t["r"], DG, 3 * UNITS + 1, m["r"], LDVE, "pg")
                    wait(dve, LACT, n, "expg")
                    one_plus(t["e2"][:, :], LDVE, "g1")
                    wait(dve, LDVE, n, "g1"), wait(dve, LSP, n - 1, "s")
                    dve.reciprocal(t["s2"][:, :], t["e2"][:, :]).then_inc(LDVE.sem, LDVE.one("sdg"))
                weights_lo(dve, WRD, WRA, hf * UNITS, "v", 2)
                lora_over(dve, hf)
                apart(dve, between["dve"])
                with dve.Fori(0, UNITS - 1) as p:
                    rw_unit(hf, p, (WRD, WRA, hf * UNITS + p + 1, rw_tiles(p + 1)))
                rw_unit(hf, UNITS - 1, (WHD, WHA, hf * UNITS, hg_tiles(0)))
                rw_over(dve, hf)
                apart(dve, between["dve"])
                with dve.Fori(0, UNITS - 1) as h:
                    hg_unit(hf, h, hg_tiles(0))
                hg_unit(hf, UNITS - 1, None)

        @block.gpsimd
        def _(pool):
            begin(pool, "pool")
            wait(pool, ULD, -1, "lora")
            pool.wait_ge(loaded_c, 48)

            def carried(mm, c, over, own, n, last, before, after, full):
                wait(pool, over, n - 1, last)
                wait(pool, own, n - 1, after)
                apart(pool, between["pool"])
                pool.tensor_copy(mm[:, 0:1], column(carry, c)).then_inc(own.sem, own.one(before))
                wait(pool, *full)
                wait(pool, own, n, before)
                apart(pool, between["pool"])
                pool.tensor_copy(column(carry, c), mm[:, BLOCK:BLOCK + 1]).then_inc(own.sem, own.one(after))

            def rw_unit(hf, p):
                u = hf * UNITS + p
                for b in range(NB):
                    n = u * NB + b
                    carried(m["k"], UNITS + p, RDVE, RPOOL, n, "k", "ck", "sk", (RACT, n, "mk"))
                    carried(m["r"], p, RDVE, RPOOL, n, "r", "cr", "sr", (RACT, n, "mr"))
                    wait(pool, RDVE, n, "a")
                    wait(pool, ULD, u, "omka")
                    apart(pool, between["pool"])
                    pool.tensor_scalar(t["tt"][:, :], t["s2"][:, :], k_a_unit[:, 0:1], k_a_unit[:, 1:2], ALU.mult, ALU.add)\
                        .then_inc(RPOOL.sem, RPOOL.one("t"))
                    wait(pool, RPOOL, n, "t"), wait(pool, RDVE, n - 1, "rk")
                    pool.tensor_tensor(t["kp"][:, :], t["k"][:, :], t["tt"][:, :], ALU.mult).then_inc(RPOOL.sem, RPOOL.one("kp"))
                    carried(m["v"], 2 * UNITS + p, RDVE, RPOOL, n, "v", "cv", "sv", (RACT, n, "mv"))
                    wait(pool, RDVE, n, "kk"), wait(pool, RDVE, n - 1, "beta")
                    pool.tensor_tensor(t["ak"][:, :], t["kk"][:, :], t["s2"][:, :], ALU.mult).then_inc(RPOOL.sem, RPOOL.one("ak"))

            with pool.Fori(0, HALVES) as hf:
                rw_over(pool, hf - 1)
                for b in range(NB):
                    n = hf * NB + b
                    carried(m["k"], 3 * UNITS, LDVE, LPOOL, n, "pa", "ca", "sa", (LACT, n, "mixa"))
                    carried(m["r"], 3 * UNITS + 1, LDVE, LPOOL, n, "pg", "cg", "sg", (LACT, n, "mixg"))
                lora_over(pool, hf)
                apart(pool, between["pool"])
                with pool.Fori(0, UNITS - 1) as p:
                    rw_unit(hf, p)
                rw_unit(hf, UNITS - 1)


def mix(nc, dims, consts, keep, A, S):
    D, T, W, COL = dims["D"], dims["T"], dims["W"], dims["COL"]
    KT = D // P
    NT = T // P
    NC = keep["NC"]
    H = W // 64
    U = W // P
    prm, ident, bd = consts["prm"], consts["ident"], consts["headsum"]
    LEVELS = (2, 4, 8, 16, 32)
    ZEROED, MASKS = 9, 4 + 6 * 3 + 3 + 4 + 3

    with ExitStack() as ctx:
        def sb(name, shape, dt=F32):
            return ctx.enter_context(nc.sbuf_tensor("m_" + name, shape, dt))

        def sem(name):
            return ctx.enter_context(nc.semaphore("m_" + name))

        wout = [sb("wout_hi", [P, KT, D], F32R), sb("wout_lo", [P, KT, D], F32R)]
        g2 = sb("g2", [P, W])
        lnw, lnb, n2row = sb("lnw", [P, W]), sb("lnb", [P, W]), sb("norm2_row", [P, D])
        ar = [sb(f"ar{i}", [P, U, 2, P]) for i in range(2)]
        bk_ch = sb("bk_ch", [P, U, 2, P])
        vr_ch = sb("vr_ch", [P, U, 2, P])
        hg_ch = sb("hg_ch", [P, U, 4, P])
        sdg = sb("sdg", [P, P])
        xt = sb("xt", [P, D])
        bk = [sb(f"bk{i}", [P, 2, W]) for i in range(2)]
        uv = [sb(f"uv{i}", [P, 2, U, 2, 64]) for i in range(2)]
        sc = [sb(f"sc{i}", [P, 2, H, P]) for i in range(2)]
        pf = [sb(f"pf{i}", [P, H, 64]) for i in range(2)]
        bv = [sb(f"bv{i}", [P, U, 2, 64]) for i in range(2)]
        at = sb("at", [P, H, 64])
        bl = [sb(f"bl{i}", [P, H, P]) for i in range(2)]
        pb = sb("pb", [P, H, P])
        ts = sb("ts", [P, H, 64])
        pst = sb("pst", [P, H, 64])
        ys = sb("ys", [P, H, 64])
        yb = sb("yb", [P, H, P])
        nst = sb("nst", [P, U, P])
        hst = sb("hst", [P, U, P])
        fb = sb("fb", [P, U, P])
        hsc = sb("hsc", [P, U, P])
        ktok, itok, gtok = sb("ktok", [P, U, P]), sb("itok", [P, U, P]), sb("gtok", [P, U, P])
        ry = sb("ry", [P, U, 2, 64])
        sq = sb("sq", [P, W])
        oh = sb("oh", [P, D])
        spl = [sb("spl_hi", [P, KT, P], F32R), sb("spl_lo", [P, KT, P], F32R)]
        bon = sb("bon", [P, H])
        st = sb("stats", [P, 8 * 6])
        lm = sb("lm", [P, 6, P])
        mk = sb("mk", [P, 2, 64])
        tri = sb("tri", [P, 2, P])
        himask = sb("himask", [P, P], I32)
        headsel = sb("headsel", [P, 2])
        bank = [ctx.enter_context(nc.psum_tensor(f"m_bank{i}", [P, 512], F32)) for i in range(8)]
        b4 = [b[:, :].rearrange("p (a b) -> p a b", a=4) for b in bank]
        b8 = [b[:, :].rearrange("p (a b) -> p a b", a=8) for b in bank]
        bp = [b[:, :].rearrange("p (a b c) -> p a b c", a=4, b=2) for b in bank]
        ystat, vstat, rstd = st[:, 0:8], st[:, 8:16], st[:, 16:24]
        ostat, orstd, xstat, xrstd = st[:, 24:28], st[:, 28:32], st[:, 32:33], st[:, 33:34]

        ldc, ldA, ldH, ldG, ldX = (sem("ld" + k) for k in "cAHGX")
        between = {k: sem("between_" + k) for k in ("sp", "pe", "dve")}
        ldW = [sem("ldW0"), sem("ldW1")]
        stX, stH = sem("st_x"), sem("st_h")
        stage = [oh[:, :], bk[1][:, :, :].rearrange("p c w -> p (c w)")]
        F3 = keep["F"][:, :].rearrange("p (u c) -> p u c", c=NC)
        setup = {k: sem("setup_" + k) for k in ("act", "dve", "pool")}
        APE = Stages(sem("a_pe"), "bk0 bk1 v bonus sc0 sc1 " + " ".join(f"y{l} z{l}" for l in LEVELS), ahead=2)
        AACT = Stages(sem("a_act"), "bk0 v0 v1 at00 at01 at10 at11 Y2 Y4 Y8 Y16 Y32a Y32b", ahead=2)
        ADVE = Stages(sem("a_dve"), "bk1 bon bv sc00 sc01 sc10 sc11 t0 t1 T2 P2a P2b T4 P4a P4b T8 P8a P8b T16 pst pfin", ahead=2)
        APOOL = Stages(sem("a_pool"), "bv b1a b1b P2 " + " ".join(f"b{l}a b{l}b" for l in LEVELS), ahead=2)
        BPE = Stages(sem("b_pe"), "r0 q0 u0 hs hk n0 y0 hi r1 q1 u1 n1 y1 hg ho hu0 o0 gate hu1 o1 ot1 ot0 op0 op1", ahead=2)
        BACT = Stages(sem("b_act"), "R0 U0 hk hi R1 U1 hg ysb sq rl re sqo ol oe oh1 oh0 sx xl xe", ahead=2)
        BDVE = Stages(sem("b_dve"), "hs a0 m0 a1 m1 sm ymu ha0 vs yn ha1 os on gy ol1 ol0 x0 x1 h", ahead=2)
        BPOOL = Stages(sem("b_pool"), "F0 F1 hm0 yw yb hm1 og", ahead=2)
        CPE = Stages(sem("c_pe"), "ht0 ht1", ahead=2)
        CACT = Stages(sem("c_act2"), "hh0 hh1", ahead=2)
        CDVE = Stages(sem("c_dve2"), "hl0 hl1", ahead=2)
        CSP = Stages(sem("c_sp"), "s", ahead=2)
        credit = {"pe": [APE, BPE, CPE], "act": [AACT, BACT, CACT], "dve": [ADVE, BDVE, CDVE], "pool": [APOOL, BPOOL],
                  "sp": [CSP]}

        def begin(eng, who):
            for s in credit[who]:
                eng.sem_inc(s.sem, s.ahead * len(s.names))

        def wait(eng, s, n, name):
            eng.wait_ge(s.sem, s.at(n, name))

        def tiles(eng, tile):
            tile(-1, 1, True, False, False)
            tile(0, 0, True, True, False)
            with eng.Fori(0, (NT - 2) // 2) as j:
                tile(2 * j + 1, 1, True, True, True)
                tile(2 * j + 2, 0, True, True, True)
            tile(NT - 1, 1, False, True, True)
            tile(NT, 0, False, False, True)

        block = ctx.enter_context(nc.Block())

        @block.sync
        def _(sp):
            begin(sp, "sp")

            def wait_sp(s, step, name):
                wait(sp, s, step, name)
                apart(sp, between["sp"])


            def load_ahead(n, s):
                for i, (dst, kinds) in enumerate(((ar[s], 0), (bk_ch, 2), (vr_ch, 4))):
                    src = S["rw"][bass.ds(n, 1)].rearrange("o p (u k) t -> p (o u) k t", k=6)[:, :, kinds:kinds + 2]
                    sp.dma_start(dst[:, :, :, :], src).then_inc(ldA, 16)

            def load_hg(n):
                sp.dma_start(hg_ch[:, :, :, :], S["hg"][bass.ds(n, 1)].rearrange("o p (u k) t -> p (o u) k t", k=4))\
                  .then_inc(ldH, 16)

            def load_gate(n):
                sp.dma_start(sdg[:, :], S["sdg"][bass.ds(n, 1)].rearrange("o p t -> p (o t)")).then_inc(ldG, 16)

            def load_x(n):
                sp.dma_start(xt[:, :], A["x"][bass.ds(n * P, P), :]).then_inc(ldX, 16)

            for k in range(KT):
                if k >= 2:
                    sp.wait_ge(setup["dve"], k - 1)
                sp.dma_start(stage[k % 2], A["w_out"][k * P:(k + 1) * P, :]).then_inc(ldW[k % 2], 16)
            load_ahead(0, 0)
            for dst, src in ((g2[:, :], A["rw_g2"]), (lnw[:, :], A["rw_ln_w"].partition_broadcast(P)),
                             (lnb[:, :], A["rw_ln_b"].partition_broadcast(P)), (n2row[:, :], A["norm2_w"].partition_broadcast(P))):
                sp.dma_start(dst, src).then_inc(ldc, 16)
            load_hg(0)
            load_gate(0)
            load_x(0)

            def tile(n, par, ahead, now, behind):
                if behind:
                    wait_sp(CDVE, n - 1, "hl1")
                    for i in range(2):
                        sp.dma_start(S["h2"][i][:, :, bass.ds((n - 1) * P, P)].rearrange("k p t -> p k t"), spl[i][:, :, :].bitcast(F32))\
                          .then_inc(stH, 16)
                    sp.wait_ge(stH, 32 * n)
                    apart(sp, between["sp"])
                    sp.sem_inc(CSP.sem, CSP.one("s"))
                if ahead and (not isinstance(n, int) or n + 2 < NT):
                    wait_sp(APE, n + 1, "sc1")
                    wait_sp(BPE, n, "q1")
                    load_ahead(n + 2, par)
                if now and (not isinstance(n, int) or n + 1 < NT):
                    wait_sp(BPE, n, "gate")
                    load_gate(n + 1)
                    wait_sp(BPE, n, "o1")
                    load_hg(n + 1)
                if now:
                    wait_sp(BDVE, n, "x1")
                    sp.dma_start(S["x2"][bass.ds(n * P, P), :], xt[:, :]).then_inc(stX, 16)
                    if not isinstance(n, int) or n + 1 < NT:
                        sp.wait_ge(stX, 16 * (n + 1))
                        apart(sp, between["sp"])
                        wait_sp(BDVE, n, "h"), wait_sp(BACT, n, "sx")
                        load_x(n + 1)
            tile(-1, 1, True, False, False)
            tile(0, 0, True, True, False)
            with sp.Fori(0, (NT - 4) // 2) as j:
                tile(2 * j + 1, 1, True, True, True)
                tile(2 * j + 2, 0, True, True, True)
            tile(NT - 3, 1, True, True, True)
            tile(NT - 2, 0, True, True, True)
            tile(NT - 1, 1, False, True, True)
            tile(NT, 0, False, False, True)
            sp.wait_ge(stX, 16 * NT)

        @block.tensor
        def _(pe):
            begin(pe, "pe")

            def mm(out, lhs, rhs, start=True, stop=True):
                return pe.matmul(out, lhs, rhs, start=start, stop=stop, skip_group_check=True)

            def A_turn(n, s):
                pe.wait_ge(ldA, 48 * (n + 1))
                for c in range(2):
                    if c == 0:
                        wait(pe, AACT, n - 1, "at10"), wait(pe, AACT, n - 1, "bk0"), wait(pe, ADVE, n - 1, "sc10")
                    else:
                        wait(pe, AACT, n - 1, "at11"), wait(pe, ADVE, n - 1, "sc11")
                    for u in range(U):
                        last = pe.transpose(b4[c][:, u], bk_ch[:, u, c], ident[:, :])
                    last.then_inc(APE.sem, APE.one(f"bk{c}"))
                wait(pe, ADVE, n - 1, "pfin")
                for u in range(U):
                    last = pe.transpose(b4[2][:, u], vr_ch[:, u, 0], ident[:, :])
                last.then_inc(APE.sem, APE.one("v"))

            def A_bonus(n):
                wait(pe, AACT, n, "bk0")
                for u in range(U):
                    last = mm(bank[0][:, 2 * u:2 * u + 2], vr_ch[:, u, 1], headsel[:, :])
                last.then_inc(APE.sem, APE.one("bonus"))

            def A_scores(n, s, c):
                if c == 0:
                    wait(pe, ADVE, n, "bon"), wait(pe, ADVE, n, "bk1")
                else:
                    wait(pe, ADVE, n, "sc00"), wait(pe, ADVE, n, "sc01")
                    wait(pe, AACT, n, "at00"), wait(pe, AACT, n, "at01")
                t = slice(c * 64, c * 64 + 64)
                for u in range(U):
                    for par in range(2):
                        rows = slice(64 * par, 64 * par + 64)
                        last = mm(b4[par][:, u], bk_ch[rows, u, c], ar[s][rows, u, :, t])
                last.then_inc(APE.sem, APE.one(f"sc{c}"))

            def A_y(n, l):
                i = LEVELS.index(l)
                wait(pe, APOOL, n, f"b{l}b")
                wait(pe, ADVE, n, "t1" if i == 0 else f"T{LEVELS[i - 1]}")
                if i == 0:
                    wait(pe, ADVE, n, "bv"), wait(pe, AACT, n, "v1")
                for h in range(H):
                    last = mm(b8[2][:, h], bl[(i + 1) % 2][:, h], ts[:, h])
                last.then_inc(APE.sem, APE.one(f"y{l}"))

            def A_z(n, l):
                i = LEVELS.index(l)
                if l == 32:
                    wait(pe, AACT, n, "Y32b"), wait(pe, ADVE, n, "pst")
                    for h in range(H):
                        last = mm(b8[2][:, h], yb[:, h], pst[:, h])
                else:
                    wait(pe, AACT, n, f"Y{l}")
                    if i == 0:
                        wait(pe, APOOL, n, "P2")
                    else:
                        wait(pe, ADVE, n, f"P{LEVELS[i - 1]}b")
                    for h in range(H):
                        last = mm(b8[2][:, h], pb[:, h], ys[:, h])
                last.then_inc(APE.sem, APE.one(f"z{l}"))

            def B_r(n, s, c):
                t = slice(c * 64, c * 64 + 64)
                if c == 0:
                    wait(pe, AACT, n, "v1"), wait(pe, ADVE, n, "sc11")
                    wait(pe, BDVE, n - 1, "gy")
                else:
                    wait(pe, BACT, n, "U0")
                apart(pe, between["pe"])
                for h in range(H):
                    mm(bp[3][t, h // 2, h % 2], sc[s][64:128, c, (h % 2) * U + h // 2, 0:64], uv[s][64:128, c, h // 2, h % 2],
                       start=(h == 0), stop=False)
                wait(pe, BDVE, n - 1 + c, f"m{1 - c}")
                for u in range(U):
                    last = mm(b4[3][t, u], ar[s][:, u, 0, t], nst[:, u], start=False)
                last.then_inc(BPE.sem, BPE.one(f"r{c}"))
                wait(pe, BDVE, n - 1, "x1")
                for u in range(U):
                    last = mm(b4[5][t, u], ar[s][:, u, 1, t], nst[:, u], start=(u == 0), stop=False)
                last.then_inc(BPE.sem, BPE.one(f"q{c}"))

            def B_u(n, s, c):
                wait(pe, BACT, n, f"R{c}"), wait(pe, ADVE, n, "pfin")
                apart(pe, between["pe"])
                for h in range(H):
                    last = mm(bp[3][0:64, h // 2, h % 2], pf[s][64 * c:64 * c + 64, (h % 2) * U + h // 2],
                              ry[64 * c:64 * c + 64, h // 2, h % 2])
                last.then_inc(BPE.sem, BPE.one(f"u{c}"))

            def B_n(n, s, c):
                t = slice(c * 64, c * 64 + 64)
                wait(pe, BACT, n, f"U{c}"), wait(pe, ADVE, n, "bk1"), wait(pe, AACT, n, "bk0")
                if c == 0:
                    wait(pe, BDVE, n - 1, "ol1")
                    wait(pe, CDVE, n - 1, "hl1")
                else:
                    wait(pe, BDVE, n, "a0")
                for u in range(U):
                    last = mm(b4[4][:, u], bk[s][:, c, u * P:(u + 1) * P], uv[s][:, c, u])
                last.then_inc(BPE.sem, BPE.one(f"n{c}"))
                for h in range(H):
                    last = mm(bp[5][t, h // 2, h % 2], sc[s][:, c, (h % 2) * U + h // 2, 64:128], uv[s][:, c, h // 2, h % 2],
                              start=False)
                last.then_inc(BPE.sem, BPE.one(f"y{c}"))

            def H_scores(n):
                pe.wait_ge(ldH, 16 * (n + 1))
                wait(pe, BDVE, n - 1, "ol0"), wait(pe, CDVE, n - 1, "hl0")
                for u in range(U):
                    last = mm(b4[6][:, u], hg_ch[:, u, 1], hg_ch[:, u, 0])
                last.then_inc(BPE.sem, BPE.one("hs"))

            def H_turn(n, kind, b, name, *free):
                for f in free:
                    wait(pe, *f)
                for u in range(U):
                    last = pe.transpose(b4[b][:, u], hg_ch[:, u, kind], ident[:, :])
                last.then_inc(BPE.sem, BPE.one(name))

            def H_o(n):
                wait(pe, BDVE, n, "hs"), wait(pe, BACT, n, "hi"), wait(pe, BACT, n, "hg")
                for u in range(U):
                    last = mm(b4[7][:, u], hsc[:, u], itok[:, u], start=(u == 0), stop=False)
                last.then_inc(BPE.sem, BPE.one("ho"))

            def H_u(n, c):
                rows = slice(64 * c, 64 * c + 64)
                if c == 0:
                    wait(pe, BACT, n, "hk")
                else:
                    wait(pe, BDVE, n, "ha0")
                for u in range(U):
                    last = mm(b4[6][:, u], ktok[rows, u], itok[rows, u])
                last.then_inc(BPE.sem, BPE.one(f"hu{c}"))

            def H_q(n, c):
                wait(pe, BPOOL, n - 1 + c, f"hm{1 - c}")
                for u in range(U):
                    last = mm(b4[7][64 * c:64 * c + 64, u], hg_ch[:, u, 0, 64 * c:64 * c + 64], hst[:, u], start=False)
                last.then_inc(BPE.sem, BPE.one(f"o{c}"))

            def tile(n, par, ahead, now, behind):
                s, t = par, 1 - par
                if behind:
                    wait(pe, BDVE, n - 1, "h")
                    for i, b in ((0, 6), (1, 4)):
                        wait(pe, BDVE, n - 1, f"ol{i}")
                        for a in range(4):
                            last = pe.transpose(b4[b][:, a], oh[:, (4 * i + a) * P:(4 * i + a + 1) * P], ident[:, :])
                        last.then_inc(CPE.sem, CPE.one(f"ht{i}"))
                if ahead:
                    A_turn(n + 1, t)
                if now:
                    B_r(n, s, 0)
                if ahead:
                    A_bonus(n + 1)
                    A_scores(n + 1, t, 0)
                if now:
                    B_u(n, s, 0)
                    H_scores(n)
                    H_turn(n, 1, 7, "hk", (BDVE, n - 1, "x0"))
                if ahead:
                    A_scores(n + 1, t, 1)
                if now:
                    B_n(n, s, 0)
                    H_turn(n, 2, 6, "hi", (BDVE, n, "hs"))
                    B_r(n, s, 1)
                    B_u(n, s, 1)
                if ahead:
                    A_y(n + 1, 2)
                if now:
                    B_n(n, s, 1)
                if ahead:
                    A_z(n + 1, 2)
                if now:
                    H_turn(n, 3, 7, "hg", (BACT, n, "hk"))
                if ahead:
                    A_y(n + 1, 4)
                if now:
                    H_o(n)
                if ahead:
                    A_z(n + 1, 4)
                if now:
                    H_u(n, 0)
                    H_q(n, 0)
                if ahead:
                    A_y(n + 1, 8)
                if now:
                    pe.wait_ge(ldG, 16 * (n + 1))
                    wait(pe, BACT, n, "U1")
                    mm(bank[3][:, :], sdg[:, :], g2[:, :]).then_inc(BPE.sem, BPE.one("gate"))
                if ahead:
                    A_z(n + 1, 8)
                if now:
                    H_u(n, 1)
                if ahead:
                    A_y(n + 1, 16)
                if now:
                    H_q(n, 1)
                if ahead:
                    A_z(n + 1, 16)
                    A_y(n + 1, 32)
                if now:
                    wait(pe, BDVE, n, "gy"), wait(pe, BDVE, n, "a1")
                    for a in range(4):
                        last = pe.transpose(b4[4][:, a], oh[:, W + a * P:W + (a + 1) * P], ident[:, :])
                    last.then_inc(BPE.sem, BPE.one("ot1"))
                if ahead:
                    A_z(n + 1, 32)
                if now:
                    wait(pe, BPOOL, n, "og"), wait(pe, BDVE, n, "ha1")
                    for a in range(4):
                        last = pe.transpose(b4[6][:, a], oh[:, a * P:(a + 1) * P], ident[:, :])
                    last.then_inc(BPE.sem, BPE.one("ot0"))
                    for i, b in ((0, 7), (1, 5)):
                        wait(pe, BDVE, n, "ol0" if i == 0 else "ymu")
                        if i == 0:
                            wait(pe, BDVE, n, "on")
                            wait(pe, BDVE, n, "ol1")
                        for k in range(KT):
                            last = three_passes(pe, bank[b][:, :], (spl[0][:, k], spl[1][:, k]),
                                                (wout[0][:, k, i * 512:(i + 1) * 512], wout[1][:, k, i * 512:(i + 1) * 512]),
                                                k == 0, k == KT - 1)
                        last.then_inc(BPE.sem, BPE.one(f"op{i}"))

            pe.wait_ge(setup["pool"], MASKS)
            pe.wait_ge(setup["dve"], KT + ZEROED)
            pe.wait_ge(ldc, 64)
            tiles(pe, tile)


        @block.scalar
        def _(act):
            begin(act, "act")
            act.preload_act_table_set(ONE_SET)
            for k in range(KT):
                act.wait_ge(ldW[k % 2], 16 * (k // 2 + 1))
                split_hi(act, wout[0][:, k], stage[k % 2]).then_inc(setup["act"], 1)
            act.wait_ge(setup["dve"], KT + ZEROED)

            def copy(dst, src, s, name, scale=1.0):
                act.activation(dst, src, ACT.Copy, scale=scale).then_inc(s.sem, s.one(name))

            def rsqrt(dst, src, width, eps, names, n):
                act.activation(dst, src, ACT.Ln, scale=1.0 / width, bias=column(prm, COL[eps])).then_inc(BACT.sem, BACT.one(names[0]))
                wait(act, BACT, n, names[0])
                act.activation(dst, dst, ACT.Exp, scale=-0.5).then_inc(BACT.sem, BACT.one(names[1]))

            def Y(n, l):
                wait(act, APE, n, f"y{l}")
                copy(ys[:, :, :], b8[2], AACT, f"Y{l}")

            def tile(n, par, ahead, now, behind):
                s, t = par, 1 - par
                if behind:
                    wait(act, BPE, n - 1, "op1")
                    for i, b in ((0, 6), (1, 4)):
                        wait(act, CPE, n - 1, f"ht{i}")
                        split_hi(act, spl[0][:, 4 * i:4 * i + 4], b4[b]).then_inc(CACT.sem, CACT.one(f"hh{i}"))
                if ahead:
                    m = n + 1
                    wait(act, APE, m, "bk0"), wait(act, BPE, m - 2, "n1")
                    copy(bk[t][:, 0], bank[0][:, :], AACT, "bk0")
                    wait(act, APE, m, "v"), wait(act, BPE, m - 2, "y1")
                    for c in range(2):
                        copy(uv[t][64:128, c], bp[2][64 * c:64 * c + 64], AACT, f"v{c}")
                if now:
                    wait(act, BPE, n, "r0"), wait(act, BDVE, n - 1, "gy")
                    copy(ry[0:64], bp[3][0:64], BACT, "R0", -1.0)
                if ahead:
                    wait(act, APOOL, m - 1, "b32b")
                    for par_ in range(2):
                        wait(act, ADVE, m, f"sc0{par_}")
                        copy(at[0:64, par_ * U:(par_ + 1) * U], b4[par_][0:64, :, 0:64], AACT, f"at0{par_}")
                if now:
                    wait(act, BPE, n, "u0")
                    copy(uv[s][0:64, 0], bp[3][0:64], BACT, "U0")
                    wait(act, BPE, n, "hk"), wait(act, BPE, n - 1, "hu1")
                    copy(ktok[:, :, :], b4[7], BACT, "hk")
                if ahead:
                    for par_ in range(2):
                        wait(act, ADVE, m, f"sc1{par_}")
                        copy(at[64:128, par_ * U:(par_ + 1) * U], b4[par_][0:64, :, 0:64], AACT, f"at1{par_}")
                if now:
                    wait(act, BPE, n, "hi")
                    copy(itok[:, :, :], b4[6], BACT, "hi")
                    wait(act, BPE, n, "r1")
                    copy(ry[64:128], bp[3][64:128], BACT, "R1", -1.0)
                    wait(act, BPE, n, "u1")
                    copy(uv[s][0:64, 1], bp[3][0:64], BACT, "U1")
                if ahead:
                    Y(m, 2)
                if now:
                    wait(act, BPE, n, "hg"), wait(act, BPOOL, n - 1, "og")
                    copy(gtok[:, :, :], b4[7], BACT, "hg")
                if ahead:
                    Y(m, 4)
                if now:
                    wait(act, BPE, n, "y1")
                    copy(ry[:, :, :, :], bp[5], BACT, "ysb")
                if ahead:
                    Y(m, 8)
                if now:
                    wait(act, BDVE, n, "ymu"), wait(act, BDVE, n - 1, "os")
                    act.activation(sq[:, :].rearrange("p (a b c) -> p a b c", a=4, b=2), ry[:, :, :, :], ACT.Square)\
                       .then_inc(BACT.sem, BACT.one("sq"))
                    wait(act, BDVE, n, "vs")
                    rsqrt(rstd, vstat, 64, "gneps", ("rl", "re"), n)
                if ahead:
                    Y(m, 16)
                if now:
                    wait(act, BPE, n, "o1")
                    act.activation(sq[:, :], bank[7][:, :], ACT.Square).then_inc(BACT.sem, BACT.one("sqo"))
                    wait(act, BDVE, n, "os"), wait(act, BDVE, n - 1, "on")
                    rsqrt(orstd, ostat, P, "eps", ("ol", "oe"), n)
                if ahead:
                    wait(act, APE, m, "y32"), wait(act, APE, m - 1, "z32")
                    for c, k in ((0, "a"), (1, "b")):
                        r = slice(64 * c, 64 * c + 64)
                        copy(yb[r, :, r], b8[2][r], AACT, "Y32" + k)
                if now:
                    wait(act, CSP, n - 1, "s")
                    for i, b in ((1, 4), (0, 6)):
                        wait(act, BPE, n, f"ot{i}")
                        split_hi(act, spl[0][:, 4 * i:4 * i + 4], b4[b]).then_inc(BACT.sem, BACT.one(f"oh{i}"))
                    wait(act, BDVE, n, "x1")
                    act.activation(oh[:, :], xt[:, :], ACT.Square, accum_out=xstat).then_inc(BACT.sem, BACT.one("sx"))
                    wait(act, BACT, n, "sx"), wait(act, BDVE, n - 1, "h")
                    rsqrt(xrstd, xstat, D, "eps", ("xl", "xe"), n)

            tiles(act, tile)

        @block.vector
        def _(dve):
            begin(dve, "dve")
            for k in range(KT):
                dve.wait_ge(setup["act"], k + 1)
                split_lo(dve, wout[1][:, k], stage[k % 2], wout[0][:, k]).then_inc(setup["dve"], 1)
            for z in (nst, hst, hsc, pb, bl[0], bl[1], yb):
                dve.memset(z[:, :, :], 0.0).then_inc(setup["dve"], 1)
            dve.tensor_copy(keep["F"][:, :], keep["L"][:, :]).then_inc(setup["dve"], 1)
            dve.wait_ge(setup["dve"], KT + 8)
            E3, L3 = (keep[k][:, :].rearrange("p (u c) -> p u c", c=NC) for k in "EL")
            dve.tensor_tensor(F3[:, :, 0:NC - 1], L3[:, :, 0:NC - 1], E3[:, :, 1:NC], ALU.mult).then_inc(setup["dve"], 1)
            dve.wait_ge(setup["dve"], KT + ZEROED)
            dve.wait_ge(setup["pool"], MASKS)
            dve.wait_ge(ldc, 64)

            def tt(dst, a, b, op, s, name):
                dve.tensor_tensor(dst, a, b, op).then_inc(s.sem, s.one(name))

            def scores(n, t, c):
                wait(dve, APE, n, f"sc{c}"), wait(dve, BPE, n - 2, "y1")
                for par in range(2):
                    tt(sc[t][:, c, par * U:(par + 1) * U], b4[par],
                       mk[:, :, :].rearrange("p a b -> p (a b)").unsqueeze(1).broadcast_to([P, U, P]), ALU.mult,
                       ADVE, f"sc{c}{par}")

            def T_(n, l):
                wait(dve, APE, n, f"z{l}")
                tt(ts[:, :, :], ts[:, :, :], b8[2], ALU.subtract, ADVE, f"T{l}")
                wait(dve, ADVE, n, f"T{l}")

            def P_(n, l):
                for c, k in ((0, "a"), (1, "b")):
                    r = slice(64 * c, 64 * c + 64)
                    dve.transpose(pb[r, :, r], ts[r]).then_inc(ADVE.sem, ADVE.one(f"P{l}{k}"))

            def state(n, c):
                wait(dve, BPE, n, f"n{c}"), wait(dve, BPE, n, f"q{c}")
                tt(nst[:, :, :], nst[:, :, :], b4[4], ALU.add, BDVE, f"a{c}")
                wait(dve, BDVE, n, f"a{c}"), wait(dve, BPOOL, n, f"F{c}")
                tt(nst[:, :, :], nst[:, :, :], fb[:, :, :], ALU.mult, BDVE, f"m{c}")

            def add_h(n, c):
                wait(dve, BPE, n, f"o{c}"), wait(dve, BPE, n, f"hu{c}"), wait(dve, BPOOL, n - 1 + c, f"hm{1 - c}")
                tt(hst[:, :, :], hst[:, :, :], b4[6], ALU.add, BDVE, f"ha{c}")

            def total(dst, src, name):
                dve.tensor_reduce(dst, src, AX.X, ALU.add).then_inc(BDVE.sem, BDVE.one(name))

            ry8 = ry[:, :, :, :].rearrange("p a b c -> p (a b) c")
            sq8 = sq[:, :].rearrange("p (a b) -> p a b", a=8)
            sq4 = sq[:, :].rearrange("p (a b) -> p a b", a=4)

            def tile(n, par, ahead, now, behind):
                s, t = par, 1 - par
                m = n + 1
                if behind:
                    for i, b in ((0, 6), (1, 4)):
                        wait(dve, CACT, n - 1, f"hh{i}")
                        split_lo(dve, spl[1][:, 4 * i:4 * i + 4], b4[b], spl[0][:, 4 * i:4 * i + 4])\
                            .then_inc(CDVE.sem, CDVE.one(f"hl{i}"))
                if ahead:
                    wait(dve, APE, m, "bk1"), wait(dve, BPE, m - 2, "n1")
                    dve.tensor_copy(bk[t][:, 1], bank[1][:, :]).then_inc(ADVE.sem, ADVE.one("bk1"))
                    wait(dve, APE, m, "bonus")
                    dve.tensor_copy(bon[:, :], bank[0][:, 0:H]).then_inc(ADVE.sem, ADVE.one("bon"))
                    wait(dve, ADVE, m, "bon"), wait(dve, AACT, m, "v1"), wait(dve, BPOOL, m - 2, "yb")
                    tt(bv[t][:, :, :, :].rearrange("p a b c -> p (a b) c"), b8[2],
                       bon[:, :].unsqueeze(2).broadcast_to([P, H, 64]), ALU.mult, ADVE, "bv")
                    scores(m, t, 0)
                    scores(m, t, 1)
                if now:
                    wait(dve, BPE, n, "hs"), wait(dve, BPE, n - 1, "ho")
                    apart(dve, between["dve"])
                    dve.copy_predicated(hsc[:, :, :], himask[:, :].unsqueeze(1).broadcast_to([P, U, P]), b4[6])\
                       .then_inc(BDVE.sem, BDVE.one("hs"))
                    state(n, 0)
                if ahead:
                    wait(dve, APOOL, m, "P2"), wait(dve, APE, m - 1, "y32")
                    for c in range(2):
                        r = slice(64 * c, 64 * c + 64)
                        dve.transpose(ts[r], pb[r, :, r]).then_inc(ADVE.sem, ADVE.one(f"t{c}"))
                if now:
                    state(n, 1)
                if ahead:
                    T_(m, 2)
                    P_(m, 2)
                if now:
                    wait(dve, BACT, n, "ysb")
                    total(ystat, ry8, "sm")
                    wait(dve, BDVE, n, "sm")
                    dve.scalar_tensor_tensor(out=ry8, in0=ystat.unsqueeze(2).broadcast_to([P, H, 64]), scalar=-1.0 / 64,
                                             in1=ry8, op0=ALU.mult, op1=ALU.add).then_inc(BDVE.sem, BDVE.one("ymu"))
                if ahead:
                    T_(m, 4)
                    P_(m, 4)
                if now:
                    add_h(n, 0)
                    wait(dve, BACT, n, "sq")
                    total(vstat, sq8, "vs")
                if ahead:
                    T_(m, 8)
                    P_(m, 8)
                if now:
                    wait(dve, BACT, n, "re")
                    tt(ry8, ry8, rstd.unsqueeze(2).broadcast_to([P, H, 64]), ALU.mult, BDVE, "yn")
                    add_h(n, 1)
                if ahead:
                    T_(m, 16)
                    dve.transpose(pst[:, :, :], ts[:, :, :]).then_inc(ADVE.sem, ADVE.one("pst"))
                if now:
                    wait(dve, BACT, n, "sqo")
                    total(ostat, sq4, "os")
                    wait(dve, BACT, n, "oe"), wait(dve, CPE, n - 1, "ht1")
                    tt(oh[:, 0:W].rearrange("p (a b) -> p a b", a=U), b4[7], orstd.unsqueeze(2).broadcast_to([P, U, P]),
                       ALU.mult, BDVE, "on")
                    wait(dve, BPOOL, n, "yb"), wait(dve, BPE, n, "gate")
                    tt(oh[:, W:D].rearrange("p (a b) -> p a b", a=H), b8[3], ry8, ALU.mult, BDVE, "gy")
                if ahead:
                    wait(dve, APE, m, "z32"), wait(dve, ADVE, m, "pst"), wait(dve, BPE, m - 2, "u1")
                    tt(pf[t][:, :, :], pst[:, :, :], b8[2], ALU.subtract, ADVE, "pfin")
                if now:
                    for i, b in ((1, 4), (0, 6)):
                        wait(dve, BACT, n, f"oh{i}")
                        split_lo(dve, spl[1][:, 4 * i:4 * i + 4], b4[b], spl[0][:, 4 * i:4 * i + 4])\
                            .then_inc(BDVE.sem, BDVE.one(f"ol{i}"))
                    dve.wait_ge(ldX, 16 * (n + 1))
                    for i, b in ((0, 7), (1, 5)):
                        wait(dve, BPE, n, f"op{i}")
                        tt(xt[:, i * 512:(i + 1) * 512], xt[:, i * 512:(i + 1) * 512], bank[b][:, :], ALU.add, BDVE, f"x{i}")
                    wait(dve, BACT, n, "xe")
                    dve.scalar_tensor_tensor(out=oh[:, :], in0=xt[:, :], scalar=xrstd, in1=n2row[:, :], op0=ALU.mult,
                                             op1=ALU.mult).then_inc(BDVE.sem, BDVE.one("h"))

            tiles(dve, tile)

        @block.gpsimd
        def _(pool):
            begin(pool, "pool")
            made = [0]

            def step(ins):
                made[0] += 1
                ins.then_inc(setup["pool"], 1)
                pool.wait_ge(setup["pool"], made[0])

            def keep_where(ap, pattern, base, per_row, op=ALU.is_ge):
                step(pool.affine_select(out=ap, in_=ap, compare_op=op, fill=0, base=base, pattern=pattern,
                                        channel_multiplier=per_row))

            step(pool.memset(headsel[:, :], 0.0))
            step(pool.memset(headsel[0:64, 0:1], 1.0))
            step(pool.memset(headsel[64:128, 1:2], 1.0))
            step(pool.memset(lm[:, :, :], 1.0))
            for i in range(6):
                L = 1 << i
                v = lm[:, i].rearrange("p (b t) -> p b t", t=2 * L)
                blocks = P // (2 * L)
                keep_where(v, [[-2 * L, blocks], [0, 2 * L]], 0, 1)
                keep_where(v, [[2 * L, blocks], [0, 2 * L]], L - 1, -1)
                keep_where(v, [[0, blocks], [1, 2 * L]], -L, 0)
            step(pool.memset(tri[:, :, :], 1.0))
            keep_where(tri[:, 0], [[1, P]], -1, -1)
            keep_where(tri[:, 1], [[1, P]], 0, -1)
            for i in range(2):
                for c in range(2):
                    r = slice(64 * c, 64 * c + 64)
                    step(pool.tensor_copy(mk[r, i], tri[r, i, r]))
            step(pool.memset(himask[:, :], 1))
            keep_where(himask[:, :], [[1, P]], 0, -1)
            step(pool.memset(himask[0:64, 64:128], 0))
            assert made[0] == MASKS, made[0]
            pool.wait_ge(setup["dve"], KT + ZEROED)
            pool.wait_ge(ldc, 64)

            def tt(dst, a, b, op, s, name):
                pool.tensor_tensor(dst, a, b, op).then_inc(s.sem, s.one(name))

            def level(n, i, *free):
                for f in free:
                    wait(pool, *f)
                for c, k in ((0, "a"), (1, "b")):
                    if c == 1:
                        wait(pool, APOOL, n, f"b{1 << i}a")
                    r = slice(64 * c, 64 * c + 64)
                    tt(bl[i % 2][r, :, r], at[r], lm[r, i, r].unsqueeze(1).broadcast_to([64, H, 64]), ALU.mult,
                       APOOL, f"b{1 << i}{k}")

            def factor(n, c):
                return keep["F"][:, :].rearrange("p (u c) -> p u c", c=NC)[:, :, bass.ds(2 * n + c, 1)]

            def fb_(n, c):
                tt(fb[:, :, :], bd[:, :].unsqueeze(1).broadcast_to([P, U, P]), factor(n, c)[:, 0:U].broadcast_to([P, U, P]),
                   ALU.mult, BPOOL, f"F{c}")

            def hm(n, c):
                wait(pool, BDVE, n, f"ha{c}")
                tt(hst[:, :, :], hst[:, :, :], factor(n, c)[:, U:2 * U].broadcast_to([P, U, P]), ALU.mult, BPOOL, f"hm{c}")

            def tile(n, par, ahead, now, behind):
                s, t = par, 1 - par
                m = n + 1
                if now:
                    wait(pool, BDVE, n - 1, "m1")
                    fb_(n, 0)
                if ahead:
                    wait(pool, ADVE, m, "bv")
                    tt(bv[t][:, :, :, :].rearrange("p a b c -> p (a b c)"), bv[t][:, :, :, :].rearrange("p a b c -> p (a b c)"),
                       lnb[:, :], ALU.add, APOOL, "bv")
                    wait(pool, AACT, m, "at11")
                    level(m, 0, (APE, m - 1, "y16"), (APOOL, m, "bv"))
                    wait(pool, APOOL, m, "b1b"), wait(pool, APE, m - 1, "z16")
                    tt(pb[:, :, :], ident[:, :].unsqueeze(1).broadcast_to([P, H, P]), bl[0][:, :, :], ALU.subtract, APOOL, "P2")
                    level(m, 1, (APE, m - 1, "y32"), (APOOL, m, "P2"))
                    wait(pool, APOOL, m, "b2b")
                if now:
                    wait(pool, BDVE, n, "m0")
                    fb_(n, 1)
                if ahead:
                    level(m, 2, (BPOOL, n, "F1"))
                    wait(pool, APOOL, m, "b4b")
                    level(m, 3, (APE, m, "y2"))
                    wait(pool, APOOL, m, "b8b")
                if now:
                    hm(n, 0)
                if ahead:
                    level(m, 4, (APE, m, "y4"), (BPOOL, n, "hm0"))
                    wait(pool, APOOL, m, "b16b")
                if now:
                    wait(pool, BDVE, n, "yn")
                    tt(ry[:, :, :, :].rearrange("p a b c -> p (a b c)"), ry[:, :, :, :].rearrange("p a b c -> p (a b c)"),
                       lnw[:, :], ALU.mult, BPOOL, "yw")
                    wait(pool, BPOOL, n, "yw"), wait(pool, APOOL, n, "bv")
                    tt(ry[:, :, :, :], ry[:, :, :, :], bv[s][:, :, :, :], ALU.add, BPOOL, "yb")
                    hm(n, 1)
                if ahead:
                    level(m, 5, (APE, m, "y8"), (BPOOL, n, "hm1"))
                    wait(pool, APOOL, m, "b32b")
                if now:
                    wait(pool, BDVE, n, "on"), wait(pool, BACT, n, "hg")
                    tt(oh[:, 0:W].rearrange("p (a b) -> p a b", a=U), oh[:, 0:W].rearrange("p (a b) -> p a b", a=U),
                       gtok[:, :, :], ALU.mult, BPOOL, "og")

            tiles(pool, tile)


def feed(nc, dims, A, S, out):
    D, T, DF = dims["D"], dims["T"], dims["F"]
    KT = D // P
    HALVES = 2
    TH = T // HALVES
    NB = TH // BLOCK
    TILES = TH // P
    GROUPS = DF // (2 * P)
    DH = D // BLOCK
    ROUNDS = TILES * DH

    with ExitStack() as ctx:
        def sb(name, shape, dt=F32):
            return ctx.enter_context(nc.sbuf_tensor("f_" + name, shape, dt))

        def sem(name):
            return ctx.enter_context(nc.semaphore("f_" + name))

        hT = [sb("hT_hi", [P, KT, TH], F32R), sb("hT_lo", [P, KT, TH], F32R)]
        acc = sb("acc", [P, TILES, D])
        mid = [sb("mid_hi", [P, 2, TH], F32R), sb("mid_lo", [P, 2, TH], F32R)]
        raw = [sb(f"raw{i}", [P, 2, KT * P]) for i in range(3)]
        wt = [[sb(f"w{i}_hi", [P, 2, KT * P], F32R), sb(f"w{i}_lo", [P, 2, KT * P], F32R)] for i in range(3)]
        silu = sb("silu", [P, 2, BLOCK])
        prod = sb("prod", [P, 2, BLOCK])
        norm_row = sb("norm_row", [P, D])
        stat = sb("stat", [P, 2 * TILES])
        bank = [ctx.enter_context(nc.psum_tensor(f"f_bank{i}", [P, BLOCK], F32)) for i in range(8)]

        loaded_n, loaded_x = sem("loaded_norm"), sem("loaded_x2")
        loaded_w = [sem("loaded_w0"), sem("loaded_w1"), sem("loaded_w2")]
        loaded_h = [sem(f"loaded_h{i}") for i in range(KT // 2)]
        stored = sem("stored")
        WACT, WDVE = Stages(sem("split_hi"), "w0 w1 w2"), Stages(sem("split_lo"), "w0 w1 w2")
        UPE = Stages(sem("up_pe"), " ".join(f"a{j}{b} b{j}{b}" for j in range(2) for b in range(NB)), ahead=1)
        UACT = Stages(sem("up_act"), " ".join(f"s{j}{b} h{j}{b}" for j in range(2) for b in range(NB)), ahead=1)
        UDVE = Stages(sem("up_dve"), " ".join(f"m{j}{b} l{j}{b}" for j in range(2) for b in range(NB)), ahead=1)
        DPE = Stages(sem("down_pe"), " ".join(f"d{i}" for i in range(ROUNDS)), ahead=1)
        DDVE = Stages(sem("down_dve"), " ".join(f"d{i}" for i in range(ROUNDS)), ahead=1)
        NACT = Stages(sem("norm_act"), " ".join(f"q{i}" for i in range(TILES)) + " root", ahead=1)
        NDVE = Stages(sem("norm_dve"), "ms rstd " + " ".join(f"y{i}" for i in range(TILES)), ahead=1)
        credit = {"pe": [UPE, DPE], "act": [UACT, NACT], "dve": [UDVE, DDVE, NDVE]}

        def begin(eng, who):
            for s in credit[who]:
                eng.sem_inc(s.sem, s.ahead * len(s.names))

        def wait(eng, s, step, name):
            eng.wait_ge(s.sem, s.at(step, name))

        def halves(eng, group, first=None, last=None):
            def half(hf, more):
                if first:
                    first(hf)
                with eng.Fori(0, GROUPS - 1) as g:
                    group(hf * GROUPS + g, g, True)
                group(hf * GROUPS + GROUPS - 1, GROUPS - 1, more)
                if last:
                    last(hf)
            with eng.Fori(0, HALVES - 1) as hf:
                half(hf, True)
            half(HALVES - 1, False)

        block = ctx.enter_context(nc.Block())

        @block.sync
        def _(sp):
            def load(g, i):
                if i < 2:
                    for k, name in enumerate(("ffn_w1", "ffn_w3")):
                        sp.dma_start(raw[i][:, k].rearrange("p (k c) -> p k c", c=P),
                                     A[name][:, bass.ds((2 * g + i) * P, P)].rearrange("(k p) c -> p k c", p=P))\
                          .then_inc(loaded_w[i], 16)
                else:
                    sp.dma_start(raw[2][:, :, :], A["ffn_w2"][bass.ds(2 * g * P, 2 * P), :].rearrange("(j p) c -> p j c", p=P))\
                      .then_inc(loaded_w[2], 16)

            def load_h(hf):
                for k in range(KT):
                    for i in range(2):
                        sp.dma_start(hT[i][:, k, :].bitcast(F32), S["h2"][i, k, :, bass.ds(hf * TH, TH)])\
                          .then_inc(loaded_h[k // 2], 16)

            def first(hf):
                wait(sp, UPE, hf * GROUPS - 1, f"b1{NB - 1}")
                load_h(hf)
                sp.wait_ge(stored, hf * TILES * 16)
                sp.dma_start(acc[:, :, :], S["x2"][bass.ds(hf * TH, TH), :].rearrange("(t p) d -> p t d", p=P))\
                  .then_inc(loaded_x, 16)

            def group(G, g, more):
                for i in range(3):
                    if more:
                        wait(sp, WDVE, G, f"w{i}")
                        load(0 if isinstance(g, int) else g + 1, i)

            def last(hf):
                for i in range(TILES):
                    wait(sp, NDVE, hf, f"y{i}")
                    sp.dma_start(out[bass.ds(hf * TH + i * P, P), :], acc[:, i]).then_inc(stored, 16)

            load(0, 0)
            load(0, 1)
            load(0, 2)
            sp.dma_start(norm_row[:, :], A["final_norm_w"].partition_broadcast(P)).then_inc(loaded_n, 16)
            halves(sp, group, first, last)
            sp.wait_ge(stored, HALVES * TILES * 16)

        @block.tensor
        def _(pe):
            begin(pe, "pe")

            def up(G, j):
                wait(pe, WACT, G, f"w{j}"), wait(pe, WDVE, G, f"w{j}")
                for b in range(NB):
                    cols = slice(b * BLOCK, (b + 1) * BLOCK)
                    for x, name in ((0, "a"), (1, "b")):
                        s, stage = (UACT, "s") if x == 0 else (UDVE, "m")
                        if j == 0:
                            wait(pe, s, G - 1, f"{stage}1{b}")
                        else:
                            wait(pe, s, G, f"{stage}0{b}")
                        for k in range(KT):
                            w = slice(k * P, (k + 1) * P)
                            end = three_passes(pe, bank[2 * b + x][:, :], (wt[j][0][:, x, w], wt[j][1][:, x, w]),
                                               (hT[0][:, k, cols], hT[1][:, k, cols]), k == 0, k == KT - 1)
                        end.then_inc(UPE.sem, UPE.one(f"{name}{j}{b}"))

            def group(G, g, more):
                up(G, 0)
                up(G, 1)
                wait(pe, WACT, G, "w2"), wait(pe, WDVE, G, "w2")
                for i in range(ROUNDS):
                    tile, half = i // DH, i % DH
                    if tile % (BLOCK // P) == 0 and half == 0:
                        wait(pe, UACT, G, f"h1{tile // (BLOCK // P)}"), wait(pe, UDVE, G, f"l1{tile // (BLOCK // P)}")
                    if i < 4:
                        wait(pe, DDVE, G - 1, f"d{ROUNDS - 4 + i}")
                    else:
                        wait(pe, DDVE, G, f"d{i - 4}")
                    tok, cols = slice(tile * P, (tile + 1) * P), slice(half * BLOCK, (half + 1) * BLOCK)
                    for j in range(2):
                        end = three_passes(pe, bank[4 + i % 4][:, :], (mid[0][:, j, tok], mid[1][:, j, tok]),
                                           (wt[2][0][:, j, cols], wt[2][1][:, j, cols]), j == 0, j == 1)
                    end.then_inc(DPE.sem, DPE.one(f"d{i}"))

            def first(hf):
                for k in range(KT // 2):
                    pe.wait_ge(loaded_h[k], (hf + 1) * 64)

            halves(pe, group, first)

        def free(eng, G, i):
            wait(eng, UPE if i < 2 else DPE, G - 1, f"b{i}{NB - 1}" if i < 2 else f"d{ROUNDS - 1}")

        @block.scalar
        def _(act):
            begin(act, "act")
            act.preload_act_table_set(SILU_SET)

            def split(G, i):
                act.wait_ge(loaded_w[i], (G + 1) * (32 if i < 2 else 16))
                free(act, G, i)
                split_hi(act, wt[i][0][:, :, :], raw[i][:, :, :]).then_inc(WACT.sem, WACT.one(f"w{i}"))

            def group(G, g, more):
                for j in range(2):
                    for b in range(NB):
                        cols = slice(b * BLOCK, (b + 1) * BLOCK)
                        wait(act, UPE, G, f"a{j}{b}")
                        if j == 0:
                            wait(act, UDVE, G - 1, f"m1{b}")
                        else:
                            wait(act, UDVE, G, f"m0{b}")
                        act.activation(silu[:, b], bank[2 * b][:, :], ACT.Silu).then_inc(UACT.sem, UACT.one(f"s{j}{b}"))
                        wait(act, UDVE, G, f"m{j}{b}"), wait(act, DPE, G - 1, f"d{ROUNDS - 1}")
                        split_hi(act, mid[0][:, j, cols], prod[:, b]).then_inc(UACT.sem, UACT.one(f"h{j}{b}"))
                    if more:
                        split(G + 1, j)
                if more:
                    split(G + 1, 2)

            def last(hf):
                G = hf * GROUPS + GROUPS - 1
                for i in range(TILES):
                    wait(act, DDVE, G, f"d{DH * i + DH - 1}")
                    act.activation(silu[:, :, :].rearrange("p a b -> p (a b)"), acc[:, i], ACT.Square,
                                   accum_out=stat[:, i:i + 1]).then_inc(NACT.sem, NACT.one(f"q{i}"))
                    wait(act, NACT, hf, f"q{i}")
                act.preload_act_table_set(SQRT_SET)
                rstd = stat[:, TILES:2 * TILES]
                wait(act, NDVE, hf, "ms")
                act.activation(rstd, rstd, ACT.Sqrt).then_inc(NACT.sem, NACT.one("root"))
                act.preload_act_table_set(SILU_SET)

            for i in range(3):
                split(0, i)
            halves(act, group, None, last)

        @block.vector
        def _(dve):
            begin(dve, "dve")
            dve.wait_ge(loaded_n, 16)

            def split(G, i):
                wait(dve, WACT, G, f"w{i}")
                free(dve, G, i)
                split_lo(dve, wt[i][1][:, :, :], raw[i][:, :, :], wt[i][0][:, :, :]).then_inc(WDVE.sem, WDVE.one(f"w{i}"))

            def group(G, g, more):
                for j in range(2):
                    for b in range(NB):
                        cols = slice(b * BLOCK, (b + 1) * BLOCK)
                        wait(dve, UPE, G, f"b{j}{b}"), wait(dve, UACT, G, f"s{j}{b}")
                        if j == 0:
                            wait(dve, UDVE, G - 1, f"l1{b}")
                        else:
                            wait(dve, UDVE, G, f"l0{b}")
                        dve.tensor_tensor(prod[:, b], silu[:, b], bank[2 * b + 1][:, :], ALU.mult)\
                           .then_inc(UDVE.sem, UDVE.one(f"m{j}{b}"))
                        wait(dve, UACT, G, f"h{j}{b}")
                        split_lo(dve, mid[1][:, j, cols], prod[:, b], mid[0][:, j, cols]).then_inc(UDVE.sem, UDVE.one(f"l{j}{b}"))
                    if more:
                        split(G + 1, j)
                for i in range(ROUNDS):
                    wait(dve, DPE, G, f"d{i}")
                    wait(dve, DDVE, G - 1, f"d{i}")
                    dst = acc[:, i // DH, (i % DH) * BLOCK:(i % DH + 1) * BLOCK]
                    dve.tensor_tensor(dst, dst, bank[4 + i % 4][:, :], ALU.add).then_inc(DDVE.sem, DDVE.one(f"d{i}"))
                if more:
                    split(G + 1, 2)

            def first(hf):
                dve.wait_ge(loaded_x, (hf + 1) * 16)

            def last(hf):
                wait(dve, NACT, hf, f"q{TILES - 1}")
                rstd = stat[:, TILES:2 * TILES]
                dve.tensor_scalar(rstd, stat[:, 0:TILES], 1.0 / D, EPS, ALU.mult, ALU.add).then_inc(NDVE.sem, NDVE.one("ms"))
                wait(dve, NACT, hf, "root")
                dve.reciprocal(rstd, rstd).then_inc(NDVE.sem, NDVE.one("rstd"))
                wait(dve, NDVE, hf, "rstd")
                for i in range(TILES):
                    dve.scalar_tensor_tensor(out=acc[:, i], in0=acc[:, i], scalar=rstd[:, i:i + 1], in1=norm_row[:, :],
                                             op0=ALU.mult, op1=ALU.mult).then_inc(NDVE.sem, NDVE.one(f"y{i}"))

            for i in range(3):
                split(0, i)
            halves(dve, group, first, last)


def prepare(nc, dims, consts, A):
    W, COL = dims["W"], dims["COL"]
    U = W // P
    prm = consts["prm"]
    with ExitStack() as ctx:
        loaded = ctx.enter_context(nc.semaphore("c_loaded"))
        made_act = ctx.enter_context(nc.semaphore("c_act"))
        made_dve = ctx.enter_context(nc.semaphore("c_dve"))
        made_pool = ctx.enter_context(nc.semaphore("c_pool"))
        made_eps = ctx.enter_context(nc.semaphore("c_eps"))
        tables = [("mix", A["rw_mix"]), ("nw0", A["rw_w0"]), ("na0", A["rw_a0"]), ("k_k", A["rw_k_k"]), ("k_a", A["rw_k_a"]),
                  ("r_k", A["rw_r_k"]), ("hgw", A["hg_norm_w"]), ("low0", A["hg_lower_bounds"][0:1]),
                  ("low1", A["hg_lower_bounds"][1:2])]

        def cols(name, n=None):
            return prm[:, COL[name]:COL[name] + (U if n is None else n)]

        block = ctx.enter_context(nc.Block())

        @block.sync
        def _(sp):
            for name, src in tables:
                if name == "r_k":
                    src = src.rearrange("o h k -> o (h k)")
                n = src.shape[1] // P
                sp.dma_start(cols(name, n), src.rearrange("o (t p) -> p (o t)", p=P),
                             allow_slow_non_contiguous=True).then_inc(loaded, 16)

        @block.gpsimd
        def _(pool):
            def step(ins, n):
                ins.then_inc(made_pool, 1)
                pool.wait_ge(made_pool, n)

            ident, headsum = consts["ident"], consts["headsum"]
            step(pool.memset(ident[:, :], 0.0), 1)
            step(pool.affine_select(out=ident[:, :], in_=ident[:, :], compare_op=ALU.not_equal, fill=1.0, base=0,
                                    pattern=[[-1, P]], channel_multiplier=1), 2)
            step(pool.memset(headsum[:, :], 0.0), 3)
            step(pool.memset(headsum[0:64, 0:64], 1.0), 4)
            step(pool.memset(headsum[64:128, 64:128], 1.0), 5)
            step(pool.memset(cols("eps", 1), EPS), 6)
            step(pool.memset(cols("gneps", 1), GN_EPS), 7)
            step(pool.memset(cols("half", 1), HALF_LN_LN_SCALE), 8)

        @block.vector
        def _(dve):
            n = [0]

            def step(ins):
                n[0] += 1
                ins.then_inc(made_dve, 1)
                dve.wait_ge(made_dve, n[0])

            dve.wait_ge(loaded, 16 * len(tables))
            step(dve.tensor_scalar(cols("omm", 14), cols("mix", 14), -1.0, 1.0, ALU.mult, ALU.add))
            step(dve.tensor_scalar(cols("omka"), cols("k_a"), -1.0, 1.0, ALU.mult, ALU.add))
            step(dve.tensor_scalar(cols("nw0"), cols("nw0"), -1.0, None, ALU.mult))
            step(dve.tensor_scalar(cols("na0"), cols("na0"), -1.0, None, ALU.mult))
            step(dve.tensor_tensor(cols("lb"), cols("low0"), cols("low1"), ALU.max))
            step(dve.tensor_tensor(cols("low0"), cols("low0"), cols("lb"), ALU.subtract))
            step(dve.tensor_tensor(cols("low1"), cols("low1"), cols("lb"), ALU.subtract))
            dve.wait_ge(made_act, 1)
            step(dve.tensor_tensor(cols("low1"), cols("low0"), cols("low1"), ALU.add))
            step(dve.reciprocal(cols("low1"), cols("low1")))
            step(dve.tensor_tensor(cols("lb"), cols("low0"), cols("low1"), ALU.mult))
            step(dve.tensor_scalar(cols("oml"), cols("lb"), -1.0, 1.0, ALU.mult, ALU.add))
            step(dve.tensor_scalar(cols("noml"), cols("oml"), -1.0, None, ALU.mult))

        @block.scalar
        def _(act):
            act.preload_act_table_set(ONE_SET)
            act.wait_ge(made_dve, 7)
            act.activation(prm[:, COL["low0"]:COL["low0"] + 2 * U], prm[:, COL["low0"]:COL["low0"] + 2 * U], ACT.Exp)\
               .then_inc(made_act, 1)


def hymba(nc, A, out):
    _, T, D = A["x"].shape
    W = D // 2
    U = W // P
    COL, c = {}, 0
    for name, n in (("mix", 14), ("omm", 14), ("nw0", U), ("na0", U), ("k_k", U), ("k_a", U), ("omka", U), ("r_k", U),
                    ("lb", U), ("oml", U), ("noml", U), ("hgw", U), ("eps", 1), ("gneps", 1), ("half", 1),
                    ("low0", U), ("low1", U)):
        COL[name] = c
        c += n
    NT, NC = T // P, T // CHUNK
    dims = {"D": D, "T": T, "W": W, "COL": COL, "F": A["ffn_w1"].shape[2]}
    A = dict(A)
    A["x"] = A["x"][0]
    for name in ("w_in", "rw_w2", "rw_a2", "rw_g2", "w_out", "ffn_w1", "ffn_w3", "ffn_w2"):
        A[name] = A[name][0]
    S = {
        "rw": nc.dram_tensor("s_rw", (NT, P, U * 6, P), F32).ap(),
        "hg": nc.dram_tensor("s_hg", (NT, P, U * 4, P), F32).ap(),
        "sdg": nc.dram_tensor("s_sdg", (NT, P, P), F32).ap(),
        "x2": nc.dram_tensor("s_x2", (T, D), F32).ap(),
        "h2": nc.dram_tensor("s_h2", (2, D // P, P, T), F32).ap(),
    }
    with ExitStack() as ctx:
        def sb(name, shape, dt=F32):
            return ctx.enter_context(nc.sbuf_tensor(name, shape, dt))

        consts = {"prm": sb("prm", [P, c]), "ident": sb("ident", [P, P]), "headsum": sb("headsum", [P, P])}
        keep = {"E": sb("keep_E", [P, 2 * U * NC]), "L": sb("keep_L", [P, 2 * U * NC]), "F": sb("keep_F", [P, 2 * U * NC]), "NC": NC}
        prepare(nc, dims, consts, A)
        project(nc, dims, consts, keep, A, S)
        mix(nc, dims, consts, keep, A, S)
        feed(nc, dims, A, S, out[0])


_INS = ["x", "norm1_w", "w_in", "hg_lower_bounds", "hg_norm_w", "rw_mix", "rw_w0", "rw_w2", "rw_a0", "rw_a2", "rw_g2",
        "rw_k_k", "rw_k_a", "rw_r_k", "rw_ln_w", "rw_ln_b", "w_out", "norm2_w", "ffn_w1", "ffn_w3", "ffn_w2", "final_norm_w"]
_OUTS = [((1, 2048, 1024), "float32")]


def kernel(**inputs):
    import numpy as _np
    import concourse.bacc as _bacc
    from concourse import mybir as _mybir
    from concourse.bass_utils import run_bass_kernel_spmd as _run

    nc = _bacc.Bacc("TRN2", target_bir_lowering=False, num_devices=1)
    arrays, args = {}, []
    for name in _INS:
        a = _np.ascontiguousarray(inputs[name])
        arrays[f"in_{name}_dram"] = a
        args.append(nc.dram_tensor(f"in_{name}_dram", a.shape, _mybir.dt.from_np(a.dtype), kind="ExternalInput").ap())
    for i, (shape, dtype) in enumerate(_OUTS):
        dt = _mybir.dt.from_np(_np.dtype(dtype))
        args.append(nc.dram_tensor(f"out_{i}_dram", shape, dt, kind="ExternalOutput").ap())
    hymba(nc, dict(zip(_INS, args)), args[-1])
    r = _run(nc, [arrays], core_ids=[0])
    got = tuple(r.results[0][f"out_{i}_dram"] for i in range(len(_OUTS)))
    return got[0]
```

```python
from contextlib import ExitStack

import concourse.bass as bass
from concourse import mybir

F32 = mybir.dt.float32
F32R = mybir.dt.float32r
I32 = mybir.dt.int32
ALU = mybir.AluOpType
ACT = mybir.ActivationFunctionType
AX = mybir.AxisListType

P = 128
CHUNK = 64
BLOCK = 512
EPS = 1e-6
GN_EPS = 64e-5
SIGMOID_CAP = 1e18
KK_GUARD = 1e-24
LN_SCALE = 65536.0
HALF_LN_LN_SCALE = 0.5 * 16 * 0.6931471805599453
DECAY = 0.6065306597126334
ONE_SET = "natural_log_exp_and_others"
SILU_SET = "silu_and_others"
SQRT_SET = "sqrt_and_others"


class Stages:

    def __init__(self, sem, names, ahead=0):
        self.sem, self.names, self.ahead, self.next = sem, names.split(), ahead, 0

    def at(self, step, name):
        return (step + self.ahead) * len(self.names) + self.names.index(name) + 1

    def one(self, name):
        assert self.names[self.next] == name, (self.names[self.next], name)
        self.next = (self.next + 1) % len(self.names)
        return 1


def apart(eng, between):
    eng.sem_inc(between, 1)


def split_hi(eng, hi, raw):
    return eng.activation(hi, raw, ACT.Copy)


def split_lo(eng, lo, raw, hi):
    return eng.tensor_tensor(lo, raw, hi.bitcast(F32), ALU.subtract)


def three_passes(eng, out, lhs, rhs, first, last):
    eng.matmul(out, lhs[0], rhs[0], start=first, stop=False)
    eng.matmul(out, lhs[0], rhs[1], start=False, stop=False)
    return eng.matmul(out, lhs[1], rhs[0], start=False, stop=last)


def column(table, c):
    return table[:, bass.ds(c, 1)]


def make_masks(pool, consts, tri, made_by):
    lm, eye, mk, himask, headsel, ident = (consts[k] for k in ("lm", "eye", "mk", "himask", "headsel", "ident"))
    made = [0]

    def step(ins):
        made[0] += 1
        ins.then_inc(made_by, 1)
        pool.wait_ge(made_by, made[0])

    def keep_where(ap, pattern, base, per_row, op=ALU.is_ge):
        step(pool.affine_select(out=ap, in_=ap, compare_op=op, fill=0, base=base, pattern=pattern,
                                channel_multiplier=per_row))

    step(pool.memset(headsel[:, :], 0.0))
    step(pool.memset(headsel[0:64, 0:1], 1.0))
    step(pool.memset(headsel[64:128, 1:2], 1.0))
    def diagonal(dst, src):
        for c in range(2):
            r = slice(64 * c, 64 * c + 64)
            step(pool.tensor_copy(dst[r], src[r, r]))

    for i in range(6):
        L = 1 << i
        v = tri[:, 0].rearrange("p (b t) -> p b t", t=2 * L)
        blocks = P // (2 * L)
        step(pool.memset(tri[:, 0], -1.0 if i == 0 else 1.0))
        keep_where(v, [[-2 * L, blocks], [0, 2 * L]], 0, 1)
        keep_where(v, [[2 * L, blocks], [0, 2 * L]], L - 1, -1)
        keep_where(v, [[0, blocks], [1, 2 * L]], -L, 0)
        diagonal(lm[:, i], tri[:, 0])
    diagonal(eye, ident)
    step(pool.memset(tri, 1.0))
    keep_where(tri[:, 0], [[1, P]], -1, -1)
    keep_where(tri[:, 1], [[1, P]], 0, -1)
    diagonal(mk[:, 0], tri[:, 0])
    diagonal(mk[:, 1], tri[:, 1])
    step(pool.memset(himask[:, :], 1))
    keep_where(himask[:, :], [[1, P]], 0, -1)
    step(pool.memset(himask[0:64, 64:128], 0))


def project(nc, dims, consts, keep, A, S):
    D, T, W = dims["D"], dims["T"], dims["W"]
    KT = D // P
    HALVES = 2
    TH = T // HALVES
    NB = TH // BLOCK
    TILES = TH // P
    BT = BLOCK // P
    BC = BLOCK // CHUNK
    UNITS = W // P
    RW0 = 4 * W
    LORA0 = RW0 + 3 * W
    COL = dims["COL"]
    prm, ident, headsum = consts["prm"], consts["ident"], consts["headsum"]
    w_in = A["w_in"]

    with ExitStack() as ctx:
        def sb(name, shape, dt=F32):
            return ctx.enter_context(nc.sbuf_tensor("p_" + name, shape, dt))

        def sem(name):
            return ctx.enter_context(nc.semaphore("p_" + name))

        hT = [sb("hT_hi", [P, KT, TH], F32R), sb("hT_lo", [P, KT, TH], F32R)]
        raw = sb("raw", [P, 4, KT, P])
        wt = [sb("w_hi", [P, 4, KT, P], F32R), sb("w_lo", [P, 4, KT, P], F32R)]
        norm_row = sb("norm_row", [P, D])
        xt = sb("xt", [P, 2, D])
        xs = sb("xs", [P, D])
        stat = sb("stat", [P, 4])
        lora2 = sb("lora2", [P, W])
        lora_unit = sb("lora_unit", [P, P])
        k_a_unit = sb("k_a_unit", [P, 2])
        tda = sb("tda", [P, max(TH, D)])
        tri = sb("tri", [P, 2, P])
        resets = sb("resets", [P, BLOCK])
        carry = sb("carry", [P, 16])
        m = {k: sb("m_" + k, [P, BLOCK + 1]) for k in "krv"}
        t = {k: sb("t_" + k, [P, BLOCK]) for k in
             "k r e1 e2 s1 s2 cs dm dx pp qq px sq ln kk tt kp ak".split()}
        out = {k: sb("out_" + k, [P, BLOCK]) for k in ("al", "rh", "v", "rk")}
        out_bk = sb("out_bk", [P, BC, 2, CHUNK])
        bank = [ctx.enter_context(nc.psum_tensor(f"p_bank{i}", [P, BLOCK], F32)) for i in range(8)]
        K_, WD, AA, R_, SS, V_ = bank[0:6]
        F_, Q_, G_, I_ = bank[6], bank[7], bank[0], bank[1]
        DWDA, DG = bank[2], bank[3]
        TURN = [bank[4 + i][:, :].rearrange("p (a b) -> p a b", a=BT) for i in range(4)]

        loaded_c, resets_made, masks_made = sem("loaded_consts"), sem("resets_made"), sem("masks_made")
        between = {k: sem("between_" + k) for k in ("sp", "pe", "act", "dve", "pool")}
        loaded_x = [sem("loaded_x0"), sem("loaded_x1")]
        loaded_l, loaded_r, loaded_h = sem("loaded_w_lora"), sem("loaded_w_rw"), sem("loaded_w_hg")
        NPE = Stages(sem("norm_pe"), "turn0 turn1", ahead=2)
        NST = Stages(sem("norm_stat"), "square ln rstd", ahead=2)
        NSC = Stages(sem("norm_scale"), "scaled", ahead=2)
        NHI, NLO = Stages(sem("norm_hi"), "hi0 hi1", ahead=2), Stages(sem("norm_lo"), "lo0 lo1", ahead=2)
        WLA, WLD = Stages(sem("split_lora_hi"), "dwda dg"), Stages(sem("split_lora_lo"), "dwda dg")
        WRA, WRD = Stages(sem("split_rw_hi"), "k r v"), Stages(sem("split_rw_lo"), "k r v")
        WHA, WHD = Stages(sem("split_hg_hi"), "f q g i"), Stages(sem("split_hg_lo"), "f q g i")
        ULD = Stages(sem("rw_unit_cols"), "k_a omka", ahead=1)
        ULL = Stages(sem("rw_unit_lora"), "lora")
        LPE = Stages(sem("lora_pe"), "dwda dg", ahead=1)
        LACT = Stages(sem("lora_act"), "mixa expa copya mixg expg", ahead=1)
        LDVE = Stages(sem("lora_dve"), "pa a1 rec tanh pg g1 sdg", ahead=1)
        LPOOL = Stages(sem("lora_pool"), "ca sa cg sg", ahead=1)
        RPE = Stages(sem("rw_pe"), "k w a r ss v", ahead=1)
        RACT = Stages(sem("rw_act"), "mk ew ea sq lw sg la a mr pp qq px ee dd mv ln inv", ahead=1)
        RDVE = Stages(sem("rw_dve"), "k w1 a1 cs dm dx r rho mx v kappa rk kk alpha beta", ahead=1)
        RPOOL = Stages(sem("rw_pool"), "ck sk cr sr t kp cv sv ak", ahead=1)
        HPE = Stages(sem("hg_pe"), "f q g i", ahead=1)
        HACT = Stages(sem("hg_act"), "ef nf sf lf eq nq sq pp qq ee dd eg ng sg i", ahead=1)
        HDVE = Stages(sem("hg_dve"), "f1 kf cs dm q1 qs qt kt g1 gs", ahead=1)
        LSP, RSP, HSP = (Stages(sem(k + "_stored"), "s", ahead=1) for k in ("lora", "rw", "hg"))
        st_lo, st_rw, st_hg = sem("st_lora"), sem("st_rw"), sem("st_hg")
        credit = {"pe": [NPE, LPE, RPE, HPE], "act": [NST, NHI, LACT, RACT, HACT],
                  "dve": [NSC, NLO, LDVE, RDVE, HDVE], "pool": [LPOOL, RPOOL], "sp": [LSP, RSP, HSP]}

        def begin(eng, who):
            for s in credit[who]:
                eng.sem_inc(s.sem, s.ahead * len(s.names))

        def lora_over(eng, hf):
            n = hf * NB + NB - 1
            eng.wait_ge(LPE.sem, LPE.at(n, "dg"))
            eng.wait_ge(LACT.sem, LACT.at(n, "expg"))
            eng.wait_ge(LDVE.sem, LDVE.at(n, "sdg"))
            eng.wait_ge(LPOOL.sem, LPOOL.at(n, "sg"))
            eng.wait_ge(LSP.sem, LSP.at(n, "s"))
            eng.wait_ge(HSP.sem, HSP.at(hf * UNITS * NB - 1, "s"))

        def rw_over(eng, hf):
            n = (hf * UNITS + UNITS) * NB - 1
            eng.wait_ge(RPE.sem, RPE.at(n, "v"))
            eng.wait_ge(RACT.sem, RACT.at(n, "inv"))
            eng.wait_ge(RDVE.sem, RDVE.at(n, "beta"))
            eng.wait_ge(RPOOL.sem, RPOOL.at(n, "ak"))
            eng.wait_ge(RSP.sem, RSP.at(n, "s"))

        def hg_over(eng, hf):
            n = (hf * UNITS + UNITS) * NB - 1
            eng.wait_ge(HPE.sem, HPE.at(n, "i"))
            eng.wait_ge(HACT.sem, HACT.at(n, "i"))
            eng.wait_ge(HDVE.sem, HDVE.at(n, "gs"))

        def lora_tiles():
            return [(2, "dwda", LORA0), (3, "dg", LORA0 + P)]

        def rw_tiles(p):
            return [(0, "k", RW0 + W + p * P), (1, "r", RW0 + p * P), (2, "v", RW0 + 2 * W + p * P)]

        def hg_tiles(h):
            return [(0, "f", W + h * P), (1, "q", h * P), (2, "g", 3 * W + h * P), (3, "i", 2 * W + h * P)]

        block = ctx.enter_context(nc.Block())

        @block.sync
        def _(sp):
            begin(sp, "sp")
            sp.dma_start(norm_row[:, :], A["norm1_w"].partition_broadcast(P)).then_inc(loaded_c, 16)
            sp.dma_start(lora2[0:64, :], A["rw_w2"]).then_inc(loaded_c, 16)
            sp.dma_start(lora2[64:128, :], A["rw_a2"]).then_inc(loaded_c, 16)

            def load(tiles, landed):
                for slot, _, first in tiles:
                    sp.dma_start(raw[:, slot], w_in[:, bass.ds(first, P)].rearrange("(k p) c -> p k c", p=P))\
                      .then_inc(landed, 16)

            def store(dst, kind, src, tile0):
                return sp.dma_start(dst[bass.ds(tile0, BT), :, kind, :].rearrange("t p k -> p t k"),
                                    src[:, :].rearrange("p (t k) -> p t k", t=BT))

            def rw_unit(hf, p, ahead):
                u = hf * UNITS + p
                for k in ("k", "r", "v"):
                    sp.wait_ge(WRD.sem, WRD.at(u, k))
                    apart(sp, between["sp"])
                load(*ahead)
                for b in range(NB):
                    n = u * NB + b
                    tile0 = hf * TILES + b * BT
                    for kind, name, stage in ((1, "rh", "rho"), (4, "v", "v"), (5, "rk", "rk"), (0, "al", "alpha")):
                        sp.wait_ge(RDVE.sem, RDVE.at(n, stage))
                        apart(sp, between["sp"])
                        store(S["rw"], p * 6 + kind, out[name], tile0).then_inc(st_rw, 16)
                    sp.wait_ge(RDVE.sem, RDVE.at(n, "beta"))
                    apart(sp, between["sp"])
                    sp.dma_start(S["rw"][bass.ds(tile0, BT), :, bass.ds(p * 6 + 2, 2), :].rearrange("t p k c -> p t (k c)"),
                                 out_bk[:, :, :, :].rearrange("p (t c) k i -> p t (c k i)", t=BT)).then_inc(st_rw, 16)
                    sp.wait_ge(st_rw, (n + 1) * 80)
                    apart(sp, between["sp"])
                    sp.sem_inc(RSP.sem, RSP.one("s"))

            def hg_unit(hf, h, ahead):
                u = hf * UNITS + h
                for k in ("f", "q", "g", "i"):
                    sp.wait_ge(WHD.sem, WHD.at(u, k))
                    apart(sp, between["sp"])
                if ahead:
                    load(*ahead)
                for b in range(NB):
                    n = u * NB + b
                    tile0 = hf * TILES + b * BT
                    for i, (src, s, stage) in enumerate(((out["al"], HDVE, "qt"), (out["rh"], HDVE, "kt"),
                                                         (out["v"], HACT, "i"), (out["rk"], HDVE, "gs"))):
                        sp.wait_ge(s.sem, s.at(n, stage))
                        apart(sp, between["sp"])
                        store(S["hg"], h * 4 + i, src, tile0).then_inc(st_hg, 16)
                    sp.wait_ge(st_hg, (n + 1) * 64)
                    apart(sp, between["sp"])
                    sp.sem_inc(HSP.sem, HSP.one("s"))

            with sp.Fori(0, HALVES) as hf:
                for s in range(2):
                    sp.wait_ge(NSC.sem, NSC.at(hf * TILES + s - 2, "scaled"))
                    apart(sp, between["sp"])
                    sp.dma_start(xt[:, s], A["x"][bass.ds((hf * TILES + s) * P, P), :]).then_inc(loaded_x[s], 16)
                load(lora_tiles(), loaded_l)
                load(rw_tiles(0)[:2], loaded_r)
                with sp.Fori(1, TILES // 2) as j:
                    for s in range(2):
                        n = hf * TILES + j * 2 + s
                        sp.wait_ge(NSC.sem, NSC.at(n - 2, "scaled"))
                        apart(sp, between["sp"])
                        sp.wait_ge(NST.sem, NST.at(n - 2, "square"))
                        apart(sp, between["sp"])
                        sp.dma_start(xt[:, s], A["x"][bass.ds(n * P, P), :]).then_inc(loaded_x[s], 16)
                sp.wait_ge(WLD.sem, WLD.at(hf, "dwda"))
                apart(sp, between["sp"])
                load(rw_tiles(0)[2:], loaded_r)
                for b in range(NB):
                    n = hf * NB + b
                    sp.wait_ge(LDVE.sem, LDVE.at(n, "sdg"))
                    apart(sp, between["sp"])
                    sp.dma_start(S["sdg"][bass.ds(hf * TILES + b * BT, BT)].rearrange("t p k -> p t k"),
                                 t["s2"][:, :].rearrange("p (t k) -> p t k", t=BT)).then_inc(st_lo, 16)
                    sp.wait_ge(st_lo, (n + 1) * 16)
                    apart(sp, between["sp"])
                    sp.sem_inc(LSP.sem, LSP.one("s"))
                with sp.Fori(0, UNITS - 1) as p:
                    rw_unit(hf, p, (rw_tiles(p + 1), loaded_r))
                rw_unit(hf, UNITS - 1, (hg_tiles(0), loaded_h))
                with sp.Fori(0, UNITS - 1) as h:
                    hg_unit(hf, h, (hg_tiles(h + 1), loaded_h))
                hg_unit(hf, UNITS - 1, None)

        def weights_hi(act, s, name, slot, landed, landings):
            act.wait_ge(landed, landings)
            split_hi(act, wt[0][:, slot], raw[:, slot]).then_inc(s.sem, s.one(name))

        def weights_lo(dve, s, his, step, name, slot):
            dve.wait_ge(his.sem, his.at(step, name))
            split_lo(dve, wt[1][:, slot], raw[:, slot], wt[0][:, slot]).then_inc(s.sem, s.one(name))

        @block.tensor
        def _(pe):
            begin(pe, "pe")

            def product(dst, slot, b):
                for k in range(KT):
                    last = three_passes(pe, dst[:, :], (wt[0][:, slot, k], wt[1][:, slot, k]),
                                        (hT[0][:, k, b * BLOCK:(b + 1) * BLOCK], hT[1][:, k, b * BLOCK:(b + 1) * BLOCK]),
                                        k == 0, k == KT - 1)
                return last

            def rw_unit(hf, p):
                u = hf * UNITS + p
                for b in range(NB):
                    n = u * NB + b

                    pe.wait_ge(WRA.sem, WRA.at(u, "k"))
                    pe.wait_ge(WRD.sem, WRD.at(u, "k"))
                    pe.wait_ge(RACT.sem, RACT.at(n - 1, "mk"))
                    pe.wait_ge(RDVE.sem, RDVE.at(n - 1, "k"))
                    product(K_, 0, b).then_inc(RPE.sem, RPE.one("k"))
                    pe.wait_ge(ULL.sem, ULL.at(u, "lora"))
                    pe.wait_ge(RACT.sem, RACT.at(n - 1, "ew"))
                    pe.matmul(WD[:, :], lora_unit[0:64, :], tda[0:64, b * BLOCK:(b + 1) * BLOCK], start=True, stop=True)\
                      .then_inc(RPE.sem, RPE.one("w"))
                    pe.wait_ge(RACT.sem, RACT.at(n - 1, "ea"))
                    pe.matmul(AA[:, :], lora_unit[64:128, :], tda[64:128, b * BLOCK:(b + 1) * BLOCK], start=True, stop=True)\
                      .then_inc(RPE.sem, RPE.one("a"))
                    pe.wait_ge(WRA.sem, WRA.at(u, "r"))
                    pe.wait_ge(WRD.sem, WRD.at(u, "r"))
                    pe.wait_ge(RACT.sem, RACT.at(n - 1, "mr"))
                    pe.wait_ge(RDVE.sem, RDVE.at(n - 1, "r"))
                    product(R_, 1, b).then_inc(RPE.sem, RPE.one("r"))
                    pe.wait_ge(RDVE.sem, RDVE.at(n - 1, "mx"))
                    pe.wait_ge(RACT.sem, RACT.at(n, "sq"))
                    pe.matmul(SS[:, :], headsum[:, :], t["sq"][:, :], start=True, stop=True)\
                      .then_inc(RPE.sem, RPE.one("ss"))
                    pe.wait_ge(WRA.sem, WRA.at(u, "v"))
                    pe.wait_ge(WRD.sem, WRD.at(u, "v"))
                    pe.wait_ge(RACT.sem, RACT.at(n - 1, "mv"))
                    pe.wait_ge(RDVE.sem, RDVE.at(n - 1, "v"))
                    product(V_, 2, b).then_inc(RPE.sem, RPE.one("v"))

            def hg_unit(hf, h):
                u = hf * UNITS + h
                for b in range(NB):
                    n = u * NB + b
                    pe.wait_ge(WHA.sem, WHA.at(u, "f"))
                    pe.wait_ge(WHD.sem, WHD.at(u, "f"))
                    pe.wait_ge(HACT.sem, HACT.at(n - 1, "ef"))
                    product(F_, 0, b).then_inc(HPE.sem, HPE.one("f"))
                    pe.wait_ge(WHA.sem, WHA.at(u, "q"))
                    pe.wait_ge(WHD.sem, WHD.at(u, "q"))
                    pe.wait_ge(HACT.sem, HACT.at(n - 1, "eq"))
                    pe.wait_ge(HDVE.sem, HDVE.at(n - 1, "qs"))
                    product(Q_, 1, b).then_inc(HPE.sem, HPE.one("q"))
                    pe.wait_ge(WHA.sem, WHA.at(u, "g"))
                    pe.wait_ge(WHD.sem, WHD.at(u, "g"))
                    pe.wait_ge(HACT.sem, HACT.at(n - 1, "eg"))
                    pe.wait_ge(HDVE.sem, HDVE.at(n - 1, "gs"))
                    product(G_, 2, b).then_inc(HPE.sem, HPE.one("g"))
                    pe.wait_ge(WHA.sem, WHA.at(u, "i"))
                    pe.wait_ge(WHD.sem, WHD.at(u, "i"))
                    pe.wait_ge(HACT.sem, HACT.at(n - 1, "i"))
                    product(I_, 3, b).then_inc(HPE.sem, HPE.one("i"))

            with pe.Fori(0, HALVES) as hf:
                pe.wait_ge(HACT.sem, HACT.at(hf * UNITS * NB - 1, "i"))
                pe.wait_ge(HDVE.sem, HDVE.at(hf * UNITS * NB - 1, "gs"))
                apart(pe, between["pe"])
                with pe.Fori(0, TILES // 2) as j:
                    for s in range(2):
                        n = hf * TILES + j * 2 + s
                        pe.wait_ge(NSC.sem, NSC.at(n, "scaled"))
                        for i in range(2):
                            pe.wait_ge(NHI.sem, NHI.at(n - 2, f"hi{i}"))
                            pe.wait_ge(NLO.sem, NLO.at(n - 2, f"lo{i}"))
                            for a in range(BT):
                                k = i * BT + a
                                last = pe.transpose(TURN[2 * s + i][:, a], xs[:, k * P:(k + 1) * P], ident[:, :])
                            last.then_inc(NPE.sem, NPE.one(f"turn{i}"))
                pe.wait_ge(NHI.sem, NHI.at(hf * TILES + TILES - 1, "hi1"))
                pe.wait_ge(NLO.sem, NLO.at(hf * TILES + TILES - 1, "lo1"))
                for b in range(NB):
                    n = hf * NB + b
                    pe.wait_ge(WLD.sem, WLD.at(hf, "dwda"))
                    pe.wait_ge(LACT.sem, LACT.at(n - 1, "copya"))
                    pe.wait_ge(LDVE.sem, LDVE.at(n - 1, "pa"))
                    product(DWDA, 2, b).then_inc(LPE.sem, LPE.one("dwda"))
                    pe.wait_ge(WLD.sem, WLD.at(hf, "dg"))
                    pe.wait_ge(LACT.sem, LACT.at(n - 1, "mixg"))
                    pe.wait_ge(LDVE.sem, LDVE.at(n - 1, "pg"))
                    product(DG, 3, b).then_inc(LPE.sem, LPE.one("dg"))
                pe.wait_ge(LACT.sem, LACT.at(hf * NB + NB - 1, "mixg"))
                pe.wait_ge(LDVE.sem, LDVE.at(hf * NB + NB - 1, "pg"))
                apart(pe, between["pe"])
                with pe.Fori(0, UNITS - 1) as p:
                    rw_unit(hf, p)
                rw_unit(hf, UNITS - 1)
                n = (hf * UNITS + UNITS) * NB - 1
                pe.wait_ge(RACT.sem, RACT.at(n, "ew"))
                pe.wait_ge(RDVE.sem, RDVE.at(n, "k"))
                apart(pe, between["pe"])
                with pe.Fori(0, UNITS - 1) as h:
                    hg_unit(hf, h)
                hg_unit(hf, UNITS - 1)

        @block.scalar
        def _(act):
            begin(act, "act")
            act.preload_act_table_set(ONE_SET)

            def sigmoid(dst, e, s, n, ln, stage):
                act.activation(e[:, :], e[:, :], ACT.Ln, bias=column(prm, COL["one"])).then_inc(s.sem, s.one(ln))
                act.wait_ge(s.sem, s.at(n, ln))
                act.activation(dst[:, :], e[:, :], ACT.Exp, scale=-1.0).then_inc(s.sem, s.one(stage))

            def shifted(dst, src, mixcol, s, stage):
                apart(act, between["act"])
                act.activation(dst[:, 1:BLOCK + 1], src[:, :], ACT.Copy, scale=column(prm, mixcol))\
                   .then_inc(s.sem, s.one(stage))

            def rw_unit(hf, p, nxt):
                u = hf * UNITS + p
                for b in range(NB):
                    n = u * NB + b
                    chunk0 = (hf * NB + b) * BC

                    def ahead(i, freed):
                        if nxt is None or b < NB - 1:
                            return
                        s, landed, landings, tiles = nxt
                        act.wait_ge(RPE.sem, RPE.at(n, freed))
                        slot, name, _ = tiles[i]
                        weights_hi(act, s, name, slot, landed, landings)

                    act.wait_ge(RPE.sem, RPE.at(n, "k"))
                    act.wait_ge(RDVE.sem, RDVE.at(n - 1, "k"))
                    act.wait_ge(RPOOL.sem, RPOOL.at(n - 1, "sk"))
                    shifted(m["k"], K_, COL["mix"] + UNITS + p, RACT, "mk")
                    act.wait_ge(RPE.sem, RPE.at(n, "w"))
                    act.wait_ge(RACT.sem, RACT.at(n - 1, "sg"))
                    apart(act, between["act"])
                    act.activation(t["e1"][:, :], WD[:, :], ACT.Exp, scale=-1.0, bias=column(prm, COL["nw0"] + p))\
                       .then_inc(RACT.sem, RACT.one("ew"))
                    act.wait_ge(RPE.sem, RPE.at(n, "a"))
                    act.wait_ge(RACT.sem, RACT.at(n - 1, "a"))
                    apart(act, between["act"])
                    act.activation(t["e2"][:, :], AA[:, :], ACT.Exp, scale=-1.0, bias=column(prm, COL["na0"] + p))\
                       .then_inc(RACT.sem, RACT.one("ea"))
                    act.wait_ge(RDVE.sem, RDVE.at(n, "k"))
                    act.wait_ge(RPE.sem, RPE.at(n - 1, "ss"))
                    apart(act, between["act"])
                    act.activation(t["sq"][:, :], t["k"][:, :], ACT.Square, scale=column(prm, COL["k_k"] + p))\
                       .then_inc(RACT.sem, RACT.one("sq"))
                    act.wait_ge(RDVE.sem, RDVE.at(n - 1, "dx"))
                    act.wait_ge(RDVE.sem, RDVE.at(n, "w1"))
                    sigmoid(t["s1"], t["e1"], RACT, n, "lw", "sg")
                    act.wait_ge(RPOOL.sem, RPOOL.at(n - 1, "ak"))
                    act.wait_ge(RDVE.sem, RDVE.at(n, "a1"))
                    sigmoid(t["s2"], t["e2"], RACT, n, "la", "a")
                    ahead(0, "k")
                    act.wait_ge(RPE.sem, RPE.at(n, "r"))
                    act.wait_ge(RDVE.sem, RDVE.at(n - 1, "r"))
                    act.wait_ge(RPOOL.sem, RPOOL.at(n - 1, "sr"))
                    shifted(m["r"], R_, COL["mix"] + p, RACT, "mr")
                    act.wait_ge(RDVE.sem, RDVE.at(n, "dm"))
                    act.wait_ge(RDVE.sem, RDVE.at(n - 1, "rho"))
                    act.activation(t["pp"][:, :], t["dm"][:, :], ACT.Exp, scale=-DECAY).then_inc(RACT.sem, RACT.one("pp"))
                    act.wait_ge(RDVE.sem, RDVE.at(n - 1, "beta"))
                    act.activation(t["qq"][:, :], t["dm"][:, :], ACT.Exp, scale=DECAY).then_inc(RACT.sem, RACT.one("qq"))
                    act.wait_ge(RDVE.sem, RDVE.at(n, "dx"))
                    act.activation(t["px"][:, :], t["dx"][:, :], ACT.Exp, scale=-DECAY).then_inc(RACT.sem, RACT.one("px"))
                    act.activation(keep["E"][:, bass.ds(p * keep["NC"] + chunk0, BC)],
                                   t["cs"][:, CHUNK // 2::CHUNK], ACT.Exp, scale=-DECAY).then_inc(RACT.sem, RACT.one("ee"))
                    act.wait_ge(RACT.sem, RACT.at(n, "pp"))
                    act.activation(keep["L"][:, bass.ds(p * keep["NC"] + chunk0, BC)],
                                   t["pp"][:, CHUNK - 1::CHUNK], ACT.Copy).then_inc(RACT.sem, RACT.one("dd"))
                    act.wait_ge(RPE.sem, RPE.at(n, "v"))
                    act.wait_ge(RDVE.sem, RDVE.at(n - 1, "v"))
                    act.wait_ge(RPOOL.sem, RPOOL.at(n - 1, "sv"))
                    shifted(m["v"], V_, COL["mix"] + 2 * UNITS + p, RACT, "mv")
                    ahead(1, "r")
                    act.wait_ge(RDVE.sem, RDVE.at(n, "mx"))
                    act.activation(t["ln"][:, :], t["ln"][:, :], ACT.Ln, scale=LN_SCALE).then_inc(RACT.sem, RACT.one("ln"))
                    act.wait_ge(RACT.sem, RACT.at(n, "ln"))
                    act.activation(t["ln"][:, :], t["ln"][:, :], ACT.Exp, scale=-0.5, bias=column(prm, COL["half"]))\
                       .then_inc(RACT.sem, RACT.one("inv"))
                    ahead(2, "v")
                    if nxt is not None and len(nxt[3]) > 3:
                        ahead(3, "v")

            def hg_unit(hf, h, nxt):
                u = hf * UNITS + h
                for b in range(NB):
                    n = u * NB + b
                    chunk0 = (hf * NB + b) * BC

                    def ahead(i):
                        if nxt is None or b < NB - 1:
                            return
                        slot, name, _ = nxt[i]
                        act.wait_ge(HPE.sem, HPE.at(n, name))
                        weights_hi(act, WHA, name, slot, loaded_h, (u + 2) * 64)

                    act.wait_ge(HPE.sem, HPE.at(n, "f"))
                    act.wait_ge(HACT.sem, HACT.at(n - 1, "sf"))
                    act.activation(t["e1"][:, :], F_[:, :], ACT.Exp, scale=-1.0).then_inc(HACT.sem, HACT.one("ef"))
                    act.wait_ge(HDVE.sem, HDVE.at(n - 1, "cs"))
                    act.wait_ge(HDVE.sem, HDVE.at(n, "f1"))
                    sigmoid(t["s1"], t["e1"], HACT, n, "nf", "sf")
                    act.wait_ge(HACT.sem, HACT.at(n, "sf"))
                    apart(act, between["act"])
                    act.activation(t["dx"][:, :], t["s1"][:, :], ACT.Ln, scale=column(prm, COL["oml"] + h),
                                   bias=column(prm, COL["lb"] + h)).then_inc(HACT.sem, HACT.one("lf"))
                    ahead(0)
                    act.wait_ge(HPE.sem, HPE.at(n, "q"))
                    act.wait_ge(HACT.sem, HACT.at(n - 1, "sq"))
                    act.activation(t["e2"][:, :], Q_[:, :], ACT.Exp, scale=-1.0).then_inc(HACT.sem, HACT.one("eq"))
                    act.wait_ge(HDVE.sem, HDVE.at(n - 1, "qs"))
                    act.wait_ge(HDVE.sem, HDVE.at(n, "q1"))
                    sigmoid(t["s2"], t["e2"], HACT, n, "nq", "sq")
                    act.wait_ge(HDVE.sem, HDVE.at(n, "dm"))
                    act.activation(t["pp"][:, :], t["dm"][:, :], ACT.Exp).then_inc(HACT.sem, HACT.one("pp"))
                    act.activation(t["qq"][:, :], t["dm"][:, :], ACT.Exp, scale=-1.0).then_inc(HACT.sem, HACT.one("qq"))
                    act.activation(keep["E"][:, bass.ds((UNITS + h) * keep["NC"] + chunk0, BC)],
                                   t["cs"][:, CHUNK // 2::CHUNK], ACT.Exp).then_inc(HACT.sem, HACT.one("ee"))
                    act.wait_ge(HACT.sem, HACT.at(n, "pp"))
                    act.activation(keep["L"][:, bass.ds((UNITS + h) * keep["NC"] + chunk0, BC)],
                                   t["pp"][:, CHUNK - 1::CHUNK], ACT.Copy).then_inc(HACT.sem, HACT.one("dd"))
                    ahead(1)
                    act.wait_ge(HPE.sem, HPE.at(n, "g"))
                    act.wait_ge(HACT.sem, HACT.at(n - 1, "sg"))
                    act.activation(t["kk"][:, :], G_[:, :], ACT.Exp, scale=-1.0).then_inc(HACT.sem, HACT.one("eg"))
                    ahead(2)
                    act.wait_ge(HDVE.sem, HDVE.at(n - 1, "gs"))
                    act.wait_ge(HDVE.sem, HDVE.at(n, "g1"))
                    sigmoid(t["ak"], t["kk"], HACT, n, "ng", "sg")
                    act.wait_ge(HPE.sem, HPE.at(n, "i"))
                    act.wait_ge(HSP.sem, HSP.at(n - 1, "s"))
                    act.activation(out["v"][:, :], I_[:, :], ACT.Copy).then_inc(HACT.sem, HACT.one("i"))
                    ahead(3)

            with act.Fori(0, HALVES) as hf:
                rw_over(act, hf - 1)
                hg_over(act, hf - 1)

                def stats(j, s):
                    n = hf * TILES + j * 2 + s
                    act.wait_ge(loaded_x[s], (hf * (TILES // 2) + j + 1) * 16)
                    act.activation(tda[:, 0:D], xt[:, s], ACT.Square, accum_out=stat[:, 0:1]).then_inc(NST.sem, NST.one("square"))
                    act.wait_ge(NST.sem, NST.at(n, "square"))
                    act.activation(stat[:, 1:2], stat[:, 0:1], ACT.Ln, scale=1.0 / D, bias=column(prm, COL["eps"]))\
                       .then_inc(NST.sem, NST.one("ln"))
                    act.wait_ge(NST.sem, NST.at(n, "ln"))
                    act.wait_ge(NSC.sem, NSC.at(n - 1, "scaled"))
                    act.activation(stat[:, 2:3], stat[:, 1:2], ACT.Exp, scale=-0.5).then_inc(NST.sem, NST.one("rstd"))

                def hi(j, s):
                    n = hf * TILES + j * 2 + s
                    for i in range(2):
                        act.wait_ge(NPE.sem, NPE.at(n, f"turn{i}"))
                        split_hi(act, hT[0][:, i * BT:(i + 1) * BT, bass.ds((j * 2 + s) * P, P)], TURN[2 * s + i])\
                            .then_inc(NHI.sem, NHI.one(f"hi{i}"))

                stats(0, 0)
                apart(act, between["act"])
                with act.Fori(0, TILES // 2 - 1) as j:
                    stats(j, 1)
                    hi(j, 0)
                    stats(j + 1, 0)
                    hi(j, 1)
                for slot, name, _ in lora_tiles():
                    weights_hi(act, WLA, name, slot, loaded_l, (hf + 1) * 32)
                stats(TILES // 2 - 1, 1)
                hi(TILES // 2 - 1, 0)
                hi(TILES // 2 - 1, 1)
                for slot, name, _ in rw_tiles(0)[:2]:
                    weights_hi(act, WRA, name, slot, loaded_r, (hf * UNITS + 1) * 48)
                for b in range(NB):
                    n = hf * NB + b
                    act.wait_ge(LPE.sem, LPE.at(n, "dwda"))
                    act.wait_ge(LDVE.sem, LDVE.at(n - 1, "pa"))
                    act.wait_ge(LPOOL.sem, LPOOL.at(n - 1, "sa"))
                    shifted(m["k"], DWDA, COL["mix"] + 3 * UNITS, LACT, "mixa")
                    act.wait_ge(LDVE.sem, LDVE.at(n, "pa"))
                    act.wait_ge(LDVE.sem, LDVE.at(n - 1, "rec"))
                    act.activation(t["e1"][0:64, :], t["k"][0:64, :], ACT.Exp, scale=-2.0).then_inc(LACT.sem, LACT.one("expa"))
                    act.activation(tda[64:128, b * BLOCK:(b + 1) * BLOCK], t["k"][64:128, :], ACT.Copy)\
                       .then_inc(LACT.sem, LACT.one("copya"))
                    act.wait_ge(LPE.sem, LPE.at(n, "dg"))
                    act.wait_ge(LDVE.sem, LDVE.at(n - 1, "pg"))
                    act.wait_ge(LPOOL.sem, LPOOL.at(n - 1, "sg"))
                    shifted(m["r"], DG, COL["mix"] + 3 * UNITS + 1, LACT, "mixg")
                    act.wait_ge(LDVE.sem, LDVE.at(n, "pg"))
                    act.wait_ge(LDVE.sem, LDVE.at(n - 1, "sdg"))
                    act.activation(t["e2"][:, :], t["r"][:, :], ACT.Exp, scale=-1.0).then_inc(LACT.sem, LACT.one("expg"))
                act.wait_ge(LPE.sem, LPE.at(hf * NB + NB - 1, "dwda"))
                weights_hi(act, WRA, "v", 2, loaded_r, (hf * UNITS + 1) * 48)
                lora_over(act, hf)
                with act.Fori(0, UNITS - 1) as p:
                    rw_unit(hf, p, (WRA, loaded_r, (hf * UNITS + p + 2) * 48, rw_tiles(p + 1)))
                rw_unit(hf, UNITS - 1, (WHA, loaded_h, (hf * UNITS + 1) * 64, hg_tiles(0)))
                rw_over(act, hf)
                with act.Fori(0, UNITS - 1) as h:
                    hg_unit(hf, h, hg_tiles(0))
                hg_unit(hf, UNITS - 1, None)

        @block.vector
        def _(dve):
            begin(dve, "dve")
            dve.wait_ge(loaded_c, 48)

            def unshift(dst, src, c, mm, s, stage):
                dve.scalar_tensor_tensor(out=dst[:, :], in0=src[:, :], scalar=column(prm, COL["omm"] + c),
                                         in1=mm[:, 0:BLOCK], op0=ALU.mult, op1=ALU.add).then_inc(s.sem, s.one(stage))

            def one_plus(e, s, stage):
                dve.tensor_scalar(e, e, 1.0, None, ALU.add).then_inc(s.sem, s.one(stage))

            def cap(e, s, stage):
                dve.tensor_scalar(e[:, :], e[:, :], SIGMOID_CAP, None, ALU.min).then_inc(s.sem, s.one(stage))

            def mult(dst, a, b, s, stage):
                dve.tensor_tensor(dst[:, :], a[:, :], b[:, :], ALU.mult).then_inc(s.sem, s.one(stage))

            def key(kind, a, stage):
                dve.tensor_tensor(out_bk[:, :, kind, :], a[:, :].rearrange("p (c t) -> p c t", t=CHUNK),
                                  t["qq"][:, :].rearrange("p (c t) -> p c t", t=CHUNK), ALU.mult)\
                   .then_inc(RDVE.sem, RDVE.one(stage))

            def relative(s, n):
                cs = t["cs"][:, :].rearrange("p (c t) -> p c t", t=CHUNK)
                dve.wait_ge(s.sem, s.at(n, "cs"))
                dve.tensor_tensor(t["dm"][:, :].rearrange("p (c t) -> p c t", t=CHUNK), cs,
                                  cs[:, :, CHUNK // 2:CHUNK // 2 + 1].broadcast_to([P, BC, CHUNK]), ALU.subtract)\
                   .then_inc(s.sem, s.one("dm"))

            def lora_of(p):
                dve.tensor_copy(lora_unit[:, :], lora2[:, bass.ds(p * P, P)]).then_inc(ULL.sem, ULL.one("lora"))

            def rw_unit(hf, p, nxt):
                u = hf * UNITS + p
                dve.wait_ge(RPOOL.sem, RPOOL.at(u * NB - 1, "t"))
                dve.tensor_copy(k_a_unit[:, 0:1], column(prm, COL["k_a"] + p)).then_inc(ULD.sem, ULD.one("k_a"))
                dve.tensor_copy(k_a_unit[:, 1:2], column(prm, COL["omka"] + p)).then_inc(ULD.sem, ULD.one("omka"))
                for b in range(NB):
                    n = u * NB + b

                    def ahead(i):
                        if b == NB - 1:
                            s, his, step, tiles = nxt
                            slot, name, _ = tiles[i]
                            weights_lo(dve, s, his, step, name, slot)

                    dve.wait_ge(RACT.sem, RACT.at(n, "mk"))
                    dve.wait_ge(RPOOL.sem, RPOOL.at(n, "ck"))
                    dve.wait_ge(RACT.sem, RACT.at(n - 1, "sq"))
                    dve.wait_ge(RPOOL.sem, RPOOL.at(n - 1, "kp"))
                    unshift(t["k"], K_, UNITS + p, m["k"], RDVE, "k")
                    dve.wait_ge(RACT.sem, RACT.at(n, "ew"))
                    cap(t["e1"], RDVE, "w1")
                    dve.wait_ge(RACT.sem, RACT.at(n, "ea"))
                    cap(t["e2"], RDVE, "a1")
                    dve.wait_ge(RACT.sem, RACT.at(n, "sg"))
                    dve.tensor_tensor_scan(t["cs"][:, :], resets[:, :], t["s1"][:, :], 0.0, ALU.mult, ALU.add)\
                       .then_inc(RDVE.sem, RDVE.one("cs"))
                    relative(RDVE, n)
                    dve.wait_ge(RDVE.sem, RDVE.at(n, "dm"))
                    dve.tensor_tensor(t["dx"][:, :], t["dm"][:, :], t["s1"][:, :], ALU.subtract)\
                       .then_inc(RDVE.sem, RDVE.one("dx"))
                    ahead(0)
                    if b == NB - 1 and len(nxt[3]) == 3:
                        dve.wait_ge(RPE.sem, RPE.at(n, "a"))
                        lora_of(p + 1)
                    dve.wait_ge(RACT.sem, RACT.at(n, "mr"))
                    dve.wait_ge(RPOOL.sem, RPOOL.at(n, "cr"))
                    unshift(t["r"], R_, p, m["r"], RDVE, "r")
                    dve.wait_ge(RDVE.sem, RDVE.at(n, "r"))
                    dve.wait_ge(RACT.sem, RACT.at(n, "pp"))
                    dve.wait_ge(RSP.sem, RSP.at(n - 1, "s"))
                    mult(out["rh"], t["r"], t["pp"], RDVE, "rho")
                    dve.wait_ge(RPE.sem, RPE.at(n, "ss"))
                    dve.tensor_scalar(t["ln"][:, :], SS[:, :], KK_GUARD, None, ALU.max).then_inc(RDVE.sem, RDVE.one("mx"))
                    dve.wait_ge(RACT.sem, RACT.at(n, "mv"))
                    dve.wait_ge(RPOOL.sem, RPOOL.at(n, "cv"))
                    unshift(out["v"], V_, 2 * UNITS + p, m["v"], RDVE, "v")
                    ahead(1)
                    dve.wait_ge(RPOOL.sem, RPOOL.at(n, "kp"))
                    dve.wait_ge(RACT.sem, RACT.at(n, "qq"))
                    key(1, t["kp"], "kappa")
                    dve.scalar_tensor_tensor(out=out["rk"][:, :], in0=t["r"][:, :], scalar=column(prm, COL["r_k"] + p),
                                             in1=t["kp"][:, :], op0=ALU.mult, op1=ALU.mult).then_inc(RDVE.sem, RDVE.one("rk"))
                    dve.wait_ge(RACT.sem, RACT.at(n, "inv"))
                    dve.wait_ge(RPOOL.sem, RPOOL.at(n - 1, "ak"))
                    dve.scalar_tensor_tensor(out=t["kk"][:, :], in0=t["k"][:, :], scalar=column(prm, COL["k_k"] + p),
                                             in1=t["ln"][:, :], op0=ALU.mult, op1=ALU.mult).then_inc(RDVE.sem, RDVE.one("kk"))
                    dve.wait_ge(RDVE.sem, RDVE.at(n, "kk"))
                    dve.wait_ge(RACT.sem, RACT.at(n, "px"))
                    mult(out["al"], t["kk"], t["px"], RDVE, "alpha")
                    dve.wait_ge(RPOOL.sem, RPOOL.at(n, "ak"))
                    key(0, t["ak"], "beta")
                    ahead(2)
                    if len(nxt[3]) > 3:
                        ahead(3)

            def hg_unit(hf, h, nxt):
                u = hf * UNITS + h
                for b in range(NB):
                    n = u * NB + b

                    def ahead(i):
                        if nxt is not None and b == NB - 1:
                            slot, name, _ = nxt[i]
                            weights_lo(dve, WHD, WHA, u + 1, name, slot)

                    dve.wait_ge(HACT.sem, HACT.at(n, "ef"))
                    cap(t["e1"], HDVE, "f1")
                    dve.wait_ge(HACT.sem, HACT.at(n, "sf"))
                    dve.tensor_scalar(t["tt"][:, :], t["s1"][:, :], column(prm, COL["noml"] + h),
                                      column(prm, COL["oml"] + h), ALU.mult, ALU.add).then_inc(HDVE.sem, HDVE.one("kf"))
                    dve.wait_ge(HACT.sem, HACT.at(n, "lf"))
                    dve.wait_ge(HACT.sem, HACT.at(n - 1, "ee"))
                    dve.tensor_tensor_scan(t["cs"][:, :], resets[:, :], t["dx"][:, :], 0.0, ALU.mult, ALU.add)\
                       .then_inc(HDVE.sem, HDVE.one("cs"))
                    dve.wait_ge(HACT.sem, HACT.at(n - 1, "qq"))
                    relative(HDVE, n)
                    ahead(0)
                    dve.wait_ge(HACT.sem, HACT.at(n, "eq"))
                    cap(t["e2"], HDVE, "q1")
                    dve.wait_ge(HACT.sem, HACT.at(n, "sq"))
                    mult(t["r"], Q_, t["s2"], HDVE, "qs")
                    dve.wait_ge(HDVE.sem, HDVE.at(n, "qs"))
                    dve.wait_ge(HACT.sem, HACT.at(n, "pp"))
                    dve.wait_ge(HSP.sem, HSP.at(n - 1, "s"))
                    mult(out["al"], t["r"], t["pp"], HDVE, "qt")
                    dve.wait_ge(HACT.sem, HACT.at(n, "qq"))
                    mult(out["rh"], t["tt"], t["qq"], HDVE, "kt")
                    ahead(1)
                    dve.wait_ge(HACT.sem, HACT.at(n, "eg"))
                    cap(t["kk"], HDVE, "g1")
                    dve.wait_ge(HACT.sem, HACT.at(n, "sg"))
                    dve.scalar_tensor_tensor(out=out["rk"][:, :], in0=G_[:, :], scalar=column(prm, COL["hgw"] + h),
                                             in1=t["ak"][:, :], op0=ALU.mult, op1=ALU.mult).then_inc(HDVE.sem, HDVE.one("gs"))
                    ahead(2)
                    ahead(3)

            dve.memset(carry[:, :], 0.0).then_inc(ULD.sem, ULD.ahead * len(ULD.names))
            dve.memset(resets[:, :], 1.0).then_inc(resets_made, 1)
            dve.wait_ge(resets_made, 1)
            dve.memset(resets[:, ::CHUNK], 0.0).then_inc(resets_made, 1)
            dve.wait_ge(resets_made, 2)
            with dve.Fori(0, HALVES) as hf:
                rw_over(dve, hf - 1)
                hg_over(dve, hf - 1)

                def scale(j, s):
                    n = hf * TILES + j * 2 + s
                    dve.wait_ge(NST.sem, NST.at(n, "rstd"))
                    dve.wait_ge(NPE.sem, NPE.at(n - 1, "turn1"))
                    dve.scalar_tensor_tensor(out=xs[:, :], in0=xt[:, s], scalar=stat[:, 2:3], in1=norm_row[:, :],
                                             op0=ALU.mult, op1=ALU.mult).then_inc(NSC.sem, NSC.one("scaled"))

                def lo(j, s):
                    n = hf * TILES + j * 2 + s
                    for i in range(2):
                        cols = (slice(None), slice(i * BT, (i + 1) * BT), bass.ds((j * 2 + s) * P, P))
                        dve.wait_ge(NHI.sem, NHI.at(n, f"hi{i}"))
                        split_lo(dve, hT[1][cols], TURN[2 * s + i], hT[0][cols]).then_inc(NLO.sem, NLO.one(f"lo{i}"))

                scale(0, 0)
                apart(dve, between["dve"])
                with dve.Fori(0, TILES // 2 - 1) as j:
                    scale(j, 1)
                    lo(j, 0)
                    scale(j + 1, 0)
                    lo(j, 1)
                for slot, name, _ in lora_tiles():
                    weights_lo(dve, WLD, WLA, hf, name, slot)
                scale(TILES // 2 - 1, 1)
                lo(TILES // 2 - 1, 0)
                lo(TILES // 2 - 1, 1)
                for slot, name, _ in rw_tiles(0)[:2]:
                    weights_lo(dve, WRD, WRA, hf * UNITS, name, slot)
                for b in range(NB):
                    n = hf * NB + b
                    dve.wait_ge(LACT.sem, LACT.at(n, "mixa"))
                    dve.wait_ge(LPOOL.sem, LPOOL.at(n, "ca"))
                    unshift(t["k"], DWDA, 3 * UNITS, m["k"], LDVE, "pa")
                    dve.wait_ge(LACT.sem, LACT.at(n, "expa"))
                    one_plus(t["e1"][0:64, :], LDVE, "a1")
                    dve.wait_ge(LDVE.sem, LDVE.at(n, "a1"))
                    dve.reciprocal(t["s1"][0:64, :], t["e1"][0:64, :]).then_inc(LDVE.sem, LDVE.one("rec"))
                    dve.wait_ge(LDVE.sem, LDVE.at(n, "rec"))
                    dve.tensor_scalar(tda[0:64, b * BLOCK:(b + 1) * BLOCK], t["s1"][0:64, :], 2.0, -1.0, ALU.mult, ALU.add)\
                       .then_inc(LDVE.sem, LDVE.one("tanh"))
                    dve.wait_ge(LACT.sem, LACT.at(n, "mixg"))
                    dve.wait_ge(LPOOL.sem, LPOOL.at(n, "cg"))
                    unshift(t["r"], DG, 3 * UNITS + 1, m["r"], LDVE, "pg")
                    dve.wait_ge(LACT.sem, LACT.at(n, "expg"))
                    one_plus(t["e2"][:, :], LDVE, "g1")
                    dve.wait_ge(LDVE.sem, LDVE.at(n, "g1"))
                    dve.wait_ge(LSP.sem, LSP.at(n - 1, "s"))
                    dve.reciprocal(t["s2"][:, :], t["e2"][:, :]).then_inc(LDVE.sem, LDVE.one("sdg"))
                weights_lo(dve, WRD, WRA, hf * UNITS, "v", 2)
                lora_over(dve, hf)
                dve.wait_ge(RPE.sem, RPE.at(hf * UNITS * NB - 1, "a"))
                lora_of(0)
                apart(dve, between["dve"])
                with dve.Fori(0, UNITS - 1) as p:
                    rw_unit(hf, p, (WRD, WRA, hf * UNITS + p + 1, rw_tiles(p + 1)))
                rw_unit(hf, UNITS - 1, (WHD, WHA, hf * UNITS, hg_tiles(0)))
                rw_over(dve, hf)
                apart(dve, between["dve"])
                with dve.Fori(0, UNITS - 1) as h:
                    hg_unit(hf, h, hg_tiles(0))
                hg_unit(hf, UNITS - 1, None)

        @block.gpsimd
        def _(pool):
            begin(pool, "pool")
            make_masks(pool, consts, tri[:, :, :], masks_made)
            pool.wait_ge(ULD.sem, ULD.at(-1, "omka"))
            pool.wait_ge(loaded_c, 48)

            def carried(mm, c, own, n, before, after, full, name):
                pool.wait_ge(own.sem, own.at(n - 1, after))
                apart(pool, between["pool"])
                pool.tensor_copy(mm[:, 0:1], column(carry, c)).then_inc(own.sem, own.one(before))
                pool.wait_ge(full.sem, full.at(n, name))
                pool.wait_ge(own.sem, own.at(n, before))
                apart(pool, between["pool"])
                pool.tensor_copy(column(carry, c), mm[:, BLOCK:BLOCK + 1]).then_inc(own.sem, own.one(after))

            def rw_unit(hf, p):
                u = hf * UNITS + p
                for b in range(NB):
                    n = u * NB + b
                    pool.wait_ge(RDVE.sem, RDVE.at(n - 1, "k"))
                    carried(m["k"], UNITS + p, RPOOL, n, "ck", "sk", RACT, "mk")
                    pool.wait_ge(RDVE.sem, RDVE.at(n - 1, "r"))
                    carried(m["r"], p, RPOOL, n, "cr", "sr", RACT, "mr")
                    pool.wait_ge(RACT.sem, RACT.at(n, "a"))
                    pool.wait_ge(ULD.sem, ULD.at(u, "omka"))
                    apart(pool, between["pool"])
                    pool.tensor_scalar(t["tt"][:, :], t["s2"][:, :], k_a_unit[:, 0:1], k_a_unit[:, 1:2], ALU.mult, ALU.add)\
                        .then_inc(RPOOL.sem, RPOOL.one("t"))
                    pool.wait_ge(RPOOL.sem, RPOOL.at(n, "t"))
                    pool.wait_ge(RDVE.sem, RDVE.at(n - 1, "rk"))
                    pool.tensor_tensor(t["kp"][:, :], t["k"][:, :], t["tt"][:, :], ALU.mult).then_inc(RPOOL.sem, RPOOL.one("kp"))
                    pool.wait_ge(RDVE.sem, RDVE.at(n - 1, "v"))
                    carried(m["v"], 2 * UNITS + p, RPOOL, n, "cv", "sv", RACT, "mv")
                    pool.wait_ge(RDVE.sem, RDVE.at(n, "kk"))
                    pool.wait_ge(RDVE.sem, RDVE.at(n - 1, "beta"))
                    pool.tensor_tensor(t["ak"][:, :], t["kk"][:, :], t["s2"][:, :], ALU.mult).then_inc(RPOOL.sem, RPOOL.one("ak"))

            with pool.Fori(0, HALVES) as hf:
                rw_over(pool, hf - 1)
                for b in range(NB):
                    n = hf * NB + b
                    pool.wait_ge(LDVE.sem, LDVE.at(n - 1, "pa"))
                    carried(m["k"], 3 * UNITS, LPOOL, n, "ca", "sa", LACT, "mixa")
                    pool.wait_ge(LDVE.sem, LDVE.at(n - 1, "pg"))
                    carried(m["r"], 3 * UNITS + 1, LPOOL, n, "cg", "sg", LACT, "mixg")
                lora_over(pool, hf)
                apart(pool, between["pool"])
                with pool.Fori(0, UNITS - 1) as p:
                    rw_unit(hf, p)
                rw_unit(hf, UNITS - 1)


def mix(nc, dims, consts, keep, A, S):
    D, T, W, COL = dims["D"], dims["T"], dims["W"], dims["COL"]
    KT = D // P
    NT = T // P
    NC = keep["NC"]
    H = W // 64
    U = W // P
    prm, ident, bd = consts["prm"], consts["ident"], consts["headsum"]
    lm, eye, mk, himask, headsel = (consts[k] for k in ("lm", "eye", "mk", "himask", "headsel"))
    LEVELS = (2, 4, 8, 16, 32)
    ZEROED = 8

    with ExitStack() as ctx:
        def sb(name, shape, dt=F32):
            return ctx.enter_context(nc.sbuf_tensor("m_" + name, shape, dt))

        def sem(name):
            return ctx.enter_context(nc.semaphore("m_" + name))

        wout = [sb("wout_hi", [P, KT, D], F32R), sb("wout_lo", [P, KT, D], F32R)]
        g2 = sb("g2", [P, W])
        lnw, lnb, n2row = sb("lnw", [P, W]), sb("lnb", [P, W]), sb("norm2_row", [P, D])
        ar = [sb(f"ar{i}", [P, U, 2, P]) for i in range(2)]
        bk_ch = sb("bk_ch", [P, U, 2, P])
        vr_ch = sb("vr_ch", [P, U, 2, P])
        hg_ch = sb("hg_ch", [P, U, 4, P])
        sdg = sb("sdg", [P, P])
        xt = sb("xt", [P, D])
        bk = [sb(f"bk{i}", [P, 2, W]) for i in range(2)]
        uv = [sb(f"uv{i}", [P, 2, U, 2, 64]) for i in range(2)]
        sc = [sb(f"sc{i}", [P, 2, H, P]) for i in range(2)]
        pf = [sb(f"pf{i}", [P, H, 64]) for i in range(2)]
        bv = [sb(f"bv{i}", [P, U, 2, 64]) for i in range(2)]
        at = sb("at", [P, H, 64])
        bl = [sb(f"bl{i}", [P, H, P]) for i in range(2)]
        pb = sb("pb", [P, H, P])
        ts = sb("ts", [P, H, 64])
        pst = sb("pst", [P, H, 64])
        ys = sb("ys", [P, H, 64])
        yb = sb("yb", [P, H, P])
        nst = sb("nst", [P, U, P])
        hst = sb("hst", [P, U, P])
        fb = sb("fb", [P, U, P])
        hsc = sb("hsc", [P, U, P])
        ktok, itok, gtok = sb("ktok", [P, U, P]), sb("itok", [P, U, P]), sb("gtok", [P, U, P])
        ry = sb("ry", [P, U, 2, 64])
        sq = sb("sq", [P, W])
        oh = sb("oh", [P, D])
        hrow = sb("hrow", [P, D])
        spl = [sb("spl_hi", [P, KT, P], F32R), sb("spl_lo", [P, KT, P], F32R)]
        bon = sb("bon", [P, H])
        st = sb("stats", [P, 8 * 6])
        bank = [ctx.enter_context(nc.psum_tensor(f"m_bank{i}", [P, 512], F32)) for i in range(8)]
        b4 = [b[:, :].rearrange("p (a b) -> p a b", a=4) for b in bank]
        b8 = [b[:, :].rearrange("p (a b) -> p a b", a=8) for b in bank]
        bp = [b[:, :].rearrange("p (a b c) -> p a b c", a=4, b=2) for b in bank]
        ystat, vstat, rstd = st[:, 0:8], st[:, 8:16], st[:, 16:24]
        ostat, orstd, xstat, xrstd = st[:, 24:28], st[:, 28:32], st[:, 32:33], st[:, 33:34]
        xhalf = st[:, 34:35]

        ldc, ldA, ldH, ldG, ldX = (sem("ld" + k) for k in "cAHGX")
        between = {k: sem("between_" + k) for k in ("sp", "pe", "dve")}
        ldW = [sem(f"ldW{k}") for k in range(KT)]
        stX, stH = sem("st_x"), sem("st_h")
        flat = [sc[1][:, c].rearrange("p h t -> p (h t)") for c in range(2)]
        flat += [hg_ch[:, 2 * i:2 * i + 2].rearrange("p u k t -> p (u k t)") for i in range(2)]
        stage = flat + [oh[:, :], hrow[:, :], xt[:, :], bk[1][:, :, :].rearrange("p c w -> p (c w)")]
        F3 = keep["L"][:, :].rearrange("p (u c) -> p u c", c=NC)
        setup = {k: sem("setup_" + k) for k in ("act", "dve")}
        APE = Stages(sem("a_pe"), "v bk0 bk1 bonus sc0 sc1 " + " ".join(f"y{l} z{l}" for l in LEVELS[:-1]) + " y32_0 y32 z32", ahead=2)
        AACT = Stages(sem("a_act"), "v0 v1 bk0 at00 at01 at10 at11 Y2 Y4 Y8 Y16 Y32a0 Y32b0 Y32a1 Y32b1", ahead=2)
        ADVE = Stages(sem("a_dve"), "bk1 bon bv sc00 sc01 sc10 sc11 Pm Pi t P1a P1b T2 P2a P2b T4 P4a P4b T8 P8a P8b T16 pst pfin", ahead=2)
        APOOL = Stages(sem("a_pool"), "bv " + " ".join(f"b{l}a b{l}b" for l in LEVELS), ahead=2)
        BPE = Stages(sem("b_pe"), "r0 q0 u0 hk hs n0 y0 hi r1 q1 u1 n1 y1 hg ho hu0 o0 hu1 gate o1", ahead=2)
        BACT = Stages(sem("b_act"), "R0 U0 hk hi R1 U1 hg ysb sq rl re sqo ol oe", ahead=2)
        BDVE = Stages(sem("b_dve"), "hs a0 m0 a1 m1 sm ymu ha0 vs yn ha1 gy os on", ahead=2)
        BPOOL = Stages(sem("b_pool"), "F0 F1 hm0 yw yb hm1 og", ahead=2)
        CPE = Stages(sem("c_pe"), "ot1 ot0 op0 op1 ht0 ht1", ahead=3)
        CACT = Stages(sem("c_act"), "oh1 oh0 sx0 xb sx xl xe h0 h1", ahead=3)
        CDVE = Stages(sem("c_dve"), "ol1 ol0 x0 x1 h", ahead=3)
        CSP = Stages(sem("c_sp"), "s", ahead=3)
        credit = {"pe": [APE, BPE, CPE], "act": [AACT, BACT, CACT], "dve": [ADVE, BDVE, CDVE], "pool": [APOOL, BPOOL],
                  "sp": [CSP]}

        def begin(eng, who):
            for s in credit[who]:
                eng.sem_inc(s.sem, s.ahead * len(s.names))

        def tiles(eng, tile, after_first=None):
            tile(-1, 1, True, False, False)
            if after_first:
                after_first()
            tile(0, 0, True, True, False)
            with eng.Fori(0, (NT - 2) // 2) as j:
                tile(2 * j + 1, 1, True, True, True)
                tile(2 * j + 2, 0, True, True, True)
            tile(NT - 1, 1, False, True, True)
            tile(NT, 0, False, False, True)

        block = ctx.enter_context(nc.Block())

        @block.sync
        def _(sp):
            begin(sp, "sp")

            def load_ahead(n, s):
                for i, (dst, kinds) in enumerate(((ar[s], 0), (bk_ch, 2), (vr_ch, 4))):
                    src = S["rw"][bass.ds(n, 1)].rearrange("o p (u k) t -> p (o u) k t", k=6)[:, :, kinds:kinds + 2]
                    sp.dma_start(dst[:, :, :, :], src).then_inc(ldA, 16)

            def load_hg(n):
                sp.dma_start(hg_ch[:, :, :, :], S["hg"][bass.ds(n, 1)].rearrange("o p (u k) t -> p (o u) k t", k=4))\
                  .then_inc(ldH, 16)

            def load_gate(n):
                sp.dma_start(sdg[:, :], S["sdg"][bass.ds(n, 1)].rearrange("o p t -> p (o t)")).then_inc(ldG, 16)

            def load_x(n):
                sp.dma_start(xt[:, :], A["x"][bass.ds(n * P, P), :]).then_inc(ldX, 16)

            load_ahead(0, 0)
            for dst, src in ((g2[:, :], A["rw_g2"]), (lnw[:, :], A["rw_ln_w"].partition_broadcast(P)),
                             (lnb[:, :], A["rw_ln_b"].partition_broadcast(P)), (n2row[:, :], A["norm2_w"].partition_broadcast(P))):
                sp.dma_start(dst, src).then_inc(ldc, 16)
            for k in range(KT):
                sp.dma_start(stage[k], A["w_out"][k * P:(k + 1) * P, :]).then_inc(ldW[k], 16)

            def tile(n, par, ahead, now, behind):
                if isinstance(n, int) and n == 0:
                    sp.wait_ge(setup["dve"], ZEROED + KT)
                    load_hg(0)
                    load_gate(0)
                    load_x(0)
                if ahead and (not isinstance(n, int) or n + 2 < NT):
                    sp.wait_ge(APE.sem, APE.at(n + 1, "sc1"))
                    apart(sp, between["sp"])
                    sp.wait_ge(BPE.sem, BPE.at(n, "q1"))
                    apart(sp, between["sp"])
                    load_ahead(n + 2, par)
                if behind:
                    sp.wait_ge(CDVE.sem, CDVE.at(n - 1, "x1"))
                    apart(sp, between["sp"])
                    sp.dma_start(S["x2"][bass.ds((n - 1) * P, P), :], xt[:, :]).then_inc(stX, 16)
                if now and (not isinstance(n, int) or n + 1 < NT):
                    sp.wait_ge(BPE.sem, BPE.at(n, "gate"))
                    apart(sp, between["sp"])
                    load_gate(n + 1)
                    sp.wait_ge(BPE.sem, BPE.at(n, "o1"))
                    apart(sp, between["sp"])
                    load_hg(n + 1)
                if behind:
                    if not isinstance(n, int) or n < NT:
                        sp.wait_ge(stX, 16 * n)
                        apart(sp, between["sp"])
                        sp.wait_ge(CDVE.sem, CDVE.at(n - 1, "h"))
                        apart(sp, between["sp"])
                        sp.wait_ge(CACT.sem, CACT.at(n - 1, "sx"))
                        apart(sp, between["sp"])
                        load_x(n)
                    sp.wait_ge(CACT.sem, CACT.at(n - 1, "h1"))
                    apart(sp, between["sp"])
                    sp.dma_start(S["h2"][:, :, bass.ds((n - 1) * P, P)].rearrange("k p t -> p k t"),
                                 hrow[:, :].rearrange("p (k t) -> p k t", k=KT)).then_inc(stH, 16)
                    sp.wait_ge(stH, 16 * n)
                    apart(sp, between["sp"])
                    sp.sem_inc(CSP.sem, CSP.one("s"))

            tile(-1, 1, True, False, False)
            tile(0, 0, True, True, False)
            with sp.Fori(0, (NT - 4) // 2) as j:
                tile(2 * j + 1, 1, True, True, True)
                tile(2 * j + 2, 0, True, True, True)
            tile(NT - 3, 1, True, True, True)
            tile(NT - 2, 0, True, True, True)
            tile(NT - 1, 1, False, True, True)
            tile(NT, 0, False, False, True)
            sp.wait_ge(stX, 16 * NT)

        @block.tensor
        def _(pe):
            begin(pe, "pe")

            def mm(out, lhs, rhs, start=True, stop=True):
                return pe.matmul(out, lhs, rhs, start=start, stop=stop, skip_group_check=True)

            def A_turn(n, s):
                pe.wait_ge(ldA, 48 * (n + 1))
                pe.wait_ge(ADVE.sem, ADVE.at(n - 1, "pfin"))
                for u in range(U):
                    last = pe.transpose(b4[2][:, u], vr_ch[:, u, 0], ident[:, :])
                last.then_inc(APE.sem, APE.one("v"))
                for c in range(2):
                    pe.wait_ge(CACT.sem, CACT.at(n - 3, f"h{c}"))
                    for u in range(U):
                        last = pe.transpose(b4[c][:, u], bk_ch[:, u, c], ident[:, :])
                    last.then_inc(APE.sem, APE.one(f"bk{c}"))

            def A_bonus(n):
                pe.wait_ge(AACT.sem, AACT.at(n, "bk0"))
                for u in range(U):
                    last = mm(bank[0][:, 2 * u:2 * u + 2], vr_ch[:, u, 1], headsel[:, :])
                last.then_inc(APE.sem, APE.one("bonus"))

            def A_scores(n, s, c):
                if c == 0:
                    pe.wait_ge(ADVE.sem, ADVE.at(n, "bon"))
                    pe.wait_ge(ADVE.sem, ADVE.at(n, "bk1"))
                else:
                    pe.wait_ge(ADVE.sem, ADVE.at(n, "sc00"))
                    pe.wait_ge(ADVE.sem, ADVE.at(n, "sc01"))
                    pe.wait_ge(AACT.sem, AACT.at(n, "at00"))
                    pe.wait_ge(AACT.sem, AACT.at(n, "at01"))
                t = slice(c * 64, c * 64 + 64)
                for u in range(U):
                    for par in range(2):
                        rows = slice(64 * par, 64 * par + 64)
                        last = mm(b4[par][:, u], bk_ch[rows, u, c], ar[s][rows, u, :, t])
                last.then_inc(APE.sem, APE.one(f"sc{c}"))

            def A_y(n, l):
                i = LEVELS.index(l)
                pe.wait_ge(APOOL.sem, APOOL.at(n, f"b{l}b"))
                pe.wait_ge(ADVE.sem, ADVE.at(n, "t" if i == 0 else f"T{LEVELS[i - 1]}"))
                if i == 0:
                    pe.wait_ge(AACT.sem, AACT.at(n, "v1"))
                if l == 32:
                    pe.wait_ge(BACT.sem, BACT.at(n - 1, "ysb"))
                for h in range(H):
                    b = 5 if l == 32 and h >= H // 2 else 2
                    last = mm(b8[b][:, h], bl[(i + 1) % 2][:, h], ts[:, h])
                    if l == 32 and h == H // 2 - 1:
                        last.then_inc(APE.sem, APE.one("y32_0"))
                last.then_inc(APE.sem, APE.one(f"y{l}"))

            def A_z(n, l):
                i = LEVELS.index(l)
                if l == 32:
                    pe.wait_ge(ADVE.sem, ADVE.at(n, "pst"))
                    for half in range(2):
                        pe.wait_ge(AACT.sem, AACT.at(n, f"Y32b{half}"))
                        for h in range(half * H // 2, (half + 1) * H // 2):
                            last = mm(b8[2][:, h], yb[:, h], pst[:, h])
                else:
                    pe.wait_ge(AACT.sem, AACT.at(n, f"Y{l}"))
                    pe.wait_ge(ADVE.sem, ADVE.at(n, f"P{l // 2}b"))
                    for h in range(H):
                        last = mm(b8[2][:, h], pb[:, h], ys[:, h])
                last.then_inc(APE.sem, APE.one(f"z{l}"))

            def B_r(n, s, c):
                t = slice(c * 64, c * 64 + 64)
                if c == 0:
                    pe.wait_ge(AACT.sem, AACT.at(n, "v1"))
                    pe.wait_ge(ADVE.sem, ADVE.at(n, "sc11"))
                    pe.wait_ge(BDVE.sem, BDVE.at(n - 1, "gy"))
                else:
                    pe.wait_ge(BACT.sem, BACT.at(n, "U0"))
                apart(pe, between["pe"])
                for h in range(H):
                    mm(bp[3][t, h // 2, h % 2], sc[s][64:128, c, (h % 2) * U + h // 2, 0:64], uv[s][64:128, c, h // 2, h % 2],
                       start=(h == 0), stop=False)
                pe.wait_ge(BDVE.sem, BDVE.at(n - 1 + c, f"m{1 - c}"))
                for u in range(U):
                    last = mm(b4[3][t, u], ar[s][:, u, 0, t], nst[:, u], start=False)
                last.then_inc(BPE.sem, BPE.one(f"r{c}"))
                pe.wait_ge(BACT.sem, BACT.at(n - 1, "ysb"))
                for u in range(U):
                    last = mm(b4[5][t, u], ar[s][:, u, 1, t], nst[:, u], start=(u == 0), stop=False)
                last.then_inc(BPE.sem, BPE.one(f"q{c}"))

            def B_u(n, s, c):
                pe.wait_ge(BACT.sem, BACT.at(n, f"R{c}"))
                pe.wait_ge(ADVE.sem, ADVE.at(n, "pfin"))
                apart(pe, between["pe"])
                for h in range(H):
                    last = mm(bp[3][0:64, h // 2, h % 2], pf[s][64 * c:64 * c + 64, (h % 2) * U + h // 2],
                              ry[64 * c:64 * c + 64, h // 2, h % 2])
                last.then_inc(BPE.sem, BPE.one(f"u{c}"))

            def B_n(n, s, c):
                t = slice(c * 64, c * 64 + 64)
                pe.wait_ge(BACT.sem, BACT.at(n, f"U{c}"))
                pe.wait_ge(ADVE.sem, ADVE.at(n, "bk1"))
                pe.wait_ge(AACT.sem, AACT.at(n, "bk0"))
                if c == 0:
                    pe.wait_ge(CDVE.sem, CDVE.at(n - 1, "ol1"))
                else:
                    pe.wait_ge(BDVE.sem, BDVE.at(n, "a0"))
                for u in range(U):
                    last = mm(b4[4][:, u], bk[s][:, c, u * P:(u + 1) * P], uv[s][:, c, u])
                last.then_inc(BPE.sem, BPE.one(f"n{c}"))

            def B_y(n, s, c):
                t = slice(c * 64, c * 64 + 64)
                for h in range(H):
                    last = mm(bp[5][t, h // 2, h % 2], sc[s][:, c, (h % 2) * U + h // 2, 64:128], uv[s][:, c, h // 2, h % 2],
                              start=False)
                last.then_inc(BPE.sem, BPE.one(f"y{c}"))

            def H_scores(n):
                pe.wait_ge(CDVE.sem, CDVE.at(n - 1, "ol0"))
                for u in range(U):
                    last = mm(b4[6][:, u], hg_ch[:, u, 1], hg_ch[:, u, 0])
                last.then_inc(BPE.sem, BPE.one("hs"))

            def H_turn(n, kind, b, name):
                for u in range(U):
                    last = pe.transpose(b4[b][:, u], hg_ch[:, u, kind], ident[:, :])
                last.then_inc(BPE.sem, BPE.one(name))

            def H_o(n):
                pe.wait_ge(BDVE.sem, BDVE.at(n, "hs"))
                pe.wait_ge(BACT.sem, BACT.at(n, "hi"))
                pe.wait_ge(BACT.sem, BACT.at(n, "hg"))
                for u in range(U):
                    last = mm(b4[7][:, u], hsc[:, u], itok[:, u], start=(u == 0), stop=False)
                last.then_inc(BPE.sem, BPE.one("ho"))

            def H_u(n, c):
                rows = slice(64 * c, 64 * c + 64)
                if c == 0:
                    pe.wait_ge(BACT.sem, BACT.at(n, "hk"))
                else:
                    pe.wait_ge(BDVE.sem, BDVE.at(n, "ha0"))
                for u in range(U):
                    last = mm(b4[6][:, u], ktok[rows, u], itok[rows, u])
                last.then_inc(BPE.sem, BPE.one(f"hu{c}"))

            def H_q(n, c):
                pe.wait_ge(BPOOL.sem, BPOOL.at(n - 1 + c, f"hm{1 - c}"))
                for u in range(U):
                    last = mm(b4[7][64 * c:64 * c + 64, u], hg_ch[:, u, 0, 64 * c:64 * c + 64], hst[:, u], start=False)
                last.then_inc(BPE.sem, BPE.one(f"o{c}"))

            def C_turn(n, src, first, b, name):
                for a in range(4):
                    last = pe.transpose(b4[b][:, a], src[:, first + a * P:first + (a + 1) * P], ident[:, :])
                last.then_inc(CPE.sem, CPE.one(name))

            def C_out(n, i, ks):
                for k in ks:
                    last = three_passes(pe, bank[i][:, :], (spl[0][:, k], spl[1][:, k]),
                                        (wout[0][:, k, i * 512:(i + 1) * 512], wout[1][:, k, i * 512:(i + 1) * 512]),
                                        k == 0, k == KT - 1)
                if k == KT - 1:
                    last.then_inc(CPE.sem, CPE.one(f"op{i}"))

            def tile(n, par, ahead, now, behind):
                s, t = par, 1 - par
                if ahead:
                    A_turn(n + 1, t)
                if now:
                    B_r(n, s, 0)
                if ahead:
                    A_bonus(n + 1)
                if behind:
                    pe.wait_ge(BDVE.sem, BDVE.at(n - 1, "gy"))
                    C_turn(n - 1, oh, W, 4, "ot1")
                    pe.wait_ge(BPOOL.sem, BPOOL.at(n - 1, "og"))
                    pe.wait_ge(BDVE.sem, BDVE.at(n - 1, "ha1"))
                    C_turn(n - 1, oh, 0, 6, "ot0")
                if ahead:
                    A_scores(n + 1, t, 0)
                if now:
                    B_u(n, s, 0)
                    pe.wait_ge(ldH, 16 * (n + 1))
                    pe.wait_ge(BDVE.sem, BDVE.at(n - 1, "on"))
                    H_turn(n, 1, 7, "hk")
                if ahead:
                    A_scores(n + 1, t, 1)
                if now:
                    H_scores(n)
                    B_n(n, s, 0)
                    B_y(n, s, 0)
                    pe.wait_ge(BDVE.sem, BDVE.at(n, "hs"))
                    H_turn(n, 2, 6, "hi")
                    B_r(n, s, 1)
                if behind:
                    if ahead:
                        pe.wait_ge(AACT.sem, AACT.at(n + 1, "at10"))
                        pe.wait_ge(ADVE.sem, ADVE.at(n + 1, "sc10"))
                    pe.wait_ge(CDVE.sem, CDVE.at(n - 1, "ol0"))
                    C_out(n - 1, 0, range(KT // 2))
                if now:
                    B_u(n, s, 1)
                if ahead:
                    A_y(n + 1, 2)
                if behind:
                    C_out(n - 1, 0, range(KT // 2, KT))
                if now:
                    B_n(n, s, 1)
                if ahead:
                    A_z(n + 1, 2)
                if now:
                    B_y(n, s, 1)
                    pe.wait_ge(BACT.sem, BACT.at(n, "hk"))
                    H_turn(n, 3, 7, "hg")
                if ahead:
                    A_y(n + 1, 4)
                if now:
                    H_o(n)
                    H_u(n, 0)
                if ahead:
                    A_z(n + 1, 4)
                if behind:
                    if ahead:
                        pe.wait_ge(AACT.sem, AACT.at(n + 1, "at11"))
                        pe.wait_ge(ADVE.sem, ADVE.at(n + 1, "sc11"))
                    C_out(n - 1, 1, range(KT // 2))
                if ahead:
                    A_y(n + 1, 8)
                if now:
                    H_q(n, 0)
                if ahead:
                    A_z(n + 1, 8)
                if behind:
                    C_out(n - 1, 1, range(KT // 2, KT - 2))
                if ahead:
                    A_y(n + 1, 16)
                if now:
                    H_u(n, 1)
                    pe.wait_ge(ldG, 16 * (n + 1))
                    pe.wait_ge(BACT.sem, BACT.at(n, "U1"))
                    mm(bank[3][:, :], sdg[:, :], g2[:, :]).then_inc(BPE.sem, BPE.one("gate"))
                if ahead:
                    A_z(n + 1, 16)
                if behind:
                    C_out(n - 1, 1, range(KT - 2, KT))
                if ahead:
                    A_y(n + 1, 32)
                if now:
                    H_q(n, 1)
                if ahead:
                    A_z(n + 1, 32)
                if behind:
                    pe.wait_ge(CDVE.sem, CDVE.at(n - 1, "h"))
                    C_turn(n - 1, hrow, 0, 0, "ht0")
                    C_turn(n - 1, hrow, 512, 1, "ht1")

            def after_first():
                pe.wait_ge(setup["dve"], KT + ZEROED)
                pe.wait_ge(ldc, 64)

            pe.wait_ge(setup["dve"], ZEROED)
            tiles(pe, tile, after_first)


        @block.scalar
        def _(act):
            begin(act, "act")
            act.preload_act_table_set(ONE_SET)
            act.wait_ge(setup["dve"], ZEROED)

            def split_w(n, ks):
                if isinstance(n, int) and n == -1:
                    for k in ks:
                        act.wait_ge(ldW[k], 16)
                        split_hi(act, wout[0][:, k], stage[k]).then_inc(setup["act"], 1)

            def copy(dst, src, s, name, scale=1.0):
                act.activation(dst, src, ACT.Copy, scale=scale).then_inc(s.sem, s.one(name))

            def rsqrt(dst, src, width, eps, names, n, s=BACT):
                act.activation(dst, src, ACT.Ln, scale=1.0 / width, bias=eps).then_inc(s.sem, s.one(names[0]))
                act.wait_ge(s.sem, s.at(n, names[0]))
                act.activation(dst, dst, ACT.Exp, scale=-0.5).then_inc(s.sem, s.one(names[1]))

            def Y(n, l):
                act.wait_ge(APE.sem, APE.at(n, f"y{l}"))
                copy(ys[:, :, :], b8[2], AACT, f"Y{l}")

            def tile(n, par, ahead, now, behind):
                s, t = par, 1 - par
                m = n + 1
                if ahead:
                    act.wait_ge(APE.sem, APE.at(m, "v"))
                    act.wait_ge(BPE.sem, BPE.at(m - 2, "y1"))
                    for c in range(2):
                        copy(uv[t][64:128, c], bp[2][64 * c:64 * c + 64], AACT, f"v{c}")
                    act.wait_ge(APE.sem, APE.at(m, "bk0"))
                    copy(bk[t][:, 0], bank[0][:, :], AACT, "bk0")
                if now:
                    act.wait_ge(BPE.sem, BPE.at(n, "r0"))
                    act.wait_ge(BDVE.sem, BDVE.at(n - 1, "gy"))
                    copy(ry[0:64], bp[3][0:64], BACT, "R0", -1.0)
                if ahead:
                    act.wait_ge(APOOL.sem, APOOL.at(m - 1, "b32b"))
                    for par_ in range(2):
                        act.wait_ge(ADVE.sem, ADVE.at(m, f"sc0{par_}"))
                        copy(at[0:64, par_ * U:(par_ + 1) * U], b4[par_][0:64, :, 0:64], AACT, f"at0{par_}")
                if behind:
                    act.wait_ge(CPE.sem, CPE.at(n - 1, "ot1"))
                    split_hi(act, spl[0][:, 4:8], b4[4]).then_inc(CACT.sem, CACT.one("oh1"))
                    act.wait_ge(CPE.sem, CPE.at(n - 1, "ot0"))
                    split_hi(act, spl[0][:, 0:4], b4[6]).then_inc(CACT.sem, CACT.one("oh0"))
                if now:
                    act.wait_ge(BPE.sem, BPE.at(n, "u0"))
                    copy(uv[s][0:64, 0], bp[3][0:64], BACT, "U0")
                if ahead:
                    for par_ in range(2):
                        act.wait_ge(ADVE.sem, ADVE.at(m, f"sc1{par_}"))
                        copy(at[64:128, par_ * U:(par_ + 1) * U], b4[par_][0:64, :, 0:64], AACT, f"at1{par_}")
                if now:
                    act.wait_ge(BPE.sem, BPE.at(n, "hk"))
                    act.wait_ge(BPE.sem, BPE.at(n - 1, "hu1"))
                    copy(ktok[:, :, :], b4[7], BACT, "hk")
                    act.wait_ge(BPE.sem, BPE.at(n, "hi"))
                    copy(itok[:, :, :], b4[6], BACT, "hi")
                    act.wait_ge(BPE.sem, BPE.at(n, "r1"))
                    copy(ry[64:128], bp[3][64:128], BACT, "R1", -1.0)
                    act.wait_ge(BPE.sem, BPE.at(n, "u1"))
                    copy(uv[s][0:64, 1], bp[3][0:64], BACT, "U1")
                if ahead:
                    Y(m, 2)
                    split_w(n, range(0, 2))
                if now:
                    act.wait_ge(BPE.sem, BPE.at(n, "hg"))
                    act.wait_ge(BPOOL.sem, BPOOL.at(n - 1, "og"))
                    copy(gtok[:, :, :], b4[7], BACT, "hg")
                    act.wait_ge(BPE.sem, BPE.at(n, "y1"))
                    copy(ry[:, :, :, :], bp[5], BACT, "ysb")
                if behind:
                    act.wait_ge(CDVE.sem, CDVE.at(n - 1, "x0"))
                    act.wait_ge(CSP.sem, CSP.at(n - 2, "s"))
                    act.activation(hrow[:, 0:W], xt[:, 0:W], ACT.Square, accum_out=xhalf).then_inc(CACT.sem, CACT.one("sx0"))
                    act.wait_ge(CACT.sem, CACT.at(n - 1, "sx0"))
                    act.activation(xhalf, xhalf, ACT.Identity, scale=1.0 / D, bias=column(prm, COL["eps"]))\
                       .then_inc(CACT.sem, CACT.one("xb"))
                if ahead:
                    Y(m, 4)
                    split_w(n, range(2, 4))
                if now:
                    act.wait_ge(BDVE.sem, BDVE.at(n, "ymu"))
                    act.wait_ge(BDVE.sem, BDVE.at(n - 1, "os"))
                    act.activation(sq[:, :].rearrange("p (a b c) -> p a b c", a=4, b=2), ry[:, :, :, :], ACT.Square)\
                       .then_inc(BACT.sem, BACT.one("sq"))
                if ahead:
                    Y(m, 8)
                    split_w(n, range(4, 6))
                if now:
                    act.wait_ge(BDVE.sem, BDVE.at(n, "vs"))
                    rsqrt(rstd, vstat, 64, column(prm, COL["gneps"]), ("rl", "re"), n)
                if ahead:
                    Y(m, 16)
                    split_w(n, range(6, KT))
                if behind:
                    act.wait_ge(CDVE.sem, CDVE.at(n - 1, "x1"))
                    act.activation(hrow[:, W:D], xt[:, W:D], ACT.Square, accum_out=xstat).then_inc(CACT.sem, CACT.one("sx"))
                if ahead:
                    for half, hs, done in ((0, slice(0, H // 2), "y32_0"), (1, slice(H // 2, H), "y32")):
                        act.wait_ge(APE.sem, APE.at(m, done))
                        for c, k in ((0, "a"), (1, "b")):
                            r = slice(64 * c, 64 * c + 64)
                            copy(yb[r, hs, r], b8[(2, 5)[half]][r, hs], AACT, f"Y32{k}{half}")
                if behind:
                    act.wait_ge(CACT.sem, CACT.at(n - 1, "sx"))
                    act.wait_ge(CDVE.sem, CDVE.at(n - 2, "h"))
                    rsqrt(xrstd, xstat, D, xhalf, ("xl", "xe"), n - 1, CACT)
                if now:
                    act.wait_ge(BPE.sem, BPE.at(n, "o1"))
                    act.activation(sq[:, :], bank[7][:, :], ACT.Square).then_inc(BACT.sem, BACT.one("sqo"))
                    act.wait_ge(BDVE.sem, BDVE.at(n, "os"))
                    act.wait_ge(BDVE.sem, BDVE.at(n - 1, "on"))
                    rsqrt(orstd, ostat, P, column(prm, COL["eps"]), ("ol", "oe"), n)
                if behind:
                    act.wait_ge(CPE.sem, CPE.at(n - 1, "ht1"))
                    copy(hrow[:, 0:512], bank[0][:, :], CACT, "h0")
                    copy(hrow[:, 512:1024], bank[1][:, :], CACT, "h1")

            tiles(act, tile)

        @block.vector
        def _(dve):
            begin(dve, "dve")
            for z in (nst, hst, hsc, pb, bl[0], bl[1], yb):
                dve.memset(z[:, :, :], 0.0).then_inc(setup["dve"], 1)
            E3 = keep["E"][:, :].rearrange("p (u c) -> p u c", c=NC)
            dve.tensor_tensor(F3[:, :, 0:NC - 1], F3[:, :, 0:NC - 1], E3[:, :, 1:NC], ALU.mult).then_inc(setup["dve"], 1)
            dve.wait_ge(setup["dve"], ZEROED)

            def split_w(n, ks):
                if isinstance(n, int) and n == -1:
                    for k in ks:
                        dve.wait_ge(setup["act"], k + 1)
                        split_lo(dve, wout[1][:, k], stage[k], wout[0][:, k]).then_inc(setup["dve"], 1)

            def after_first():
                dve.wait_ge(setup["dve"], KT + ZEROED)
                dve.wait_ge(ldc, 64)

            def tt(dst, a, b, op, s, name):
                dve.tensor_tensor(dst, a, b, op).then_inc(s.sem, s.one(name))

            def scores(n, t, c):
                dve.wait_ge(APE.sem, APE.at(n, f"sc{c}"))
                dve.wait_ge(BPE.sem, BPE.at(n - 2, "y1"))
                for par in range(2):
                    tt(sc[t][:, c, par * U:(par + 1) * U], b4[par],
                       mk[:, :, :].rearrange("p a b -> p (a b)").unsqueeze(1).broadcast_to([P, U, P]), ALU.mult,
                       ADVE, f"sc{c}{par}")

            def T_(n, l):
                dve.wait_ge(APE.sem, APE.at(n, f"z{l}"))
                tt(ts[:, :, :], ts[:, :, :], b8[2], ALU.subtract, ADVE, f"T{l}")
                dve.wait_ge(ADVE.sem, ADVE.at(n, f"T{l}"))

            def P_(n, l):
                for c, k in ((0, "a"), (1, "b")):
                    r = slice(64 * c, 64 * c + 64)
                    dve.transpose(pb[r, :, r], ts[r]).then_inc(ADVE.sem, ADVE.one(f"P{l}{k}"))

            def state(n, c):
                dve.wait_ge(BPE.sem, BPE.at(n, f"n{c}"))
                dve.wait_ge(BPE.sem, BPE.at(n, f"q{c}"))
                tt(nst[:, :, :], nst[:, :, :], b4[4], ALU.add, BDVE, f"a{c}")
                dve.wait_ge(BDVE.sem, BDVE.at(n, f"a{c}"))
                dve.wait_ge(BPOOL.sem, BPOOL.at(n, f"F{c}"))
                tt(nst[:, :, :], nst[:, :, :], fb[:, :, :], ALU.mult, BDVE, f"m{c}")

            def add_h(n, c):
                dve.wait_ge(BPE.sem, BPE.at(n, f"o{c}"))
                dve.wait_ge(BPE.sem, BPE.at(n, f"hu{c}"))
                dve.wait_ge(BPOOL.sem, BPOOL.at(n - 1 + c, f"hm{1 - c}"))
                tt(hst[:, :, :], hst[:, :, :], b4[6], ALU.add, BDVE, f"ha{c}")

            def total(dst, src, name):
                dve.tensor_reduce(dst, src, AX.X, ALU.add).then_inc(BDVE.sem, BDVE.one(name))

            ry8 = ry[:, :, :, :].rearrange("p a b c -> p (a b) c")
            sq8 = sq[:, :].rearrange("p (a b) -> p a b", a=8)
            sq4 = sq[:, :].rearrange("p (a b) -> p a b", a=4)

            def C_lo(n, i, b, name):
                dve.wait_ge(CACT.sem, CACT.at(n, name[0] + "h" + name[2]))
                split_lo(dve, spl[1][:, 4 * i:4 * i + 4], b4[b], spl[0][:, 4 * i:4 * i + 4]).then_inc(CDVE.sem, CDVE.one(name))

            def add_x(n, i):
                dve.wait_ge(ldX, 16 * (n + 1))
                dve.wait_ge(CPE.sem, CPE.at(n, f"op{i}"))
                tt(xt[:, i * 512:(i + 1) * 512], xt[:, i * 512:(i + 1) * 512], bank[i][:, :], ALU.add, CDVE, f"x{i}")

            def tile(n, par, ahead, now, behind):
                s, t = par, 1 - par
                m = n + 1
                if ahead:
                    dve.wait_ge(APE.sem, APE.at(m, "bk1"))
                    dve.wait_ge(BPE.sem, BPE.at(m - 2, "n1"))
                    dve.tensor_copy(bk[t][:, 1], bank[1][:, :]).then_inc(ADVE.sem, ADVE.one("bk1"))
                    dve.wait_ge(APE.sem, APE.at(m, "bonus"))
                    dve.tensor_copy(bon[:, :], bank[0][:, 0:H]).then_inc(ADVE.sem, ADVE.one("bon"))
                    dve.wait_ge(ADVE.sem, ADVE.at(m, "bon"))
                    dve.wait_ge(AACT.sem, AACT.at(m, "v1"))
                    dve.wait_ge(BPOOL.sem, BPOOL.at(m - 2, "yb"))
                    tt(bv[t][:, :, :, :].rearrange("p a b c -> p (a b) c"), b8[2],
                       bon[:, :].unsqueeze(2).broadcast_to([P, H, 64]), ALU.mult, ADVE, "bv")
                    scores(m, t, 0)
                if behind:
                    C_lo(n - 1, 1, 4, "ol1")
                    C_lo(n - 1, 0, 6, "ol0")
                if ahead:
                    scores(m, t, 1)
                if now:
                    dve.wait_ge(BPE.sem, BPE.at(n, "hs"))
                    dve.wait_ge(BPE.sem, BPE.at(n - 1, "ho"))
                    apart(dve, between["dve"])
                    dve.copy_predicated(hsc[:, :, :], himask[:, :].unsqueeze(1).broadcast_to([P, U, P]), b4[6])\
                       .then_inc(BDVE.sem, BDVE.one("hs"))
                if ahead:
                    dve.wait_ge(AACT.sem, AACT.at(m, "at11"))
                    dve.wait_ge(ADVE.sem, ADVE.at(m - 1, "pfin"))
                    tt(pst[:, :, :], at[:, :, :], lm[:, 0].unsqueeze(1).broadcast_to([P, H, 64]), ALU.mult, ADVE, "Pm")
                    dve.wait_ge(ADVE.sem, ADVE.at(m, "Pm"))
                    tt(pst[:, :, :], pst[:, :, :], eye[:, :].unsqueeze(1).broadcast_to([P, H, 64]), ALU.add, ADVE, "Pi")
                    dve.wait_ge(ADVE.sem, ADVE.at(m, "Pi"))
                    dve.wait_ge(APE.sem, APE.at(m - 1, "y32"))
                    dve.transpose(ts[:, :, :], pst[:, :, :]).then_inc(ADVE.sem, ADVE.one("t"))
                if now:
                    state(n, 0)
                if ahead:
                    dve.wait_ge(APE.sem, APE.at(m - 1, "z16"))
                    for c, k in ((0, "a"), (1, "b")):
                        r = slice(64 * c, 64 * c + 64)
                        dve.tensor_copy(pb[r, :, r], pst[r]).then_inc(ADVE.sem, ADVE.one("P1" + k))
                if behind:
                    add_x(n - 1, 0)
                if now:
                    state(n, 1)
                if ahead:
                    T_(m, 2)
                    P_(m, 2)
                    split_w(n, range(0, 2))
                if now:
                    dve.wait_ge(BACT.sem, BACT.at(n, "ysb"))
                    total(ystat, ry8, "sm")
                    dve.wait_ge(BDVE.sem, BDVE.at(n, "sm"))
                    dve.scalar_tensor_tensor(out=ry8, in0=ystat.unsqueeze(2).broadcast_to([P, H, 64]), scalar=-1.0 / 64,
                                             in1=ry8, op0=ALU.mult, op1=ALU.add).then_inc(BDVE.sem, BDVE.one("ymu"))
                if ahead:
                    T_(m, 4)
                    P_(m, 4)
                    split_w(n, range(2, 4))
                if now:
                    add_h(n, 0)
                    dve.wait_ge(BACT.sem, BACT.at(n, "sq"))
                    total(vstat, sq8, "vs")
                if ahead:
                    T_(m, 8)
                    P_(m, 8)
                    split_w(n, range(4, 6))
                if now:
                    dve.wait_ge(BACT.sem, BACT.at(n, "re"))
                    tt(ry8, ry8, rstd.unsqueeze(2).broadcast_to([P, H, 64]), ALU.mult, BDVE, "yn")
                if ahead:
                    T_(m, 16)
                    dve.transpose(pst[:, :, :], ts[:, :, :]).then_inc(ADVE.sem, ADVE.one("pst"))
                    split_w(n, range(6, KT))
                if behind:
                    add_x(n - 1, 1)
                if now:
                    add_h(n, 1)
                if behind:
                    dve.wait_ge(CACT.sem, CACT.at(n - 1, "xe"))
                    dve.scalar_tensor_tensor(out=hrow[:, :], in0=xt[:, :], scalar=xrstd, in1=n2row[:, :], op0=ALU.mult,
                                             op1=ALU.mult).then_inc(CDVE.sem, CDVE.one("h"))
                if ahead:
                    dve.wait_ge(APE.sem, APE.at(m, "z32"))
                    dve.wait_ge(ADVE.sem, ADVE.at(m, "pst"))
                    dve.wait_ge(BPE.sem, BPE.at(m - 2, "u1"))
                    tt(pf[t][:, :, :], pst[:, :, :], b8[2], ALU.subtract, ADVE, "pfin")
                if now:
                    dve.wait_ge(BPOOL.sem, BPOOL.at(n, "yb"))
                    dve.wait_ge(BPE.sem, BPE.at(n, "gate"))
                    dve.wait_ge(CPE.sem, CPE.at(n - 1, "ot1"))
                    tt(oh[:, W:D].rearrange("p (a b) -> p a b", a=H), b8[3], ry8, ALU.mult, BDVE, "gy")
                    dve.wait_ge(BACT.sem, BACT.at(n, "sqo"))
                    total(ostat, sq4, "os")
                    dve.wait_ge(BACT.sem, BACT.at(n, "oe"))
                    dve.wait_ge(CPE.sem, CPE.at(n - 1, "ot0"))
                    tt(oh[:, 0:W].rearrange("p (a b) -> p a b", a=U), b4[7], orstd.unsqueeze(2).broadcast_to([P, U, P]),
                       ALU.mult, BDVE, "on")

            tiles(dve, tile, after_first)

        @block.gpsimd
        def _(pool):
            begin(pool, "pool")
            pool.wait_ge(setup["dve"], ZEROED)
            pool.wait_ge(ldc, 64)

            def tt(dst, a, b, op, s, name):
                pool.tensor_tensor(dst, a, b, op).then_inc(s.sem, s.one(name))

            def level(n, i):
                for c, k in ((0, "a"), (1, "b")):
                    if c == 1:
                        pool.wait_ge(APOOL.sem, APOOL.at(n, f"b{1 << i}a"))
                    r = slice(64 * c, 64 * c + 64)
                    tt(bl[i % 2][r, :, r], at[r], lm[r, i].unsqueeze(1).broadcast_to([64, H, 64]), ALU.mult,
                       APOOL, f"b{1 << i}{k}")

            def factor(n, c):
                return F3[:, :, bass.ds(2 * n + c, 1)]

            def fb_(n, c):
                tt(fb[:, :, :], bd[:, :].unsqueeze(1).broadcast_to([P, U, P]), factor(n, c)[:, 0:U].broadcast_to([P, U, P]),
                   ALU.mult, BPOOL, f"F{c}")

            def hm(n, c):
                pool.wait_ge(BDVE.sem, BDVE.at(n, f"ha{c}"))
                tt(hst[:, :, :], hst[:, :, :], factor(n, c)[:, U:2 * U].broadcast_to([P, U, P]), ALU.mult, BPOOL, f"hm{c}")

            def tile(n, par, ahead, now, behind):
                s, t = par, 1 - par
                m = n + 1
                if now:
                    pool.wait_ge(BDVE.sem, BDVE.at(n - 1, "m1"))
                    fb_(n, 0)
                if ahead:
                    pool.wait_ge(ADVE.sem, ADVE.at(m, "bv"))
                    tt(bv[t][:, :, :, :].rearrange("p a b c -> p (a b c)"), bv[t][:, :, :, :].rearrange("p a b c -> p (a b c)"),
                       lnb[:, :], ALU.add, APOOL, "bv")
                    pool.wait_ge(AACT.sem, AACT.at(m, "at11"))
                    pool.wait_ge(APE.sem, APE.at(m - 1, "y32"))
                    pool.wait_ge(APOOL.sem, APOOL.at(m, "bv"))
                    level(m, 1)
                    pool.wait_ge(APOOL.sem, APOOL.at(m, "b2b"))
                if now:
                    pool.wait_ge(BDVE.sem, BDVE.at(n, "m0"))
                    fb_(n, 1)
                if ahead:
                    pool.wait_ge(APE.sem, APE.at(m - 1, "y16"))
                    pool.wait_ge(BPOOL.sem, BPOOL.at(n, "F1"))
                    level(m, 2)
                    pool.wait_ge(APOOL.sem, APOOL.at(m, "b4b"))
                    pool.wait_ge(APE.sem, APE.at(m, "y2"))
                    level(m, 3)
                    pool.wait_ge(APOOL.sem, APOOL.at(m, "b8b"))
                    pool.wait_ge(APE.sem, APE.at(m, "y4"))
                    level(m, 4)
                    pool.wait_ge(APOOL.sem, APOOL.at(m, "b16b"))
                if now:
                    hm(n, 0)
                if ahead:
                    pool.wait_ge(APE.sem, APE.at(m, "y8"))
                    pool.wait_ge(BPOOL.sem, BPOOL.at(n, "hm0"))
                    level(m, 5)
                    pool.wait_ge(APOOL.sem, APOOL.at(m, "b32b"))
                if now:
                    pool.wait_ge(BDVE.sem, BDVE.at(n, "yn"))
                    tt(ry[:, :, :, :].rearrange("p a b c -> p (a b c)"), ry[:, :, :, :].rearrange("p a b c -> p (a b c)"),
                       lnw[:, :], ALU.mult, BPOOL, "yw")
                    pool.wait_ge(BPOOL.sem, BPOOL.at(n, "yw"))
                    pool.wait_ge(APOOL.sem, APOOL.at(n, "bv"))
                    tt(ry[:, :, :, :], ry[:, :, :, :], bv[s][:, :, :, :], ALU.add, BPOOL, "yb")
                    hm(n, 1)
                    pool.wait_ge(BDVE.sem, BDVE.at(n, "on"))
                    pool.wait_ge(BACT.sem, BACT.at(n, "hg"))
                    tt(oh[:, 0:W].rearrange("p (a b) -> p a b", a=U), oh[:, 0:W].rearrange("p (a b) -> p a b", a=U),
                       gtok[:, :, :], ALU.mult, BPOOL, "og")

            tiles(pool, tile)


def feed(nc, dims, A, S, out):
    D, T, DF = dims["D"], dims["T"], dims["F"]
    KT = D // P
    HALVES = 2
    TH = T // HALVES
    NB = TH // BLOCK
    TILES = TH // P
    GROUPS = DF // (2 * P)
    DH = D // BLOCK
    ROUNDS = TILES * DH

    with ExitStack() as ctx:
        def sb(name, shape, dt=F32):
            return ctx.enter_context(nc.sbuf_tensor("f_" + name, shape, dt))

        def sem(name):
            return ctx.enter_context(nc.semaphore("f_" + name))

        hT = [sb("hT_hi", [P, KT, TH], F32R), sb("hT_lo", [P, KT, TH], F32R)]
        acc = sb("acc", [P, TILES, D])
        mid = [sb("mid_hi", [P, 2, TH], F32R), sb("mid_lo", [P, 2, TH], F32R)]
        raw = [sb(f"raw{i}", [P, 2, KT * P]) for i in range(3)]
        wt = [[sb(f"w{i}_hi", [P, 2, KT * P], F32R), sb(f"w{i}_lo", [P, 2, KT * P], F32R)] for i in range(3)]
        silu = sb("silu", [P, 2, BLOCK])
        prod = sb("prod", [P, 2, BLOCK])
        norm_row = sb("norm_row", [P, D])
        stat = sb("stat", [P, 2 * TILES])
        bank = [ctx.enter_context(nc.psum_tensor(f"f_bank{i}", [P, BLOCK], F32)) for i in range(8)]

        loaded_n, loaded_x = sem("loaded_norm"), sem("loaded_x2")
        loaded_w = [sem("loaded_w0"), sem("loaded_w1"), sem("loaded_w2")]
        loaded_h = [[sem(f"loaded_h{b}{k}") for k in range(KT // 2)] for b in range(NB)]
        stored = sem("stored")
        WACT, WDVE = Stages(sem("split_hi"), "w0 w1 w2"), Stages(sem("split_lo"), "w0 w1 w2")
        UPE = Stages(sem("up_pe"), " ".join(f"a{j}{b} b{j}{b}" for j in range(2) for b in range(NB)), ahead=1)
        UACT = Stages(sem("up_act"), " ".join(f"s{j}{b} h{j}{b}" for j in range(2) for b in range(NB)), ahead=1)
        UDVE = Stages(sem("up_dve"), " ".join(f"m{j}{b} l{j}{b}" for j in range(2) for b in range(NB)), ahead=1)
        DPE = Stages(sem("down_pe"), " ".join(f"d{i}" for i in range(ROUNDS)), ahead=1)
        DDVE = Stages(sem("down_dve"), " ".join(f"d{i}" for i in range(ROUNDS)), ahead=1)
        SACT, SDVE = (Stages(sem("h_" + k), " ".join(f"h{b}{i}" for b in range(NB) for i in range(KT // 2))) for k in ("hi", "lo"))
        NACT = Stages(sem("norm_act"), " ".join(f"q{i}" for i in range(TILES)) + " root", ahead=1)
        NDVE = Stages(sem("norm_dve"), "ms rstd " + " ".join(f"y{i}" for i in range(TILES)), ahead=1)
        credit = {"pe": [UPE, DPE], "act": [UACT, NACT], "dve": [UDVE, DDVE, NDVE]}

        def begin(eng, who):
            for s in credit[who]:
                eng.sem_inc(s.sem, s.ahead * len(s.names))

        def halves(eng, group, first=None, last=None):
            def half(hf, more):
                if first:
                    first(hf)
                with eng.Fori(0, GROUPS - 1) as g:
                    group(hf * GROUPS + g, g, True, hf)
                group(hf * GROUPS + GROUPS - 1, GROUPS - 1, more, hf)
                if last:
                    last(hf)
            with eng.Fori(0, HALVES - 1) as hf:
                half(hf, True)
            half(HALVES - 1, False)

        block = ctx.enter_context(nc.Block())

        @block.sync
        def _(sp):
            def load(g, i):
                if i < 2:
                    for k, name in enumerate(("ffn_w1", "ffn_w3")):
                        sp.dma_start(raw[i][:, k].rearrange("p (k c) -> p k c", c=P),
                                     A[name][:, bass.ds((2 * g + i) * P, P)].rearrange("(k p) c -> p k c", p=P))\
                          .then_inc(loaded_w[i], 16)
                else:
                    sp.dma_start(raw[2][:, :, :], A["ffn_w2"][bass.ds(2 * g * P, 2 * P), :].rearrange("(j p) c -> p j c", p=P))\
                      .then_inc(loaded_w[2], 16)

            def load_h(hf, b):
                for k in range(KT // 2):
                    sp.dma_start(hT[1][:, 2 * k:2 * k + 2, b * BLOCK:(b + 1) * BLOCK].bitcast(F32),
                                 S["h2"][2 * k:2 * k + 2, :, bass.ds(hf * TH + b * BLOCK, BLOCK)].rearrange("k p t -> p k t"))\
                      .then_inc(loaded_h[b][k], 16)

            def first(hf):
                sp.wait_ge(stored, hf * TILES * 16)
                sp.dma_start(acc[:, :, :], S["x2"][bass.ds(hf * TH, TH), :].rearrange("(t p) d -> p t d", p=P))\
                  .then_inc(loaded_x, 16)

            def group(G, g, more, hf):
                for i in range(3):
                    if more:
                        sp.wait_ge(WDVE.sem, WDVE.at(G, f"w{i}"))
                        load(0 if isinstance(g, int) else g + 1, i)
                if more and isinstance(g, int):
                    for b in range(NB):
                        sp.wait_ge(UPE.sem, UPE.at(G, f"b1{b}"))
                        load_h(hf + 1, b)

            def last(hf):
                for i in range(TILES):
                    sp.wait_ge(NDVE.sem, NDVE.at(hf, f"y{i}"))
                    sp.dma_start(out[bass.ds(hf * TH + i * P, P), :], acc[:, i]).then_inc(stored, 16)

            load(0, 0)
            load_h(0, 0)
            for b in range(1, NB):
                load_h(0, b)
            load(0, 1)
            load(0, 2)
            sp.dma_start(norm_row[:, :], A["final_norm_w"].partition_broadcast(P)).then_inc(loaded_n, 16)
            halves(sp, group, first, last)
            sp.wait_ge(stored, HALVES * TILES * 16)

        @block.tensor
        def _(pe):
            begin(pe, "pe")

            def up(G, j, hf):
                pe.wait_ge(WACT.sem, WACT.at(G, f"w{j}"))
                pe.wait_ge(WDVE.sem, WDVE.at(G, f"w{j}"))
                for b in range(NB):
                    cols = slice(b * BLOCK, (b + 1) * BLOCK)
                    for x, name in ((0, "a"), (1, "b")):
                        s, stage = (UACT, "s") if x == 0 else (UDVE, "m")
                        if j == 0:
                            pe.wait_ge(s.sem, s.at(G - 1, f"{stage}1{b}"))
                        else:
                            pe.wait_ge(s.sem, s.at(G, f"{stage}0{b}"))
                        for k in range(KT):
                            w = slice(k * P, (k + 1) * P)
                            if j == 0 and x == 0 and k % 2 == 0:
                                pe.wait_ge(SDVE.sem, SDVE.at(hf, f"h{b}{k // 2}"))
                            end = three_passes(pe, bank[2 * b + x][:, :], (wt[j][0][:, x, w], wt[j][1][:, x, w]),
                                               (hT[0][:, k, cols], hT[1][:, k, cols]), k == 0, k == KT - 1)
                        end.then_inc(UPE.sem, UPE.one(f"{name}{j}{b}"))

            def group(G, g, more, hf):
                up(G, 0, hf)
                up(G, 1, hf)
                pe.wait_ge(WACT.sem, WACT.at(G, "w2"))
                pe.wait_ge(WDVE.sem, WDVE.at(G, "w2"))
                for i in range(ROUNDS):
                    tile, half = i // DH, i % DH
                    if tile % (BLOCK // P) == 0 and half == 0:
                        pe.wait_ge(UACT.sem, UACT.at(G, f"h1{tile // (BLOCK // P)}"))
                        pe.wait_ge(UDVE.sem, UDVE.at(G, f"l1{tile // (BLOCK // P)}"))
                    if i < 4:
                        pe.wait_ge(DDVE.sem, DDVE.at(G - 1, f"d{ROUNDS - 4 + i}"))
                    else:
                        pe.wait_ge(DDVE.sem, DDVE.at(G, f"d{i - 4}"))
                    tok, cols = slice(tile * P, (tile + 1) * P), slice(half * BLOCK, (half + 1) * BLOCK)
                    for j in range(2):
                        end = three_passes(pe, bank[4 + i % 4][:, :], (mid[0][:, j, tok], mid[1][:, j, tok]),
                                           (wt[2][0][:, j, cols], wt[2][1][:, j, cols]), j == 0, j == 1)
                    end.then_inc(DPE.sem, DPE.one(f"d{i}"))

            halves(pe, group)

        def free(eng, G, i):
            if i < 2:
                eng.wait_ge(UPE.sem, UPE.at(G - 1, f"b{i}{NB - 1}"))
            else:
                eng.wait_ge(DPE.sem, DPE.at(G - 1, f"d{ROUNDS - 1}"))

        @block.scalar
        def _(act):
            begin(act, "act")
            act.preload_act_table_set(SILU_SET)

            def split(G, i):
                act.wait_ge(loaded_w[i], (G + 1) * (32 if i < 2 else 16))
                free(act, G, i)
                split_hi(act, wt[i][0][:, :, :], raw[i][:, :, :]).then_inc(WACT.sem, WACT.one(f"w{i}"))

            def split_h(hf, b):
                cols = slice(b * BLOCK, (b + 1) * BLOCK)
                for k in range(KT // 2):
                    ks = slice(2 * k, 2 * k + 2)
                    act.wait_ge(loaded_h[b][k], (hf + 1) * 16)
                    split_hi(act, hT[0][:, ks, cols], hT[1][:, ks, cols].bitcast(F32)).then_inc(SACT.sem, SACT.one(f"h{b}{k}"))

            def group(G, g, more, hf):
                for j in range(2):
                    for b in range(NB):
                        cols = slice(b * BLOCK, (b + 1) * BLOCK)
                        act.wait_ge(UPE.sem, UPE.at(G, f"a{j}{b}"))
                        if j == 0:
                            act.wait_ge(UDVE.sem, UDVE.at(G - 1, f"m1{b}"))
                        else:
                            act.wait_ge(UDVE.sem, UDVE.at(G, f"m0{b}"))
                        act.activation(silu[:, b], bank[2 * b][:, :], ACT.Silu).then_inc(UACT.sem, UACT.one(f"s{j}{b}"))
                        act.wait_ge(UDVE.sem, UDVE.at(G, f"m{j}{b}"))
                        act.wait_ge(DPE.sem, DPE.at(G - 1, f"d{ROUNDS - 1}"))
                        split_hi(act, mid[0][:, j, cols], prod[:, b]).then_inc(UACT.sem, UACT.one(f"h{j}{b}"))
                    if more:
                        split(G + 1, j)
                if more and isinstance(g, int):
                    for b in range(NB):
                        split_h(hf + 1, b)
                if more:
                    split(G + 1, 2)

            def last(hf):
                G = hf * GROUPS + GROUPS - 1
                for i in range(TILES):
                    act.wait_ge(DDVE.sem, DDVE.at(G, f"d{DH * i + DH - 1}"))
                    act.activation(silu[:, :, :].rearrange("p a b -> p (a b)"), acc[:, i], ACT.Square,
                                   accum_out=stat[:, i:i + 1]).then_inc(NACT.sem, NACT.one(f"q{i}"))
                    act.wait_ge(NACT.sem, NACT.at(hf, f"q{i}"))
                act.preload_act_table_set(SQRT_SET)
                rstd = stat[:, TILES:2 * TILES]
                act.wait_ge(NDVE.sem, NDVE.at(hf, "ms"))
                act.activation(rstd, rstd, ACT.Sqrt).then_inc(NACT.sem, NACT.one("root"))
                act.preload_act_table_set(SILU_SET)

            split(0, 0)
            split_h(0, 0)
            for b in range(1, NB):
                split_h(0, b)
            split(0, 1)
            split(0, 2)
            halves(act, group, None, last)

        @block.vector
        def _(dve):
            begin(dve, "dve")

            def split(G, i):
                dve.wait_ge(WACT.sem, WACT.at(G, f"w{i}"))
                free(dve, G, i)
                split_lo(dve, wt[i][1][:, :, :], raw[i][:, :, :], wt[i][0][:, :, :]).then_inc(WDVE.sem, WDVE.one(f"w{i}"))

            def split_h(hf, b):
                cols = slice(b * BLOCK, (b + 1) * BLOCK)
                for k in range(KT // 2):
                    ks = slice(2 * k, 2 * k + 2)
                    dve.wait_ge(SACT.sem, SACT.at(hf, f"h{b}{k}"))
                    split_lo(dve, hT[1][:, ks, cols], hT[1][:, ks, cols].bitcast(F32), hT[0][:, ks, cols])\
                        .then_inc(SDVE.sem, SDVE.one(f"h{b}{k}"))

            def group(G, g, more, hf):
                for j in range(2):
                    for b in range(NB):
                        cols = slice(b * BLOCK, (b + 1) * BLOCK)
                        dve.wait_ge(UPE.sem, UPE.at(G, f"b{j}{b}"))
                        dve.wait_ge(UACT.sem, UACT.at(G, f"s{j}{b}"))
                        if j == 0:
                            dve.wait_ge(UDVE.sem, UDVE.at(G - 1, f"l1{b}"))
                        else:
                            dve.wait_ge(UDVE.sem, UDVE.at(G, f"l0{b}"))
                        dve.tensor_tensor(prod[:, b], silu[:, b], bank[2 * b + 1][:, :], ALU.mult)\
                           .then_inc(UDVE.sem, UDVE.one(f"m{j}{b}"))
                        dve.wait_ge(UACT.sem, UACT.at(G, f"h{j}{b}"))
                        split_lo(dve, mid[1][:, j, cols], prod[:, b], mid[0][:, j, cols]).then_inc(UDVE.sem, UDVE.one(f"l{j}{b}"))
                    if more and j == 0:
                        split(G + 1, 0)
                dve.wait_ge(loaded_x, (hf + 1) * 16)
                for i in range(ROUNDS):
                    dve.wait_ge(DPE.sem, DPE.at(G, f"d{i}"))
                    dve.wait_ge(DDVE.sem, DDVE.at(G - 1, f"d{i}"))
                    dst = acc[:, i // DH, (i % DH) * BLOCK:(i % DH + 1) * BLOCK]
                    dve.tensor_tensor(dst, dst, bank[4 + i % 4][:, :], ALU.add).then_inc(DDVE.sem, DDVE.one(f"d{i}"))
                    if more and isinstance(g, int) and i == ROUNDS - 5:
                        split_h(hf + 1, 0)
                if more and isinstance(g, int):
                    for b in range(1, NB):
                        split_h(hf + 1, b)
                if more:
                    split(G + 1, 1)
                    split(G + 1, 2)

            def last(hf):
                dve.wait_ge(NACT.sem, NACT.at(hf, f"q{TILES - 1}"))
                rstd = stat[:, TILES:2 * TILES]
                dve.tensor_scalar(rstd, stat[:, 0:TILES], 1.0 / D, EPS, ALU.mult, ALU.add).then_inc(NDVE.sem, NDVE.one("ms"))
                dve.wait_ge(NACT.sem, NACT.at(hf, "root"))
                dve.reciprocal(rstd, rstd).then_inc(NDVE.sem, NDVE.one("rstd"))
                dve.wait_ge(NDVE.sem, NDVE.at(hf, "rstd"))
                dve.wait_ge(loaded_n, 16)
                for i in range(TILES):
                    dve.scalar_tensor_tensor(out=acc[:, i], in0=acc[:, i], scalar=rstd[:, i:i + 1], in1=norm_row[:, :],
                                             op0=ALU.mult, op1=ALU.mult).then_inc(NDVE.sem, NDVE.one(f"y{i}"))

            split(0, 0)
            split_h(0, 0)
            for b in range(1, NB):
                split_h(0, b)
            split(0, 1)
            split(0, 2)
            halves(dve, group, None, last)


def prepare(nc, dims, consts, A):
    W, COL = dims["W"], dims["COL"]
    U = W // P
    prm = consts["prm"]
    with ExitStack() as ctx:
        loaded = ctx.enter_context(nc.semaphore("c_loaded"))
        made_act = ctx.enter_context(nc.semaphore("c_act"))
        made_dve = ctx.enter_context(nc.semaphore("c_dve"))
        made_pool = ctx.enter_context(nc.semaphore("c_pool"))
        made_eps = ctx.enter_context(nc.semaphore("c_eps"))
        tables = [("mix", A["rw_mix"]), ("nw0", A["rw_w0"]), ("na0", A["rw_a0"]), ("k_k", A["rw_k_k"]), ("k_a", A["rw_k_a"]),
                  ("r_k", A["rw_r_k"]), ("hgw", A["hg_norm_w"]), ("low0", A["hg_lower_bounds"][0:1]),
                  ("low1", A["hg_lower_bounds"][1:2])]

        def cols(name, n=None):
            return prm[:, COL[name]:COL[name] + (U if n is None else n)]

        block = ctx.enter_context(nc.Block())

        @block.sync
        def _(sp):
            for name, src in tables:
                if name == "r_k":
                    src = src.rearrange("o h k -> o (h k)")
                n = src.shape[1] // P
                sp.dma_start(cols(name, n), src.rearrange("o (t p) -> p (o t)", p=P),
                             allow_slow_non_contiguous=True).then_inc(loaded, 16)

        @block.gpsimd
        def _(pool):
            def step(ins, n):
                ins.then_inc(made_pool, 1)
                pool.wait_ge(made_pool, n)

            ident, headsum = consts["ident"], consts["headsum"]
            step(pool.memset(ident[:, :], 0.0), 1)
            step(pool.affine_select(out=ident[:, :], in_=ident[:, :], compare_op=ALU.not_equal, fill=1.0, base=0,
                                    pattern=[[-1, P]], channel_multiplier=1), 2)
            step(pool.memset(headsum[:, :], 0.0), 3)
            step(pool.memset(headsum[0:64, 0:64], 1.0), 4)
            step(pool.memset(headsum[64:128, 64:128], 1.0), 5)
            step(pool.memset(cols("eps", 1), EPS), 6)
            step(pool.memset(cols("gneps", 1), GN_EPS), 7)
            step(pool.memset(cols("half", 1), HALF_LN_LN_SCALE), 8)
            step(pool.memset(cols("one", 1), 1.0), 9)

        @block.vector
        def _(dve):
            n = [0]

            def step(ins):
                n[0] += 1
                ins.then_inc(made_dve, 1)
                dve.wait_ge(made_dve, n[0])

            dve.wait_ge(loaded, 16 * len(tables))
            step(dve.tensor_scalar(cols("omm", 14), cols("mix", 14), -1.0, 1.0, ALU.mult, ALU.add))
            step(dve.tensor_scalar(cols("omka"), cols("k_a"), -1.0, 1.0, ALU.mult, ALU.add))
            step(dve.tensor_scalar(cols("nw0"), cols("nw0"), -1.0, None, ALU.mult))
            step(dve.tensor_scalar(cols("na0"), cols("na0"), -1.0, None, ALU.mult))
            step(dve.tensor_tensor(cols("lb"), cols("low0"), cols("low1"), ALU.max))
            step(dve.tensor_tensor(cols("low0"), cols("low0"), cols("lb"), ALU.subtract))
            step(dve.tensor_tensor(cols("low1"), cols("low1"), cols("lb"), ALU.subtract))
            dve.wait_ge(made_act, 1)
            step(dve.tensor_tensor(cols("low1"), cols("low0"), cols("low1"), ALU.add))
            step(dve.reciprocal(cols("low1"), cols("low1")))
            step(dve.tensor_tensor(cols("lb"), cols("low0"), cols("low1"), ALU.mult))
            step(dve.tensor_scalar(cols("oml"), cols("lb"), -1.0, 1.0, ALU.mult, ALU.add))
            step(dve.tensor_scalar(cols("noml"), cols("oml"), -1.0, None, ALU.mult))

        @block.scalar
        def _(act):
            act.preload_act_table_set(ONE_SET)
            act.wait_ge(made_dve, 7)
            act.activation(prm[:, COL["low0"]:COL["low0"] + 2 * U], prm[:, COL["low0"]:COL["low0"] + 2 * U], ACT.Exp)\
               .then_inc(made_act, 1)


def hymba(nc, A, out):
    _, T, D = A["x"].shape
    W = D // 2
    U = W // P
    COL, c = {}, 0
    for name, n in (("mix", 14), ("omm", 14), ("nw0", U), ("na0", U), ("k_k", U), ("k_a", U), ("omka", U), ("r_k", U),
                    ("lb", U), ("oml", U), ("noml", U), ("hgw", U), ("eps", 1), ("one", 1), ("gneps", 1), ("half", 1),
                    ("low0", U), ("low1", U)):
        COL[name] = c
        c += n
    NT, NC = T // P, T // CHUNK
    dims = {"D": D, "T": T, "W": W, "COL": COL, "F": A["ffn_w1"].shape[2]}
    A = dict(A)
    A["x"] = A["x"][0]
    for name in ("w_in", "rw_w2", "rw_a2", "rw_g2", "w_out", "ffn_w1", "ffn_w3", "ffn_w2"):
        A[name] = A[name][0]
    S = {
        "rw": nc.dram_tensor("s_rw", (NT, P, U * 6, P), F32).ap(),
        "hg": nc.dram_tensor("s_hg", (NT, P, U * 4, P), F32).ap(),
        "sdg": nc.dram_tensor("s_sdg", (NT, P, P), F32).ap(),
        "x2": nc.dram_tensor("s_x2", (T, D), F32).ap(),
        "h2": nc.dram_tensor("s_h2", (D // P, P, T), F32).ap(),
    }
    with ExitStack() as ctx:
        def sb(name, shape, dt=F32):
            return ctx.enter_context(nc.sbuf_tensor(name, shape, dt))

        consts = {"prm": sb("prm", [P, c]), "ident": sb("ident", [P, P]), "headsum": sb("headsum", [P, P]),
                  "lm": sb("lm", [P, 6, 64]), "eye": sb("eye", [P, 64]), "mk": sb("mk", [P, 2, 64]),
                  "himask": sb("himask", [P, P], I32), "headsel": sb("headsel", [P, 2])}
        keep = {"E": sb("keep_E", [P, 2 * U * NC]), "L": sb("keep_L", [P, 2 * U * NC]), "NC": NC}
        prepare(nc, dims, consts, A)
        project(nc, dims, consts, keep, A, S)
        mix(nc, dims, consts, keep, A, S)
        feed(nc, dims, A, S, out[0])


_INS = ["x", "norm1_w", "w_in", "hg_lower_bounds", "hg_norm_w", "rw_mix", "rw_w0", "rw_w2", "rw_a0", "rw_a2", "rw_g2",
        "rw_k_k", "rw_k_a", "rw_r_k", "rw_ln_w", "rw_ln_b", "w_out", "norm2_w", "ffn_w1", "ffn_w3", "ffn_w2", "final_norm_w"]
_OUTS = [((1, 2048, 1024), "float32")]


def kernel(**inputs):
    import numpy as _np
    import concourse.bacc as _bacc
    from concourse import mybir as _mybir
    from concourse.bass_utils import run_bass_kernel_spmd as _run

    nc = _bacc.Bacc("TRN2", target_bir_lowering=False, num_devices=1)
    arrays, args = {}, []
    for name in _INS:
        a = _np.ascontiguousarray(inputs[name])
        arrays[f"in_{name}_dram"] = a
        args.append(nc.dram_tensor(f"in_{name}_dram", a.shape, _mybir.dt.from_np(a.dtype), kind="ExternalInput").ap())
    for i, (shape, dtype) in enumerate(_OUTS):
        dt = _mybir.dt.from_np(_np.dtype(dtype))
        args.append(nc.dram_tensor(f"out_{i}_dram", shape, dt, kind="ExternalOutput").ap())
    hymba(nc, dict(zip(_INS, args)), args[-1])
    r = _run(nc, [arrays], core_ids=[0])
    got = tuple(r.results[0][f"out_{i}_dram"] for i in range(len(_OUTS)))
    return got[0]
```
